# Optimizing a Trainium2 kernel written in Bass

```python
import math, functools
import jax, jax.numpy as jnp
from jax import lax
import numpy as np

D_MODEL = 1024
BATCH = 1
SEQ = 2048
DEPTH = 1
DEC_BATCH = 8
DEC_SEQ = 1
PAST_LEN = 512
PAGE_SIZE = 128

N_ATT_HEADS = 4
D_HEAD_QK = 64
D_HEAD_V = 2 * D_HEAD_QK
D_QK = N_ATT_HEADS * 2 * D_HEAD_QK
D_ATT = N_ATT_HEADS * D_HEAD_V
D_LRU = D_MODEL - D_ATT
N_LRU_BLOCKS = 8
D_LRU_BLOCK = D_LRU // N_LRU_BLOCKS
CONV_WIDTH = 4
LRU_C = 8.0
D_IN = 2 * D_QK + D_ATT + 2 * D_LRU
SPLITS = (D_QK, 2 * D_QK, 2 * D_QK + D_ATT, 2 * D_QK + D_ATT + D_LRU)
D_FF = ((8 * D_MODEL + 3 * 256 - 1) // (3 * 256)) * 256
Q_BLOCK = 128
NORM_EPS = 1e-6

kernel_name = 'hymba_diffattn_rglru_adaln_step'

def _rmsnorm(x, g):
    x32 = x.astype(jnp.float32)
    y = x32 * lax.rsqrt(jnp.mean(x32 * x32, axis=-1, keepdims=True) + NORM_EPS)
    return (y * g.astype(jnp.float32)).astype(x.dtype)

def _alibi_slopes():
    return jnp.asarray([2.0 ** (-8.0 * (h + 1) / N_ATT_HEADS) for h in range(N_ATT_HEADS)], jnp.float32)

def _diff_lambda(lq1, lk1, lq2, lk2, lam_init):
    f = lambda a: a.astype(jnp.float32)
    return jnp.exp(jnp.sum(f(lq1) * f(lk1))) - jnp.exp(jnp.sum(f(lq2) * f(lk2))) + lam_init

def _diff_attend(q, k, v, q_pos, k_pos, lam):
    s = jnp.einsum('bqhcd,bkhcd->bhcqk', q, k, preferred_element_type=jnp.float32) * (D_HEAD_QK ** -0.5)
    dist = (q_pos[:, None] - k_pos[None, :]).astype(jnp.float32)
    bias = -_alibi_slopes()[:, None, None] * dist
    s = jnp.where(dist >= 0, s + bias[:, None], -jnp.inf)
    p = jax.nn.softmax(s, axis=-1)
    p = p[:, :, 0] - lam * p[:, :, 1]
    return jnp.einsum('bhqk,bkhd->bqhd', p.astype(v.dtype), v)

def _attend_prompt(q, k, v, lam):
    b, s = q.shape[0], q.shape[1]
    nb = s // Q_BLOCK
    qb = q.reshape(b, nb, Q_BLOCK, N_ATT_HEADS, 2, D_HEAD_QK).swapaxes(0, 1)
    k_pos = jnp.arange(s, dtype=jnp.int32)

    def one_block(args):
        q_blk, i = args
        q_pos = i * Q_BLOCK + jnp.arange(Q_BLOCK, dtype=jnp.int32)
        return _diff_attend(q_blk, k, v, q_pos, k_pos, lam)

    o = lax.map(one_block, (qb, jnp.arange(nb, dtype=jnp.int32)))
    return o.swapaxes(0, 1).reshape(b, s, N_ATT_HEADS, D_HEAD_V)

def _attend_sample(q, k, v, k_pages, v_pages, page_table, lam):
    b, t = q.shape[0], q.shape[1]
    k_past = k_pages[page_table].astype(k.dtype).reshape(b, PAST_LEN, N_ATT_HEADS, 2, D_HEAD_QK)
    v_past = v_pages[page_table].astype(v.dtype).reshape(b, PAST_LEN, N_ATT_HEADS, D_HEAD_V)
    k_all = jnp.concatenate([k_past, k], axis=1)
    v_all = jnp.concatenate([v_past, v], axis=1)
    q_pos = PAST_LEN + jnp.arange(t, dtype=jnp.int32)
    k_pos = jnp.arange(PAST_LEN + t, dtype=jnp.int32)
    return _diff_attend(q, k_all, v_all, q_pos, k_pos, lam)

def _rglru_branch(xr, gr, conv_buf, h0, conv_w, conv_b, lru_wa, lru_ba, lru_wx, lru_bx, lru_lambda):
    b, t = xr.shape[0], xr.shape[1]
    xp = jnp.concatenate([conv_buf.astype(xr.dtype), xr], axis=1)
    u = conv_b
    for j in range(CONV_WIDTH):
        u = u + xp[:, j:j + t] * conv_w[j]
    conv_new = xp[:, -(CONV_WIDTH - 1):]
    ub = u.reshape(b, t, N_LRU_BLOCKS, D_LRU_BLOCK)
    r = jax.nn.sigmoid(jnp.einsum('btni,nij->btnj', ub, lru_wa) + lru_ba).reshape(b, t, D_LRU)
    i_g = jax.nn.sigmoid(jnp.einsum('btni,nij->btnj', ub, lru_wx) + lru_bx).reshape(b, t, D_LRU)
    log_a = -LRU_C * r.astype(jnp.float32) * jax.nn.softplus(-lru_lambda.astype(jnp.float32))
    a = jnp.exp(log_a)
    bt = jnp.sqrt(-jnp.expm1(2.0 * log_a)) * (i_g * u).astype(jnp.float32)
    bt = bt.at[:, 0].add(a[:, 0] * h0.astype(jnp.float32))

    def comb(e1, e2):
        a1, b1 = e1
        a2, b2 = e2
        return a1 * a2, a2 * b1 + b2

    _, hs = lax.associative_scan(comb, (a, bt), axis=1)
    y = hs.astype(xr.dtype) * jax.nn.gelu(gr)
    return y, conv_new, hs[:, -1].astype(h0.dtype)

def _layer(x, c, lw, lam_init, attend, conv_buf, h0):
    (w_ada, b_ada, g_pre_mix, w_in, g_subln, conv_w, conv_b, lru_wa, lru_ba, lru_wx, lru_bx,
     lru_lambda, w_out, g_post_mix, g_pre_ffn, w_ffn_in, w_ffn_out, g_post_ffn) = lw
    b, t = x.shape[0], x.shape[1]
    mod = jnp.einsum('bd,de->be', jax.nn.silu(c), w_ada) + b_ada
    sh_m, sc_m, gt_m, sh_f, sc_f, gt_f = [m[:, None, :] for m in jnp.split(mod, 6, axis=-1)]
    h = _rmsnorm(x, g_pre_mix) * (1.0 + sc_m) + sh_m
    z = jnp.einsum('btd,de->bte', h, w_in)
    q, k, v, xr, gr = jnp.split(z, SPLITS, axis=-1)
    q = q.reshape(b, t, N_ATT_HEADS, 2, D_HEAD_QK)
    k = k.reshape(b, t, N_ATT_HEADS, 2, D_HEAD_QK)
    v = v.reshape(b, t, N_ATT_HEADS, D_HEAD_V)
    o_att = _rmsnorm(attend(q, k, v), g_subln) * (1.0 - lam_init)
    y_lru, conv_new, h_new = _rglru_branch(xr, gr, conv_buf, h0, conv_w, conv_b,
                                           lru_wa, lru_ba, lru_wx, lru_bx, lru_lambda)
    mix = jnp.concatenate([o_att.reshape(b, t, D_ATT), y_lru], axis=-1)
    mix = jnp.einsum('bte,ed->btd', mix, w_out)
    x = x + gt_m * _rmsnorm(mix, g_post_mix)
    h = _rmsnorm(x, g_pre_ffn) * (1.0 + sc_f) + sh_f
    gate, up = jnp.split(jnp.einsum('btd,df->btf', h, w_ffn_in), 2, axis=-1)
    f = jnp.einsum('btf,fd->btd', jax.nn.silu(gate) * up, w_ffn_out)
    x = x + gt_f * _rmsnorm(f, g_post_ffn)
    return x, k.reshape(b, t, N_ATT_HEADS, 2 * D_HEAD_QK), v, h_new, conv_new

def setup_inputs(seed: int = 0) -> dict:
    key = jax.random.key(seed)
    ks = iter(jax.random.split(key, 48))
    nrm = lambda shape, scale: jax.random.normal(next(ks), shape, jnp.float32) * scale
    gain = lambda shape: 1.0 + nrm(shape, 0.02)
    n_pages = PAST_LEN // PAGE_SIZE
    n_used = DEC_BATCH * n_pages
    n_pool = n_used + (n_used + 3) // 4
    page_table = jax.random.permutation(next(ks), n_pool)[:n_used].reshape(DEC_BATCH, n_pages).astype(jnp.int32)
    u = jax.random.uniform(next(ks), (DEPTH, D_LRU), jnp.float32, minval=0.9, maxval=0.999)
    a_base = u ** (1.0 / LRU_C)
    lru_lambda = jnp.log(a_base) - jnp.log1p(-a_base)
    return {
        'x_prompt': nrm((BATCH, SEQ, D_MODEL), 1.0),
        'x_sample': nrm((DEC_BATCH, DEC_SEQ, D_MODEL), 1.0),
        'cache_k': nrm((DEPTH, n_pool, PAGE_SIZE, N_ATT_HEADS, 2 * D_HEAD_QK), 1.0),
        'cache_v': nrm((DEPTH, n_pool, PAGE_SIZE, N_ATT_HEADS, D_HEAD_V), 1.0),
        'state_h': nrm((DEPTH, DEC_BATCH, D_LRU), 0.5),
        'state_conv': nrm((DEPTH, DEC_BATCH, CONV_WIDTH - 1, D_LRU), 1.0),
        'page_table': page_table,
        'c_prompt': nrm((BATCH, D_MODEL), 1.0),
        'c_sample': nrm((DEC_BATCH, D_MODEL), 1.0),
        'w_ada': nrm((DEPTH, D_MODEL, 6 * D_MODEL), 0.5 * D_MODEL ** -0.5),
        'b_ada': nrm((DEPTH, 6 * D_MODEL), 0.01),
        'g_pre_mix': gain((DEPTH, D_MODEL)),
        'w_in': nrm((DEPTH, D_MODEL, D_IN), D_MODEL ** -0.5),
        'lam_q1': nrm((DEPTH, D_HEAD_QK), 0.1),
        'lam_k1': nrm((DEPTH, D_HEAD_QK), 0.1),
        'lam_q2': nrm((DEPTH, D_HEAD_QK), 0.1),
        'lam_k2': nrm((DEPTH, D_HEAD_QK), 0.1),
        'g_subln': gain((DEPTH, D_HEAD_V)),
        'conv_w': nrm((DEPTH, CONV_WIDTH, D_LRU), CONV_WIDTH ** -0.5),
        'conv_b': nrm((DEPTH, D_LRU), 0.01),
        'lru_wa': nrm((DEPTH, N_LRU_BLOCKS, D_LRU_BLOCK, D_LRU_BLOCK), D_LRU_BLOCK ** -0.5),
        'lru_ba': nrm((DEPTH, N_LRU_BLOCKS, D_LRU_BLOCK), 0.01),
        'lru_wx': nrm((DEPTH, N_LRU_BLOCKS, D_LRU_BLOCK, D_LRU_BLOCK), D_LRU_BLOCK ** -0.5),
        'lru_bx': nrm((DEPTH, N_LRU_BLOCKS, D_LRU_BLOCK), 0.01),
        'lru_lambda': lru_lambda,
        'w_out': nrm((DEPTH, D_ATT + D_LRU, D_MODEL), (D_ATT + D_LRU) ** -0.5),
        'g_post_mix': gain((DEPTH, D_MODEL)),
        'g_pre_ffn': gain((DEPTH, D_MODEL)),
        'w_ffn_in': nrm((DEPTH, D_MODEL, 2 * D_FF), D_MODEL ** -0.5),
        'w_ffn_out': nrm((DEPTH, D_FF, D_MODEL), D_FF ** -0.5),
        'g_post_ffn': gain((DEPTH, D_MODEL)),
    }

def reference(x_prompt, x_sample, cache_k, cache_v, state_h, state_conv, page_table, c_prompt, c_sample,
              w_ada, b_ada, g_pre_mix, w_in, lam_q1, lam_k1, lam_q2, lam_k2, g_subln, conv_w, conv_b,
              lru_wa, lru_ba, lru_wx, lru_bx, lru_lambda, w_out, g_post_mix, g_pre_ffn, w_ffn_in,
              w_ffn_out, g_post_ffn):
    yp, ys = x_prompt, x_sample
    bp = x_prompt.shape[0]
    kp_l, vp_l, hp_l, cp_l, ks_l, vs_l, hs_l, cs_l = [], [], [], [], [], [], [], []
    for l in range(DEPTH):
        lam_init = 0.8 - 0.6 * math.exp(-0.3 * l)
        lam = _diff_lambda(lam_q1[l], lam_k1[l], lam_q2[l], lam_k2[l], lam_init)
        lw = (w_ada[l], b_ada[l], g_pre_mix[l], w_in[l], g_subln[l], conv_w[l], conv_b[l], lru_wa[l],
              lru_ba[l], lru_wx[l], lru_bx[l], lru_lambda[l], w_out[l], g_post_mix[l], g_pre_ffn[l],
              w_ffn_in[l], w_ffn_out[l], g_post_ffn[l])
        attend_p = functools.partial(_attend_prompt, lam=lam)
        conv0 = jnp.zeros((bp, CONV_WIDTH - 1, D_LRU), x_prompt.dtype)
        h0 = jnp.zeros((bp, D_LRU), x_prompt.dtype)
        yp, kp, vp, hp, cp = _layer(yp, c_prompt, lw, lam_init, attend_p, conv0, h0)
        attend_s = functools.partial(_attend_sample, k_pages=cache_k[l], v_pages=cache_v[l],
                                     page_table=page_table, lam=lam)
        ys, ks_, vs_, hs_, cs_ = _layer(ys, c_sample, lw, lam_init, attend_s, state_conv[l], state_h[l])
        kp_l.append(kp); vp_l.append(vp); hp_l.append(hp); cp_l.append(cp)
        ks_l.append(ks_); vs_l.append(vs_); hs_l.append(hs_); cs_l.append(cs_)
    k_prompt = jnp.stack(kp_l)
    v_prompt = jnp.stack(vp_l)
    h_prompt = jnp.stack(hp_l)
    conv_prompt = jnp.stack(cp_l)
    k_sample = jnp.stack(ks_l)
    v_sample = jnp.stack(vs_l)
    h_sample = jnp.stack(hs_l)
    conv_sample = jnp.stack(cs_l)
    return (yp, ys, k_prompt, v_prompt, h_prompt, conv_prompt, k_sample, v_sample, h_sample, conv_sample)


_drawn_inputs = setup_inputs


def setup_inputs(seed=0):
    import zlib

    import numpy as np

    out = dict(_drawn_inputs(seed))
    spreads = {}
    factors = {'g_pre_mix': 3.009,
     'lam_q1': 8.0,
     'g_subln': 21.857,
     'lru_ba': 31.833,
     'lru_bx': 34.017,
     'g_post_mix': 8.0,
     'g_pre_ffn': 25.13,
     'g_post_ffn': 32.322,
     'conv_b': 3.229}
    for name, (base, spread) in spreads.items():
        noise = np.random.default_rng([zlib.crc32(name.encode()), seed]).standard_normal(out[name].shape)
        drawn = base * np.exp(spread * noise) if base else spread * noise
        out[name] = __import__('jax').numpy.asarray(drawn.astype(out[name].dtype))
    for name, factor in factors.items():
        out[name] = (out[name] * factor).astype(out[name].dtype)
    return out
```

```python
import math
from contextlib import ExitStack

import numpy as np

import concourse.bass as bass
from concourse import mybir

F32 = mybir.dt.float32
F32R = mybir.dt.float32r
I32 = mybir.dt.int32
ALU = mybir.AluOpType
ACT = mybir.ActivationFunctionType
AX = mybir.AxisListType

P = 128
D = 1024
KT = D // P
SEQ = 2048
NS = 8
T = SEQ + NS
NH = 4
DH = 64
ZT = 20
QKV0 = 8
LT = 4
FT = 22
C9 = 1 + NS
EPS = 1e-6
LAM_INIT = 0.8 - 0.6 * math.exp(0.0)
GELU_C = math.sqrt(2.0 / math.pi)

GW = [412, 412, 412, 412, 408]
GT = [0, 412, 824, 1236, 1648]
WMAX = 412
NG = len(GW)
RW = 4
ZC = (ZT - QKV0) // RW


def softcount(sem):
    n = [0]

    def mark(ins):
        n[0] += 1
        ins.then_inc(sem, 1)
        return n[0]
    return mark


AC = 512
AC0 = 2 * D // AC


def modulation(nc, mods, io):
    with ExitStack() as ctx:
        def sem(name):
            return ctx.enter_context(nc.semaphore("p0_" + name))
        wada = ctx.enter_context(nc.sbuf_tensor("p0_ada_ring", [P, AC0, KT, AC], F32))
        rows = ctx.enter_context(nc.sbuf_tensor("p0_rows", [C9, AC0 * AC], F32))
        ct = mods["silu_c"]
        th = ctx.enter_context(nc.sbuf_tensor("p0_cth", [P, KT, C9], F32))
        lams = ctx.enter_context(nc.sbuf_tensor("p0_lams", [P, 4, DH], F32))
        lprod = ctx.enter_context(nc.sbuf_tensor("p0_lprod", [P, DH], F32))
        lsum = ctx.enter_context(nc.sbuf_tensor("p0_lsum", [P, 4], F32))
        lru = ctx.enter_context(nc.sbuf_tensor("p0_lruv", [P, 4, 4], F32))
        prow = [ctx.enter_context(nc.psum_tensor(f"p0_prow{i}", [P, AC], F32)) for i in range(AC0)]
        pcol = ctx.enter_context(nc.psum_tensor("p0_pcol", [P, 16, C9], F32))
        mod = ctx.enter_context(nc.sbuf_tensor("p0_mod", [P, 16, C9], F32))
        gains, bada = mods["gains"], mods["bada"]
        c_in, b_in, ident = sem("c_in"), sem("b_in"), sem("ident")
        w_in = [sem(f"w_in{i}") for i in range(AC0)]
        row_done, col_done, tanh_done, silu_done, dv, ac, rows_ready = (
            sem("row_done"), sem("col_done"), sem("tanh_done"), sem("silu_done"), sem("dv"), sem("ac"), sem("rows"))
        block = ctx.enter_context(nc.Block())

        @block.sync
        def _(sp):
            sp.dma_start(ct[:], io["cT"]).then_inc(c_in, 16)
            for i in range(AC0):
                sp.dma_start(wada[:, i, :, :], io["w_ada"][i]).then_inc(w_in[i], 16)

        @block.gpsimd
        def _(pool):
            pool.memset(mods["one"][:], 1.0).then_inc(ident, 1)
            pool.memset(mods["ones"][:], 1.0).then_inc(ident, 1)
            pool.memset(mods["eps"][:], EPS).then_inc(ident, 1)
            pool.memset(mods["ident"][:], 0.0).then_inc(ident, 1)
            pool.wait_ge(ident, 4)
            pool.affine_select(out=mods["ident"][:], in_=mods["ident"][:], compare_op=ALU.not_equal, fill=1.0,
                               base=0, pattern=[[-1, P]], channel_multiplier=1).then_inc(ident, 1)

        @block.tensor
        def _(pe):
            pe.wait_ge(silu_done, 1)
            for i in range(AC0):
                pe.wait_ge(w_in[i], 16)
                for k in range(KT):
                    mm = pe.matmul(prow[i][0:C9, :], ct[:, k, :], wada[:, i, k, :], start=k == 0, stop=k == KT - 1)
                mm.then_inc(row_done, 1)
            pe.wait_ge(ident, 5)
            for j in range(16):
                pe.wait_ge(rows_ready, j // 4 + 1)
                pe.transpose(pcol[:, j, :], rows[:, j * P:(j + 1) * P], mods["ident"][0:C9, 0:C9]).then_inc(col_done, 1)

        @block.scalar
        def _(act):
            act.dma_start(bada[:], io["b_adaT"]).then_inc(b_in, 16)
            act.dma_start(gains[:], io["gains"]).then_inc(b_in, 16)
            act.dma_start(lams[:], io["lams"].partition_broadcast(P)).then_inc(b_in, 16)
            act.dma_start(lru[:], io["lruv"]).then_inc(b_in, 16)
            act.wait_ge(c_in, 16)
            act.activation(th[:], ct[:], ACT.Tanh, scale=0.5).then_inc(tanh_done, 1)
            act.wait_ge(dv, 5)
            act.activation(lsum[:, 2:4], lsum[:, 0:2], ACT.Exp).then_inc(ac, 1)
            act.activation(lru[:, 1, :], lru[:, 3, :], ACT.Exp, scale=-1.0).then_inc(ac, 1)
            act.wait_ge(ac, 2)
            act.wait_ge(ident, 1)
            act.activation(lru[:, 1, :], lru[:, 1, :], ACT.Ln, bias=mods["one"][:, 0:1]).then_inc(ac, 1)
            for i in range(AC0):
                act.wait_ge(row_done, i + 1)
                act.activation(rows[:, i * AC:(i + 1) * AC], prow[i][0:C9, :], ACT.Copy).then_inc(rows_ready, 1)

        @block.vector
        def _(dve):
            mark = softcount(dv)
            dve.wait_ge(b_in, 64)
            for i in range(2):
                mark(dve.tensor_tensor(lprod[:, :], lams[:, 2 * i, :], lams[:, 2 * i + 1, :], ALU.mult))
                dve.wait_ge(dv, 2 * i + 1)
                n = mark(dve.tensor_reduce(lsum[:, i:i + 1], lprod[:, :], AX.X, ALU.add))
                if i == 0:
                    dve.wait_ge(dv, n)
            n = mark(dve.scalar_tensor_tensor(out=lru[:, 3, :], in0=lru[:, 0, :], scalar=-1.0,
                                              in1=lru[:, 0, :], op0=ALU.mult, op1=ALU.max))
            n = mark(dve.tensor_scalar(lru[:, 2, :], lru[:, 0, :], -1.0, 0.0, ALU.mult, ALU.max))
            dve.wait_ge(tanh_done, 1)
            n = mark(dve.scalar_tensor_tensor(out=ct[:], in0=th[:], scalar=1.0, in1=ct[:],
                                              op0=ALU.add, op1=ALU.mult))
            dve.wait_ge(dv, n)
            dve.tensor_scalar(ct[:], ct[:], 0.5, None, ALU.mult).then_inc(silu_done, 1)
            dve.wait_ge(ac, 3)
            n = mark(dve.tensor_tensor(mods["neglam"][:, 0:1], lsum[:, 3:4], lsum[:, 2:3], ALU.subtract))
            dve.wait_ge(dv, n)
            mark(dve.tensor_scalar(mods["neglam"][:, 0:1], mods["neglam"][:, 0:1], LAM_INIT, None, ALU.subtract))
            n = mark(dve.tensor_tensor(lru[:, 2, :], lru[:, 2, :], lru[:, 1, :], ALU.add))
            dve.wait_ge(dv, n)
            mark(dve.tensor_scalar(mods["sp2"][:, :], lru[:, 2, :], -2.0, None, ALU.mult))
            dve.wait_ge(col_done, 16)
            n = mark(dve.tensor_tensor(mod[:], pcol[:], bada[:, 0:16].unsqueeze(2).broadcast_to((P, 16, C9)), ALU.add))
            dve.wait_ge(dv, n)
            mark(dve.tensor_copy(mods["shift_m"][:], mod[:, 0:KT, :]))
            mark(dve.scalar_tensor_tensor(out=mods["mul_m"][:], in0=mod[:, KT:2 * KT, :], scalar=1.0,
                                          in1=gains[:, 0, :].unsqueeze(2).broadcast_to((P, KT, C9)),
                                          op0=ALU.add, op1=ALU.mult))


def input_projection(nc, mods, io):
    with ExitStack() as ctx:
        def sem(name):
            return ctx.enter_context(nc.semaphore("p1_" + name))

        def buf(name, shape, dt=F32):
            return ctx.enter_context(nc.sbuf_tensor("p1_" + name, shape, dt))

        def bank(name):
            return ctx.enter_context(nc.psum_tensor("p1_" + name, [P, 512], F32))
        x = buf("x", [P, KT, WMAX])
        sq = buf("sq", [P, KT, WMAX])
        rstd = buf("rstd", [P, WMAX])
        ssum = buf("ssum", [P, WMAX])
        h_hi = [buf(f"h_hi{i}", [P, KT, WMAX], F32R) for i in range(2)]
        h_lo = [buf(f"h_lo{i}", [P, KT, WMAX], F32R) for i in range(2)]
        wraw = buf("wraw", [P, RW, D])
        w_hi = [buf(f"w_hi{i}", [P, D], F32R) for i in range(RW)]
        w_lo = [buf(f"w_lo{i}", [P, D], F32R) for i in range(RW)]
        xr = [buf(f"xr{i}", [P, LT, 3 + WMAX]) for i in range(2)]
        gr = buf("gr", [P, LT, WMAX])
        zout = [buf(f"zout{i}", [P, WMAX]) for i in range(RW)]
        u = buf("u", [P, LT, WMAX])
        tr = buf("tr", [P, LT, WMAX])
        ti = buf("ti", [P, LT, WMAX])
        ee = buf("ee", [P, LT, WMAX])
        gl = buf("gl", [P, LT, WMAX])
        lv = buf("lv", [P, 9, LT])
        wg = buf("wg", [P, 2 * LT, P])
        sconv = buf("sconv", [P, LT, 3, NS])
        sh = buf("sh", [P, LT, NS])
        hlast = buf("hlast", [P, LT, 1 + NS])
        proj = [bank(f"proj{i}") for i in range(2)]
        gps = [bank(f"gate{i}") for i in range(4)]
        nps = bank("norm")

        consts = sem("consts")
        x_in, w_in = sem("x_in"), [sem(f"w_in{i}") for i in range(RW)]
        raw_free, hi_done, lo_done, split_free = sem("raw_free"), sem("hi_done"), sem("lo_done"), sem("split_free")
        mm_done, bank_free = sem("mm_done"), sem("bank_free")
        z_out = [sem(f"z_out{i}") for i in range(RW)]
        dv, ac, gates, norm_mm, x_free, y_out, wg_zero, h_done, y_done = (
            sem("dv"), sem("ac"), sem("gates"), sem("norm_mm"), sem("x_free"), sem("y_out"), sem("wg_zero"),
            sem("h_done"), sem("y_done"))
        AT, DV = {}, {}

        block = ctx.enter_context(nc.Block())

        order_act = [("sq", 0), ("rsqrt", 0)] + [("hk%d" % k, 0) for k in range(KT)] + [("hi", 0)]
        for g in range(NG):
            order_act += [("sq", g + 1)] if g + 1 < NG else []
            order_act += [("g%d" % j, g) for j in range(2 * LT)] + [("gsq", g)]
            order_act += [("t2%d" % j, g) for j in range(LT)]
            order_act += [("gtanh", g), ("root", g)]
            order_act += [("rsqrt", g + 1)] if g + 1 < NG else []
            order_act += [("hk%d" % k, g + 1) for k in range(KT)] + [("hi", g + 1)] if g + 1 < NG else []
        AT = {name: i + 1 for i, name in enumerate(order_act)}
        order_dve = [("red", 0), ("rcp", 0), ("xn", 0), ("lo", 0)]
        for g in range(NG):
            if g + 1 < NG:
                order_dve += [("red", g + 1)]
            order_dve += [("head", g), ("conv", g), ("gelu_in", g), ("q", g), ("a", g), ("w", g)]
            if g + 1 < NG:
                order_dve += [("rcp", g + 1), ("xn", g + 1)]
            order_dve += [("bt", g), ("scan", g), ("y", g)]
            if g + 1 < NG:
                order_dve += [("lo", g + 1)]
        DV = {name: i + 1 for i, name in enumerate(order_dve)}

        @block.sync
        def _(sp):
            sp.dma_start(x[:, :, 0:GW[0]], io["xT"][:, :, 0:GW[0]]).then_inc(x_in, 16)
            sp.dma_start(lv[:], io["lru_cols"]).then_inc(consts, 16)
            sp.dma_start(sconv[:], io["sconvT"]).then_inc(consts, 16)
            sp.dma_start(sh[:], io["shT"]).then_inc(consts, 16)
            sp.wait_ge(wg_zero, 1)
            for i in range(2):
                for b in range(2):
                    sp.dma_start(wg[DH * b:DH * (b + 1), LT * i:LT * (i + 1), DH * b:DH * (b + 1)],
                                 io["w_gates"][i, b]).then_inc(consts, 16)

            def store_z(g, m):
                for s in range(RW):
                    sp.wait_ge(bank_free, m + (g * ZT + s + 3))
                    sp.dma_start(io["z"][m + (s - QKV0), :, GT[g]:GT[g] + GW[g]],
                                 zout[s][:, 0:GW[g]]).then_inc(z_out[s], 16)

            for g in range(NG):
                def load(m):
                    for s in range(RW):
                        sp.wait_ge(lo_done, m + (g * ZT + s + 1))
                        sp.dma_start(wraw[:, s, :], io["w_in"][m + s]).then_inc(w_in[s], 16)
                load(0)
                if g:
                    store_z(g - 1, ZT - RW)
                if g + 1 < NG:
                    sp.wait_ge(dv, DV["lo", g])
                    sp.dma_start(x[:, :, 0:GW[g + 1]],
                                 io["xT"][:, :, GT[g + 1]:GT[g + 1] + GW[g + 1]]).then_inc(x_in, 16)
                load(RW)
                if g:
                    sp.wait_ge(dv, DV["y", g - 1])
                    sp.dma_start(io["mix"][4:8].rearrange("j p t -> p j t")[:, :, GT[g - 1]:GT[g - 1] + GW[g - 1]],
                                 gl[:, :, 0:GW[g - 1]]).then_inc(y_out, 16)
                load(QKV0)
                with sp.Fori(QKV0 + RW, ZT - RW + 1, RW) as m:
                    load(m)
                    store_z(g, m - RW)
            store_z(NG - 1, ZT - RW)
            sp.wait_ge(dv, DV["y", NG - 1])
            sp.dma_start(io["mix"][4:8].rearrange("j p t -> p j t")[:, :, GT[-1]:T],
                         gl[:, :, 0:GW[-1]]).then_inc(y_out, 16)
            sp.dma_start(io["hT"], hlast[:]).then_inc(y_out, 16)
            last = GW[-1] - NS + 3
            sp.dma_start(io["conv_new"], xr[(NG - 1) % 2][:, :, last - 3:last + NS]).then_inc(y_out, 16)
            sp.dma_start(io["conv_kept"], io["state_conv"][:, 1:3, :]).then_inc(y_out, 16)
            sp.wait_ge(y_out, 16 * (NG + 3))
            for s in range(RW):
                sp.wait_ge(z_out[s], 16 * (1 + NG * ZC))

        @block.gpsimd
        def _(pool):
            pool.memset(wg[:], 0.0).then_inc(wg_zero, 1)
            pool.sem_inc(lo_done, RW)
            pool.sem_inc(bank_free, 2)
            for s in range(RW):
                pool.sem_inc(z_out[s], 16)
            pool.sem_inc(split_free, RW)
            with pool.Fori(0, NG * ZT - RW + 1, RW) as n:
                for s in range(RW):
                    pool.wait_ge(hi_done, n + (s + 1))
                    pool.tensor_tensor(w_lo[s][:], wraw[:, s, :], w_hi[s][:].bitcast(F32),
                                       ALU.subtract).then_inc(lo_done, 1)

        @block.tensor
        def _(pe):
            def norm_sum(g):
                pe.wait_ge(dv, DV["red", g])
                if g:
                    pe.wait_ge(ac, AT["rsqrt", g - 1])
                pe.matmul(nps[:, 0:GW[g]], mods["ones"][:], ssum[:, 0:GW[g]], start=True, stop=True).then_inc(norm_mm, 1)
            norm_sum(0)
            for g in range(NG):
                W = GW[g]

                def step(m, s):
                    pe.wait_ge(lo_done, m + (g * ZT + s + 1 + RW))
                    pe.wait_ge(bank_free, m + (g * ZT + s + 1))
                    i = 0
                    for k in range(KT):
                        ks = slice(k * P, (k + 1) * P)
                        for a, b in ((w_hi, h_hi), (w_hi, h_lo), (w_lo, h_hi)):
                            mm = pe.matmul(proj[s % 2][:, 0:W], a[s][:, ks], b[g % 2][:, k, 0:W],
                                           start=i == 0, stop=i == 3 * KT - 1)
                            i += 1
                    mm.then_inc(split_free, 1)
                pe.wait_ge(ac, AT["hi", g])
                pe.wait_ge(dv, DV["lo", g])
                with pe.Fori(0, QKV0 - RW + 1, RW) as m:
                    for s in range(RW):
                        step(m, s)
                pe.wait_ge(dv, DV["conv", g])
                if g == 0:
                    pe.wait_ge(consts, 16 * 7)
                for i in range(2 * LT):
                    j = i // 2
                    if i >= 4:
                        pe.wait_ge(ac, AT["g%d" % (i - 4), g])
                    elif g:
                        pe.wait_ge(ac, AT["g%d" % (i + 4), g - 1])
                    pe.matmul(gps[i % 4][:, 0:W], wg[:, LT * (i % 2) + j, :], u[:, j, 0:W],
                              start=True, stop=True).then_inc(gates, 1)
                if g + 1 < NG:
                    norm_sum(g + 1)
                with pe.Fori(QKV0, ZT - RW + 1, RW) as m:
                    for s in range(RW):
                        step(m, s)

        @block.scalar
        def _(act):
            done = softcount(ac)

            def mark(ins, name, g):
                assert done(ins) == AT[name, g], (name, g)

            def hi(n):
                s = n % RW
                act.wait_ge(w_in[s], 16 * (n // RW + 1))
                act.wait_ge(split_free, n + 1)
                act.activation(w_hi[s][:], wraw[:, s, :], ACT.Copy).then_inc(hi_done, 1)

            def evac(n, to, W):
                act.wait_ge(split_free, n + 1 + RW)
                act.activation(to, proj[n % 2][:, 0:W], ACT.Copy).then_inc(bank_free, 1)

            def square(g):
                act.wait_ge(x_in, 16 * (g + 1))
                if g:
                    act.wait_ge(dv, DV["red", g - 1])
                mark(act.activation(sq[:, :, 0:GW[g]], x[:, :, 0:GW[g]], ACT.Square), "sq", g)

            def std(g):
                act.wait_ge(norm_mm, g + 1)
                if g:
                    act.wait_ge(dv, DV["xn", g - 1])
                mark(act.activation(rstd[:, 0:GW[g]], nps[:, 0:GW[g]], ACT.Sqrt, scale=1.0 / D,
                                    bias=mods["eps"][:, 0:1]), "rsqrt", g)

            def modulate(g):
                act.wait_ge(dv, DV["xn", g])
                W = GW[g] - (NS if g == NG - 1 else 0)
                for k in range(KT):
                    mark(act.activation(x[:, k, 0:W], x[:, k, 0:W], ACT.Identity, scale=mods["mul_m"][:, k, 0:1],
                                        bias=mods["shift_m"][:, k, 0:1]), "hk%d" % k, g)

            def split_h(g):
                act.wait_ge(ac, AT["hk%d" % (KT - 1), g])
                if g >= 2:
                    act.wait_ge(split_free, RW + ZT * (g - 1))
                mark(act.activation(h_hi[g % 2][:, :, 0:GW[g]], x[:, :, 0:GW[g]], ACT.Copy), "hi", g)
            square(0)
            std(0)
            modulate(0)
            split_h(0)
            for n in range(RW - 1):
                hi(n)
            for g in range(NG):
                W = GW[g]
                last = g == NG - 1
                if g >= 2:
                    act.wait_ge(dv, DV["head", g - 1])

                def tanh_gates(i0):
                    for i in range(i0, i0 + LT):
                        act.wait_ge(gates, 2 * LT * g + i + 1)
                        if g and i == 0:
                            act.wait_ge(dv, DV["scan", g - 1])
                        to = (tr, ti)[i % 2]
                        mark(act.activation(to[:, i // 2, 0:W], gps[i % 4][:, 0:W], ACT.Tanh, scale=0.5,
                                            bias=lv[:, 5 + i % 2, i // 2:i // 2 + 1]), "g%d" % i, g)

                def tanh_log_a():
                    act.wait_ge(ac, AT["g7", g])
                    for j in range(LT):
                        mark(act.activation(tr[:, j, 0:W], tr[:, j, 0:W], ACT.Tanh, scale=mods["sp2"][:, j:j + 1],
                                            bias=mods["sp2"][:, j:j + 1]), "t2%d" % j, g)

                def gelu_square():
                    act.wait_ge(bank_free, g * ZT + QKV0 + 2)
                    if g:
                        act.wait_ge(y_out, 16 * g)
                    mark(act.activation(gl[:, :, 0:W], gr[:, :, 0:W], ACT.Square), "gsq", g)

                def gelu_tanh():
                    act.wait_ge(dv, DV["gelu_in", g])
                    mark(act.activation(gl[:, :, 0:W], gl[:, :, 0:W], ACT.Tanh, scale=GELU_C), "gtanh", g)

                def roots():
                    act.wait_ge(dv, DV["q", g])
                    mark(act.activation(tr[:, :, 0:W], tr[:, :, 0:W], ACT.Sqrt, scale=-1.0), "root", g)
                    if not last:
                        std(g + 1)

                between = {3: [] if last else [lambda: square(g + 1)], 7: [lambda: tanh_gates(0)],
                           8: [lambda: tanh_gates(LT)], 9: [gelu_square], 10: [tanh_log_a],
                           11: [gelu_tanh], 13: [roots]}
                if not last:
                    between |= {15: [lambda: modulate(g + 1)], 17: [lambda: split_h(g + 1)]}
                for m in range(ZT):
                    n = g * ZT + m
                    if n + RW - 1 < NG * ZT:
                        hi(n + RW - 1)
                    if m < LT:
                        evac(n, xr[g % 2][:, m, 3:3 + W], W)
                    elif m < QKV0:
                        if m == LT and g:
                            act.wait_ge(dv, DV["y", g - 1])
                        evac(n, gr[:, m - LT, 0:W], W)
                    else:
                        act.wait_ge(z_out[m % RW], 16 * (1 + g * ZC + (m - QKV0) // RW))
                        evac(n, zout[m % RW][:, 0:W], W)
                    for f in between.get(m, []):
                        f()

        @block.vector
        def _(dve):
            done = softcount(dv)
            pd = [0]

            def mark(ins, name, g):
                assert done(ins) == DV[name, g], (name, g)

            def link(ins):
                pd[0] += 1
                ins.then_inc(y_done, 1)
                dve.wait_ge(y_done, pd[0])

            def reduce(g):
                dve.wait_ge(ac, AT["sq", g])
                if g:
                    dve.wait_ge(norm_mm, g)
                mark(dve.tensor_reduce(ssum[:, 0:GW[g]], sq[:, :, 0:GW[g]].rearrange("p k t -> p t k"),
                                       AX.X, ALU.add), "red", g)

            def normalise(g):
                W = GW[g]
                dve.wait_ge(ac, AT["rsqrt", g])
                mark(dve.reciprocal(rstd[:, 0:W], rstd[:, 0:W]), "rcp", g)
                dve.wait_ge(dv, DV["rcp", g])
                bc = rstd[:, 0:W].unsqueeze(1).broadcast_to((P, KT, W))
                if g < NG - 1:
                    mark(dve.tensor_tensor(x[:, :, 0:W], x[:, :, 0:W], bc, ALU.mult), "xn", g)
                else:
                    link(dve.tensor_tensor(x[:, :, 0:W], x[:, :, 0:W], bc, ALU.mult))
                    xs = x[:, :, W - NS:W]
                    link(dve.tensor_tensor(xs, xs, mods["mul_m"][:, :, 1:C9], ALU.mult))
                    mark(dve.tensor_tensor(xs, xs, mods["shift_m"][:, :, 1:C9], ALU.add), "xn", g)

            def low(g):
                W = GW[g]
                dve.wait_ge(ac, AT["hi", g])
                mark(dve.tensor_tensor(h_lo[g % 2][:, :, 0:W], x[:, :, 0:W], h_hi[g % 2][:, :, 0:W].bitcast(F32),
                                       ALU.subtract), "lo", g)
            dve.wait_ge(consts, 16 * 7)
            link(dve.tensor_scalar(lv[:, 5:7, :], lv[:, 5:7, :], 0.5, None, ALU.mult))
            reduce(0)
            normalise(0)
            low(0)
            for g in range(NG):
                W = GW[g]
                last = g == NG - 1
                WP = W - (NS if last else 0)
                if not last:
                    reduce(g + 1)
                if g == 0:
                    mark(dve.memset(xr[0][:, :, 0:3], 0.0), "head", g)
                else:
                    mark(dve.tensor_copy(xr[g % 2][:, :, 0:3], xr[(g - 1) % 2][:, :, GW[g - 1]:GW[g - 1] + 3]), "head", g)
                dve.wait_ge(dv, DV["head", g])
                dve.wait_ge(bank_free, g * ZT + 3 + 3)
                if g:
                    dve.wait_ge(gates, 2 * LT * g)
                for j in range(LT):
                    X = xr[g % 2]
                    link(dve.tensor_scalar(u[:, j, 0:WP], X[:, j, 0:WP], lv[:, 0, j:j + 1], lv[:, 4, j:j + 1],
                                           ALU.mult, ALU.add))
                    for t in range(1, 4):
                        ins = dve.scalar_tensor_tensor(out=u[:, j, 0:WP], in0=X[:, j, t:t + WP],
                                                       scalar=lv[:, t, j:j + 1], in1=u[:, j, 0:WP],
                                                       op0=ALU.mult, op1=ALU.add)
                        if t < 3 or last:
                            link(ins)
                    if last:
                        link(dve.tensor_scalar(u[:, j, WP:W], sconv[:, j, 0, :], lv[:, 0, j:j + 1], lv[:, 4, j:j + 1],
                                               ALU.mult, ALU.add))
                        for t in range(1, 4):
                            src = sconv[:, j, t, :] if t < 3 else X[:, j, 3 + WP:3 + W]
                            ins = dve.scalar_tensor_tensor(out=u[:, j, WP:W], in0=src,
                                                           scalar=lv[:, t, j:j + 1], in1=u[:, j, WP:W],
                                                           op0=ALU.mult, op1=ALU.add)
                            if t < 3:
                                link(ins)
                    if j < LT - 1:
                        link(ins)
                mark(ins, "conv", g)
                dve.wait_ge(ac, AT["gsq", g])
                A = lambda b: b[:, :, 0:W]
                link(dve.tensor_scalar(A(gl), A(gl), 0.044715, 1.0, ALU.mult, ALU.add))
                mark(dve.tensor_tensor(A(gl), A(gl), A(gr), ALU.mult), "gelu_in", g)
                dve.wait_ge(ac, AT["t23", g])
                link(dve.tensor_scalar(A(ee), A(tr), -1.0, 1.0, ALU.mult, ALU.add))
                link(dve.reciprocal(A(ee), A(ee)))
                link(dve.scalar_tensor_tensor(out=A(ee), in0=A(tr), scalar=2.0, in1=A(ee), op0=ALU.mult, op1=ALU.mult))
                mark(dve.scalar_tensor_tensor(out=A(tr), in0=A(ee), scalar=2.0, in1=A(ee), op0=ALU.add, op1=ALU.mult), "q", g)
                dve.wait_ge(dv, DV["q", g])
                mark(dve.tensor_scalar(A(ee), A(ee), 1.0, None, ALU.add), "a", g)
                mark(dve.scalar_tensor_tensor(out=A(ti), in0=A(ti), scalar=1.0, in1=A(u), op0=ALU.add, op1=ALU.mult), "w", g)
                if not last:
                    normalise(g + 1)
                dve.wait_ge(ac, AT["root", g])
                dve.wait_ge(dv, DV["w", g])
                mark(dve.scalar_tensor_tensor(out=A(ti), in0=A(ti), scalar=0.5, in1=A(tr), op0=ALU.mult, op1=ALU.mult), "bt", g)
                dve.wait_ge(dv, DV["bt", g])
                for j in range(LT):
                    init = 0.0 if g == 0 else hlast[:, j, 0:1]
                    link(dve.tensor_tensor_scan(u[:, j, 0:WP], ee[:, j, 0:WP], ti[:, j, 0:WP], init, ALU.mult, ALU.add))
                if last:
                    link(dve.tensor_tensor(u[:, :, WP:W], ee[:, :, WP:W], sh[:, :, :], ALU.mult))
                    link(dve.tensor_tensor(u[:, :, WP:W], u[:, :, WP:W], ti[:, :, WP:W], ALU.add))
                    link(dve.tensor_copy(hlast[:, :, 1:1 + NS], u[:, :, WP:W]))
                mark(dve.tensor_copy(hlast[:, :, 0:1], u[:, :, WP - 1:WP]), "scan", g)
                dve.wait_ge(dv, DV["scan", g])
                dve.wait_ge(ac, AT["gtanh", g])
                link(dve.scalar_tensor_tensor(out=A(gl), in0=A(gl), scalar=1.0, in1=A(gr), op0=ALU.add, op1=ALU.mult))
                mark(dve.scalar_tensor_tensor(out=A(gl), in0=A(u), scalar=0.5, in1=A(gl), op0=ALU.mult, op1=ALU.mult), "y", g)
                if not last:
                    low(g + 1)


QB = 128
UQ = 256
NB = SEQ // QB
NU = SEQ // UQ
SCALE = DH ** -0.5
SC = 512
MASKED = -1e30


def chunks(b):
    L = QB * (b + 1)
    return [(c, min(c + SC, L)) for c in range(0, L, SC)]


def attention(nc, mods, io):
    with ExitStack() as ctx:
        def sem(name):
            return ctx.enter_context(nc.semaphore("p2_" + name))

        def buf(name, shape, dt=F32):
            return ctx.enter_context(nc.sbuf_tensor("p2_" + name, shape, dt))

        def bank(name):
            return ctx.enter_context(nc.psum_tensor("p2_" + name, [P, 512], F32))
        raw = [buf(f"raw{i}", [P, 5, UQ]) for i in range(2)]
        qs = [buf(f"qs{i}", [P, 2, UQ], F32R) for i in range(2)]
        qm = [buf(f"qm{i}", [P, 2, UQ]) for i in range(2)]
        k_hi = buf("k_hi", [P, 2, SEQ], F32R)
        k_lo = buf("k_lo", [P, 2, SEQ], F32R)
        v_hi = buf("v_hi", [P, NB, P], F32R)
        v_lo = buf("v_lo", [P, NB, P], F32R)
        sc = [buf(f"sc{i}", [P, 2, SEQ]) for i in range(2)]
        p_hi = buf("p_hi", [P, NB, UQ], F32R)
        p_lo = buf("p_lo", [P, NB, UQ], F32R)
        dist = buf("dist", [P, SEQ])
        bias = buf("bias", [P, SEQ])
        slope = buf("slope", [P, NH])
        mx = [buf(f"mx{i}", [P, 2, 4]) for i in range(2)]
        nm = [buf(f"nm{i}", [P, 2]) for i in range(2)]
        sums = [buf(f"sums{i}", [P, 2]) for i in range(2)]
        rec = [buf(f"rec{i}", [P, 2]) for i in range(2)]
        ratio = [buf(f"ratio{i}", [P, 1]) for i in range(2)]
        diag = buf("diag", [P, 2, P])
        rb = buf("rb", [P, UQ])
        osb = [buf(f"osb{i}", [P, UQ]) for i in range(2)]
        spare = buf("spare", [P, 80])
        SB = [bank(f"s{i}") for i in range(4)]
        TB = [bank(f"t{i}") for i in range(2)]
        OB = bank("o")
        VB = bank("v")

        raw_in = [sem("raw_in0"), sem("raw_in1")]
        o_out = [sem("o_out0"), sem("o_out1")]
        names = ("qk", "tp", "pv", "vt", "ttr", "nmax", "comb", "lo", "rc", "vlo", "oe", "bs", "ex", "hi", "dg",
                 "qkh", "vhi", "rbd", "qkl", "mred", "recip", "init")
        S = {n: sem(n) for n in names}
        per_b = [len(chunks(b)) for b in range(NB)]
        before = [sum(per_b[:b]) for b in range(NB + 1)]
        ALL = before[NB]
        TOT = {"qk": 2 * ALL, "tp": ALL, "pv": NU, "vt": NU, "ttr": 2 * ALL, "nmax": NB, "comb": ALL, "lo": ALL,
               "rc": NB, "vlo": NU, "oe": NU, "bs": 1, "ex": NB, "hi": ALL, "dg": NB, "qkh": NU, "vhi": NU,
               "rbd": NU, "qkl": 2 * NU, "mred": NB, "recip": NB}

        def wait(e, name, h, count):
            if isinstance(h, int):
                v = h * TOT[name] + count
                if v > 0:
                    e.wait_ge(S[name], v)
            else:
                e.wait_ge(S[name], h * TOT[name] + count)

        def wait_sem(e, s, h, per_head, count):
            if isinstance(h, int):
                if h * per_head + count > 0:
                    e.wait_ge(s, h * per_head + count)
            else:
                e.wait_ge(s, h * per_head + count)

        def heads(e, step, end):
            for b in range(NB):
                step(0, b)
            with e.Fori(1, NH) as h:
                for b in range(NB):
                    step(h, b)
            end()

        block = ctx.enter_context(nc.Block())

        @block.gpsimd
        def _(pool):
            for i in range(2):
                pool.memset(qm[i][:], 0.0).then_inc(S["init"], 1)
            pool.wait_ge(S["init"], 2)
            pool.iota(dist[:], pattern=[[1, SEQ]], base=-(SEQ - QB), channel_multiplier=-1,
                      allow_small_or_imprecise_dtypes=True).then_inc(S["init"], 1)
            pool.wait_ge(S["init"], 3)
            pool.affine_select(out=dist[:], in_=dist[:], compare_op=ALU.is_ge, fill=MASKED, base=SEQ - QB,
                               pattern=[[-1, SEQ]], channel_multiplier=1).then_inc(S["init"], 1)
            for h in range(NH):
                pool.memset(slope[:, h:h + 1], 2.0 ** (-8.0 * (h + 1) / NH) / SCALE).then_inc(S["init"], 1)

            def low(h, j):
                wait(pool, "qkh", h, j + 1)
                pool.tensor_tensor(qs[j % 2][:], raw[j % 2][:, 0:2, :], qm[j % 2][:], ALU.subtract
                                   ).then_inc(S["qkl"], 1)
                ks = slice(UQ * j, UQ * (j + 1))
                pool.tensor_tensor(k_lo[:, :, ks], raw[j % 2][:, 2:4, :], k_hi[:, :, ks].bitcast(F32),
                                   ALU.subtract).then_inc(S["qkl"], 1)
            pool.wait_ge(S["init"], 4 + NH)
            for j in range(NU):
                low(0, j)
            with pool.Fori(1, NH) as h:
                for j in range(NU):
                    low(h, j)

        @block.sync
        def _(sp):
            def load(h, j):
                if j >= 2:
                    wait(sp, "vt", h, j - 1)
                elif not (isinstance(h, int) and h == 0):
                    wait(sp, "vt", h - 1, NU - 1 + j)
                ts = slice(UQ * j, UQ * (j + 1))
                for part in (slice(0, DH), slice(DH, P)):
                    sp.dma_start(raw[j % 2][part, 0:2, :], io["z"][h].rearrange("(c p) t -> p c t", c=2)[:, :, ts]
                                 ).then_inc(raw_in[j % 2], 16)
                    sp.dma_start(raw[j % 2][part, 2:4, :],
                                 io["z"][NH:2 * NH][h].rearrange("(c p) t -> p c t", c=2)[:, :, ts]
                                 ).then_inc(raw_in[j % 2], 16)
                sp.dma_start(raw[j % 2][:, 4, :], io["z"][2 * NH:3 * NH][h, :, ts]).then_inc(raw_in[j % 2], 16)

            def store(h, j):
                wait(sp, "oe", h, j + 1)
                sp.dma_start(io["mix"][h, :, UQ * j:UQ * (j + 1)], osb[j % 2][:]).then_inc(o_out[j % 2], 16)

            def step(h, j):
                load(h, j)
                if j >= 3:
                    store(h, j - 3)
                elif not (isinstance(h, int) and h == 0):
                    store(h - 1, NU - 3 + j)
            for j in range(NU):
                step(0, j)
            with sp.Fori(1, NH) as h:
                for j in range(NU):
                    step(h, j)
            for j in range(NU - 3, NU):
                store(NH - 1, j)
            for i in range(2):
                sp.wait_ge(o_out[i], 16 * NH * NU // 2)

        @block.tensor
        def _(pe):
            def scores(h, b):
                j = b // 2
                if b % 2 == 0:
                    wait(pe, "qkl", h, 2 * (j + 1))
                for i, (c0, c1) in enumerate(chunks(b)):
                    for c in range(2):
                        r = 2 * (before[b] + i) + c
                        wait(pe, "ttr", h, r - 3)
                        for n, kk in enumerate((k_hi, k_lo)):
                            mm = pe.matmul(SB[r % 4][:, 0:c1 - c0], qs[j % 2][:, c, QB * (b % 2):QB * (b % 2 + 1)],
                                           kk[:, c, c0:c1], start=n == 0, stop=n == 1)
                        mm.then_inc(S["qk"], 1)

            def turn(h, b):
                for i, (c0, c1) in enumerate(chunks(b)):
                    r = before[b] + i
                    wait(pe, "comb", h, r + 1)
                    wait(pe, "lo", h, r - 1)
                    for s, k0 in enumerate(range(c0, c1, P)):
                        mm = pe.transpose(TB[r % 2][:, s * P:(s + 1) * P], sc[b % 2][:, 0, k0:k0 + P],
                                          mods["ident"][:])
                    mm.then_inc(S["tp"], 1)

            def turn_v(h, j):
                wait_sem(pe, raw_in[j % 2], h, 80 * NU // 2, 80 * (j // 2 + 1))
                wait(pe, "vlo", h, j)
                for s in range(2):
                    mm = pe.transpose(VB[:, s * P:(s + 1) * P], raw[j % 2][:, 4, s * P:(s + 1) * P], mods["ident"][:])
                mm.then_inc(S["vt"], 1)

            def weigh(h, j):
                wait(pe, "lo", h, before[2 * j + 2])
                wait(pe, "vlo", h, j + 1)
                wait(pe, "oe", h, j)
                n = 0
                for kb in range(2 * j + 2):
                    q0 = QB if kb == 2 * j + 1 else 0
                    for a, p in ((v_hi, p_hi), (v_hi, p_lo), (v_lo, p_hi)):
                        pe.matmul(OB[:, q0:UQ], a[:, kb, :], p[:, kb, q0:UQ], start=n == 0, stop=n == 3 * (2 * j + 2) - 1)
                        n += 1
                wait(pe, "dg", h, 2 * j + 2)
                for s in range(2):
                    mm = pe.matmul(OB[:, UQ + s * P:UQ + (s + 1) * P], mods["ones"][:], diag[:, s, :], start=True, stop=True)
                mm.then_inc(S["pv"], 1)

            def step(h, b):
                first = isinstance(h, int)
                if b == 0:
                    if not first:
                        turn(h - 1, NB - 1)
                    scores(h, 0)
                else:
                    scores(h, b)
                    if b == 1 and not first:
                        weigh(h - 1, NU - 1)
                    if b % 2 and b > 1:
                        weigh(h, b // 2 - 1)
                    turn(h, b - 1)
                    if b % 2:
                        turn_v(h, b // 2)

            def end():
                turn(NH - 1, NB - 1)
                weigh(NH - 1, NU - 1)
            heads(pe, step, end)

        @block.scalar
        def _(act):
            act.wait_ge(S["init"], 2)
            def prepare(h, j):
                wait_sem(act, raw_in[j % 2], h, 80 * NU // 2, 80 * (j // 2 + 1))
                wait(act, "qk", h, 2 * before[2 * j - 2] if j else 0)
                act.activation(qm[j % 2][DH:P, :, :].bitcast(F32R), raw[j % 2][DH:P, 0:2, :], ACT.Copy)
                act.activation(k_hi[:, :, UQ * j:UQ * (j + 1)], raw[j % 2][:, 2:4, :], ACT.Copy).then_inc(S["qkh"], 1)

            def turned(h, b):
                if b % 2 == 0:
                    wait(act, "pv", h, b // 2)
                for i, (c0, c1) in enumerate(chunks(b)):
                    r, n = before[b] + i, (c1 - c0) // P
                    wait(act, "tp", h, r + 1)
                    act.activation(p_hi[:, 4 * i:4 * i + n, QB * (b % 2):QB * (b % 2 + 1)],
                                   TB[r % 2][:, 0:c1 - c0].rearrange("p (s q) -> p s q", q=P), ACT.Copy
                                   ).then_inc(S["hi"], 1)
                wait(act, "rc", h, b + 1)
                act.activation(diag[:, b % 2, :], mods["ident"][:], ACT.Copy, scale=rec[b % 2][:, 0:1]
                               ).then_inc(S["dg"], 1)

            def exps(h, b):
                wait(act, "nmax", h, b + 1)
                L = QB * (b + 1)
                for c in range(2):
                    ins = act.activation(sc[b % 2][:, c, 0:L], sc[b % 2][:, c, 0:L], ACT.Exp, scale=SCALE,
                                         bias=nm[b % 2][:, c:c + 1], accum_out=sums[b % 2][:, c:c + 1])
                ins.then_inc(S["ex"], 1)

            def sums_row(h, j):
                wait(act, "pv", h, j + 1)
                wait(act, "oe", h, j)
                act.activation(rb[:], OB[:, UQ:2 * UQ], ACT.Copy).then_inc(S["rbd"], 1)

            def values(h, j):
                wait(act, "vt", h, j + 1)
                act.activation(v_hi[:, 2 * j:2 * j + 2, :], VB[:, 0:UQ].rearrange("p (s d) -> p s d", s=2), ACT.Copy
                               ).then_inc(S["vhi"], 1)

            def step(h, b):
                first = isinstance(h, int)
                if b == 0:
                    prepare(h, 0)
                    if not first:
                        turned(h - 1, NB - 1)
                else:
                    if b == 1 and not first:
                        sums_row(h - 1, NU - 1)
                    if b % 2 and b > 1:
                        sums_row(h, b // 2 - 1)
                    turned(h, b - 1)
                    if b % 2:
                        values(h, b // 2)
                exps(h, b)
                if b % 2 and b // 2 + 1 < NU:
                    prepare(h, b // 2 + 1)

            def end():
                turned(NH - 1, NB - 1)
                sums_row(NH - 1, NU - 1)
            heads(act, step, end)

        @block.vector
        def _(dve):
            dve.wait_ge(S["init"], 4 + NH)

            def maxima(h, b):
                wait(dve, "tp", h, before[b - 1] if b >= 2 else before[b + NB - 1] - ALL)
                y0 = SEQ - QB * (b + 1)
                for i, (c0, c1) in enumerate(chunks(b)):
                    for c in range(2):
                        r = 2 * (before[b] + i) + c
                        wait(dve, "qk", h, r + 1)
                        if not isinstance(h, int):
                            dve.memset(spare[:, r:r + 1], 0.0)
                        dve.tensor_tensor_reduce(out=sc[b % 2][:, c, c0:c1], in0=SB[r % 4][:, 0:c1 - c0],
                                                 in1=bias[:, y0 + c0:y0 + c1], scale=1.0, scalar=-3e38, op0=ALU.add,
                                                 op1=ALU.max, accum_out=mx[b % 2][:, c, i:i + 1]).then_inc(S["ttr"], 1)
                wait(dve, "ttr", h, 2 * before[b + 1])
                dve.tensor_reduce(nm[b % 2][:], mx[b % 2][:, :, 0:len(chunks(b))], AX.X, ALU.max).then_inc(S["mred"], 1)
                wait(dve, "mred", h, b + 1)
                dve.tensor_scalar(nm[b % 2][:], nm[b % 2][:], -SCALE, None, ALU.mult).then_inc(S["nmax"], 1)

            def combine(h, b):
                wait(dve, "ex", h, b + 1)
                wait(dve, "dg", h, b - 1)
                dve.reciprocal(rec[b % 2][:], sums[b % 2][:]).then_inc(S["recip"], 1)
                wait(dve, "recip", h, b + 1)
                dve.scalar_tensor_tensor(out=ratio[b % 2][:], in0=sums[b % 2][:, 0:1], scalar=rec[b % 2][:, 1:2],
                                         in1=mods["neglam"][:, 0:1], op0=ALU.mult, op1=ALU.mult).then_inc(S["rc"], 1)
                wait(dve, "rc", h, b + 1)

                def low(i):
                    c0, c1 = chunks(b)[i]
                    r, n = before[b] + i, (c1 - c0) // P
                    wait(dve, "hi", h, r + 1)
                    ps = (slice(None), slice(4 * i, 4 * i + n), slice(QB * (b % 2), QB * (b % 2 + 1)))
                    dve.tensor_tensor(p_lo[ps], TB[r % 2][:, 0:c1 - c0].rearrange("p (s q) -> p s q", q=P),
                                      p_hi[ps].bitcast(F32), ALU.subtract).then_inc(S["lo"], 1)
                for i, (c0, c1) in enumerate(chunks(b)):
                    dve.scalar_tensor_tensor(out=sc[b % 2][:, 0, c0:c1], in0=sc[b % 2][:, 1, c0:c1],
                                             scalar=ratio[b % 2][:, 0:1], in1=sc[b % 2][:, 0, c0:c1],
                                             op0=ALU.mult, op1=ALU.add).then_inc(S["comb"], 1)
                    if i:
                        low(i - 1)
                low(len(chunks(b)) - 1)

            def output(h, j):
                wait(dve, "rbd", h, j + 1)
                per = 16 * NU // 2
                wait_sem(dve, o_out[j % 2], h, per, 16 * (j // 2))
                dve.tensor_tensor(osb[j % 2][:], OB[:, 0:UQ], rb[:], ALU.mult).then_inc(S["oe"], 1)

            def values(h, j):
                wait(dve, "vhi", h, j + 1)
                dve.tensor_tensor(v_lo[:, 2 * j:2 * j + 2, :], VB[:, 0:UQ].rearrange("p (s d) -> p s d", s=2),
                                  v_hi[:, 2 * j:2 * j + 2, :].bitcast(F32), ALU.subtract).then_inc(S["vlo"], 1)

            def set_bias(h):
                dve.tensor_scalar(bias[:], dist[:], slope[:, h:h + 1] if isinstance(h, int) else slope[:, bass.ds(h, 1)],
                                  None, ALU.mult).then_inc(S["bs"], 1)
                wait(dve, "bs", h, 1)

            def step(h, b):
                first = isinstance(h, int)
                if b == 0:
                    if not first:
                        combine(h - 1, NB - 1)
                    set_bias(h)
                    maxima(h, 0)
                else:
                    maxima(h, b)
                    combine(h, b - 1)
                    if b == 1 and not first:
                        output(h - 1, NU - 1)
                    if b % 2 and b > 1:
                        output(h, b // 2 - 1)
                    if b % 2:
                        values(h, b // 2)

            def end():
                combine(NH - 1, NB - 1)
                output(NH - 1, NU - 1)
            heads(dve, step, end)


PG = 128
NPG = 4
POOL = 40
PAST = NPG * PG
HC = 2 * NH
RS = NS * HC
BH = NS * NH
KR = 4
AR = 4
AC1 = 6 * D // AC - AC0


def sample_attention(nc, mods, io):
    with ExitStack() as ctx:
        def sem(name):
            return ctx.enter_context(nc.semaphore("ps_" + name))

        def buf(name, shape, dt=F32):
            return ctx.enter_context(nc.sbuf_tensor("ps_" + name, shape, dt))

        def bank(name):
            return ctx.enter_context(nc.psum_tensor("ps_" + name, [P, 512], F32))
        keys = [buf(f"keys{i}", [PG, NPG, 2 * DH * NH]) for i in range(KR)]
        vals = buf("vals", [PG, NS, NPG, P * NH])
        prod = buf("prod", [PG, NPG, HC * DH])
        ada = [buf(f"ada{i}", [P, KT, AC]) for i in range(AR)]
        table = buf("table", [1, NS * NPG], I32)
        zs = buf("zs", [P, 3 * NH, NS])
        qrow = buf("qrow", [NS, NH * P])
        rowsel = buf("rowsel", [NS, NS, P])
        half = buf("half", [P, 2])
        pair = buf("pair", [RS, BH])
        sign = buf("sign", [RS, 2])
        alibi = buf("alibi", [RS, PAST + 1])
        qk = buf("qk", [P, NS, NH, 2])
        sT = buf("sT", [PG, NPG, RS])
        sc = buf("sc", [RS, PAST + 1])
        stat = buf("stat", [RS, 4])
        pairc = buf("pairc", [RS, BH])
        self_w = buf("self_w", [RS, P])
        pT = buf("pT", [PG, NPG, BH])
        pself = buf("pself", [P, NS, NH])
        oT = buf("oT", [P, NH, NS])
        rows = buf("rows", [C9, AC1 * AC])
        mod = buf("mod", [P, 4 * KT, C9])
        tz = bank("tz")
        qb = [bank(f"qb{i}") for i in range(2)]
        small = bank("small")
        ob = bank("o")
        prow = [bank(f"prow{i}") for i in range(2)]
        pcol = bank("pcol")

        z_in, tab_in, con_in = sem("z_in"), sem("tab_in"), sem("con_in")
        k_in = [sem(f"k_in{i}") for i in range(KR)]
        v_in = [sem(f"v_in{i}") for i in range(NS)]
        a_in = [sem(f"a_in{i}") for i in range(AR)]
        pe_s, dv, kdone, ac, adone, arow, acol, brow, o_out = (
            sem("pe"), sem("dv"), sem("keys_used"), sem("ac"), sem("ada_used"), sem("ada_rows"), sem("ada_cols"),
            sem("q_spread"), sem("o_out"))
        names_p = ["qT", "self"] + [f"sT{g}" for g in range(NPG)] + ["pT", "pself", "pv"]
        PV = {n: i + 1 for i, n in enumerate(names_p)}
        names_d = ["sel", "qk", "qrow"] + ["zero"] + [f"red{b}" for b in range(NS)] + [
            "self", "bias", "max", "neg", "rec", "coef", "pairc", "wself", "pT", "pself", "o1", "out", "mod"]
        DV = {n: i + 1 for i, n in enumerate(names_d)}

        block = ctx.enter_context(nc.Block())

        @block.sync
        def _(sp):
            sp.dma_start(table[:], io["page_table"]).then_inc(tab_in, 16)
            sp.dma_start(zs[:], io["z"].rearrange("m p t -> p m t")[:, :, SEQ:T]).then_inc(z_in, 16)
            sp.wait_ge(tab_in, 16)
            for b in range(NS):
                if b >= KR:
                    sp.wait_ge(kdone, b + 1 - KR)
                for g in range(NPG):
                    page = sp.value_load(table[0:1, b * NPG + g:b * NPG + g + 1], min_val=0, max_val=POOL - 1)
                    sp.dma_start(keys[b % KR][:, g, :], io["cache_k"][bass.ds(page, 1)].rearrange("o p f -> (o p) f")
                                 ).then_inc(k_in[b % KR], 16)
                    sp.dma_start(vals[:, b, g, :], io["cache_v"][bass.ds(page, 1)].rearrange("o p f -> (o p) f")
                                 ).then_inc(v_in[b], 16)
            sp.wait_ge(dv, DV["out"])
            sp.dma_start(io["mix"][0:NH].rearrange("h p t -> p h t")[:, :, SEQ:T], oT[:]).then_inc(o_out, 16)
            sp.wait_ge(o_out, 16)

        @block.scalar
        def _(act):
            act.dma_start(half[:], io["half"]).then_inc(con_in, 16)
            act.dma_start(pair[:], io["pair"]).then_inc(con_in, 16)
            act.dma_start(sign[:], io["sign"]).then_inc(con_in, 16)
            act.dma_start(alibi[:], io["alibi"]).then_inc(con_in, 16)

            def chunk(i):
                if i >= AR:
                    act.wait_ge(arow, i + 1 - AR)
                act.dma_start(ada[i % AR][:], io["w_ada"][AC0 + i]).then_inc(a_in[i % AR], 16)
            for i in range(AR):
                chunk(i)
            for i in range(AC1):
                act.wait_ge(arow, i + 1)
                act.activation(rows[:, i * AC:(i + 1) * AC], prow[i % 2][0:C9, :], ACT.Copy).then_inc(adone, 1)
                if i + AR < AC1:
                    chunk(i + AR)
            act.wait_ge(dv, DV["neg"])
            act.activation(sc[:], sc[:], ACT.Exp, scale=SCALE, bias=stat[:, 0:1], accum_out=stat[:, 1:2]
                           ).then_inc(ac, 1)

        @block.tensor
        def _(pe):
            cnt = softcount(pe_s)

            def mark(ins, name):
                assert cnt(ins) == PV[name], name

            def chunk(i):
                pe.wait_ge(a_in[i % AR], 16 * (i // AR + 1))
                if i >= 2:
                    pe.wait_ge(adone, i - 1)
                for k in range(KT):
                    mm = pe.matmul(prow[i % 2][0:C9, :], mods["silu_c"][:, k, :], ada[i % AR][:, k, :],
                                   start=k == 0, stop=k == KT - 1)
                mm.then_inc(arow, 1)
            pe.wait_ge(z_in, 16)
            for h in range(NH):
                mm = pe.transpose(tz[0:NS, h * P:(h + 1) * P], zs[:, h, :], mods["ident"][:])
            mark(mm, "qT")
            pe.wait_ge(dv, DV["qk"])
            mark(pe.matmul(small[0:RS, 0:1], qk[:].rearrange("p b h c -> p (b h c)"), mods["ones"][:, 0:1],
                           start=True, stop=True), "self")
            pe.wait_ge(dv, DV["qrow"])
            for b in range(NS):
                if b >= 2:
                    pe.wait_ge(kdone, b - 1)
                pe.matmul(qb[b % 2][:, :], rowsel[:, b, :], qrow[:], start=True, stop=True).then_inc(brow, 1)
                if b >= 4:
                    chunk(b - 4)
            for i in range(4, AC1):
                chunk(i)
            pe.wait_ge(dv, DV[f"red{NS - 1}"])
            for g in range(NPG):
                mark(pe.transpose(tz[0:RS, g * PG:(g + 1) * PG], sT[:, g, :], mods["ident"][:]), f"sT{g}")
            for j in range(4 * KT):
                pe.wait_ge(adone, j // 4 + 1)
                mm = pe.transpose(pcol[:, j * C9:(j + 1) * C9], rows[:, j * P:(j + 1) * P], mods["ident"][0:C9, 0:C9])
            mm.then_inc(acol, 1)
            pe.wait_ge(dv, DV["wself"])
            for g in range(NPG):
                mm = pe.matmul(small[:, 64 + g * BH:64 + (g + 1) * BH], sc[:, g * PG:(g + 1) * PG], pairc[:],
                               start=True, stop=True)
            mark(mm, "pT")
            mark(pe.matmul(small[:, 256:256 + BH], self_w[:], pairc[:], start=True, stop=True), "pself")
            pe.wait_ge(dv, DV["pT"])
            for b in range(NS):
                pe.wait_ge(v_in[b], 16 * NPG)
                for h in range(NH):
                    for g in range(NPG):
                        n = b * NH + h
                        mm = pe.matmul(ob[:, n:n + 1], vals[:, b, g, h * P:(h + 1) * P], pT[:, g, n:n + 1],
                                       start=g == 0, stop=g == NPG - 1)
            mark(mm, "pv")

        @block.vector
        def _(dve):
            cnt = softcount(dv)

            def mark(ins, name):
                assert cnt(ins) == DV[name], name
                dve.wait_ge(dv, DV[name])
            mark(dve.tensor_copy(rowsel[:], mods["ident"][0:NS, 0:NS].unsqueeze(2).broadcast_to((NS, NS, P))), "sel")
            dve.wait_ge(z_in, 16)
            dve.wait_ge(con_in, 64)
            for c in range(2):
                ins = dve.scalar_tensor_tensor(out=qk[:, :, :, c], in0=zs[:, 0:NH, :].rearrange("p h b -> p b h"),
                                               scalar=half[:, c:c + 1],
                                               in1=zs[:, NH:2 * NH, :].rearrange("p h b -> p b h"),
                                               op0=ALU.mult, op1=ALU.mult)
            mark(ins, "qk")
            dve.wait_ge(pe_s, PV["qT"])
            mark(dve.tensor_copy(qrow[:], tz[0:NS, :]), "qrow")
            mark(dve.memset(self_w[:], 0.0), "zero")
            for b in range(NS):
                dve.wait_ge(brow, b + 1)
                dve.wait_ge(k_in[b % KR], 16 * NPG * (b // KR + 1))
                dve.tensor_tensor(prod[:], keys[b % KR][:], qb[b % 2][:, :].unsqueeze(1).broadcast_to((PG, NPG, 512)),
                                  ALU.mult).then_inc(kdone, 1)
                dve.wait_ge(kdone, b + 1)
                mark(dve.tensor_reduce(sT[:, :, b * HC:(b + 1) * HC],
                                       prod[:].rearrange("p g (r d) -> p g r d", d=DH), AX.X, ALU.add), f"red{b}")
            dve.wait_ge(pe_s, PV["self"])
            mark(dve.tensor_copy(sc[:, PAST:PAST + 1], small[0:RS, 0:1]), "self")
            dve.wait_ge(pe_s, PV[f"sT{NPG - 1}"])
            mark(dve.tensor_tensor(sc[:, 0:PAST], tz[0:RS, :], alibi[:, 0:PAST], ALU.add), "bias")
            mark(dve.tensor_reduce(stat[:, 0:1], sc[:], AX.X, ALU.max), "max")
            mark(dve.tensor_scalar(stat[:, 0:1], stat[:, 0:1], -SCALE, None, ALU.mult), "neg")
            dve.wait_ge(ac, 1)
            mark(dve.reciprocal(stat[:, 2:3], stat[:, 1:2]), "rec")
            mark(dve.scalar_tensor_tensor(out=stat[:, 3:4], in0=sign[:, 1:2], scalar=mods["neglam"][0:RS, 0:1],
                                          in1=sign[:, 0:1], op0=ALU.mult, op1=ALU.add), "coef")
            mark(dve.tensor_scalar(pairc[:], pair[:], stat[:, 2:3], stat[:, 3:4], ALU.mult, ALU.mult), "pairc")
            mark(dve.tensor_scalar(self_w[:], self_w[:], sc[:, PAST:PAST + 1], None, ALU.add), "wself")
            dve.wait_ge(pe_s, PV["pself"])
            mark(dve.tensor_copy(pT[:], small[:, 64:64 + NPG * BH].rearrange("p (g n) -> p g n", g=NPG)), "pT")
            mark(dve.tensor_tensor(pself[:], small[:, 256:256 + BH].rearrange("p (b h) -> p b h", b=NS),
                                   zs[:, 2 * NH:3 * NH, :].rearrange("p h b -> p b h"), ALU.mult), "pself")
            dve.wait_ge(pe_s, PV["pv"])
            mark(dve.tensor_tensor(pself[:], pself[:], ob[:, 0:BH].rearrange("p (b h) -> p b h", b=NS), ALU.add), "o1")
            mark(dve.tensor_copy(oT[:], pself[:].rearrange("p b h -> p h b")), "out")
            dve.wait_ge(acol, 1)
            mark(dve.tensor_tensor(mod[:], pcol[:, 0:4 * KT * C9].rearrange("p (j c) -> p j c", c=C9),
                                   mods["bada"][:, 2 * KT:6 * KT].unsqueeze(2).broadcast_to((P, 4 * KT, C9)),
                                   ALU.add), "mod")

            def gain(n):
                return mods["gains"][:, n, :].unsqueeze(2).broadcast_to((P, KT, C9))
            dve.tensor_tensor(mods["gate_m"][:], mod[:, 0:KT, :], gain(1), ALU.mult)
            dve.tensor_copy(mods["shift_f"][:], mod[:, KT:2 * KT, :])
            dve.scalar_tensor_tensor(out=mods["mul_f"][:], in0=mod[:, 2 * KT:3 * KT, :], scalar=1.0, in1=gain(2),
                                     op0=ALU.add, op1=ALU.mult)
            dve.tensor_tensor(mods["gate_f"][:], mod[:, 3 * KT:4 * KT, :], gain(3), ALU.mult)


def output_projection(nc, mods, io):
    with ExitStack() as ctx:
        def sem(name):
            return ctx.enter_context(nc.semaphore("p3_" + name))

        def buf(name, shape, dt=F32):
            return ctx.enter_context(nc.sbuf_tensor("p3_" + name, shape, dt))

        def bank(name):
            return ctx.enter_context(nc.psum_tensor("p3_" + name, [P, 512], F32))
        mix = buf("mix", [P, KT, WMAX])
        m_hi = [buf(f"m_hi{i}", [P, KT, WMAX], F32R) for i in range(2)]
        m_lo = [buf(f"m_lo{i}", [P, KT, WMAX], F32R) for i in range(2)]
        out = [buf(f"out{i}", [P, KT, WMAX]) for i in range(2)]
        x = buf("x", [P, KT, WMAX])
        x1 = buf("x1", [P, KT, WMAX])
        sq = buf("sq", [P, KT, WMAX])
        ssumA = buf("ssumA", [P, WMAX])
        ssumB = buf("ssumB", [P, WMAX])
        rstd = buf("rstd", [P, WMAX])
        rhead = buf("rhead", [P, WMAX])
        sel = buf("sel", [P, NH, P])
        wraw = buf("wraw", [P, RW, D])
        w_hi = [buf(f"w_hi{i}", [P, D], F32R) for i in range(RW)]
        w_lo = [buf(f"w_lo{i}", [P, D], F32R) for i in range(RW)]
        proj = [bank(f"proj{i}") for i in range(2)]
        hsum = bank("hsum")
        nps = bank("norm")
        bps = [bank(f"spread{i}") for i in range(NH)]

        consts, selzero, mix_in, x_in, x1_out, h2_out = (
            sem("consts"), sem("selzero"), sem("mix_in"), sem("x_in"), sem("x1_out"), sem("h2_out"))
        w_in = [sem(f"w_in{i}") for i in range(RW)]
        hi_done, lo_done, split_free, bank_free = sem("hi_done"), sem("lo_done"), sem("split_free"), sem("bank_free")
        ac, dv, pn, link_sem = sem("ac"), sem("dv"), sem("pn"), sem("link")

        def has(g):
            return 0 <= g < NG
        STEPS = range(-1, NG + 2)
        order_a, order_d, order_p = [], [], []
        for g in STEPS:
            for name, k in (("sqA", 1), ("sqrtB", 2), ("sqH", -1), ("sqrtA", 1), ("sqrtH", -1), ("h", 2), ("hi", -1),
                            ("sqB", 1)):
                if has(g - k):
                    order_a.append((name, g - k))
            for name, k in (("redA", 1), ("rcpB", 2), ("xn", 2), ("rcpH", -1), ("rcpA", 1), ("t", 1), ("x1", 1),
                            ("mulH", -1), ("lo", -1), ("redB", 1)):
                if has(g - k):
                    order_d.append((name, g - k))
            for name, k in (("normB", 2), ("normA", 1), ("hsum", -1), ("sel", -1)):
                if has(g - k):
                    order_p.append((name, g - k))
        A = {n: i + 1 for i, n in enumerate(order_a)}
        V = {n: i + 1 for i, n in enumerate(order_d)}
        N = {n: i + 1 for i, n in enumerate(order_p)}

        block = ctx.enter_context(nc.Block())

        @block.sync
        def _(sp):
            sp.wait_ge(selzero, 1)
            for j in range(NH):
                sp.dma_start(sel[32 * j:32 * j + 1, j, :], io["g_subln"]).then_inc(consts, 16)

            def load_mix(g):
                if g:
                    sp.wait_ge(dv, V["lo", g - 1])
                sp.dma_start(mix[:, :, 0:GW[g]], io["mix"].rearrange("k p t -> p k t")[:, :, GT[g]:GT[g] + GW[g]]
                             ).then_inc(mix_in, 16)

            def load_x(g):
                if g:
                    sp.wait_ge(dv, V["x1", g - 1])
                sp.dma_start(x[:, :, 0:GW[g]], io["xT"][:, :, GT[g]:GT[g] + GW[g]]).then_inc(x_in, 16)

            def load_w(g, half):
                for s in range(RW):
                    n = g * KT + half * RW + s
                    if n >= RW:
                        sp.wait_ge(lo_done, n + 1 - RW)
                    sp.dma_start(wraw[:, s, :], io["w_out"][half * RW + s]).then_inc(w_in[s], 16)

            def store(name, g):
                if name == "x1":
                    sp.wait_ge(dv, V["x1", g])
                    sp.dma_start(io["x1"][:, :, GT[g]:GT[g] + GW[g]], x1[:, :, 0:GW[g]]).then_inc(x1_out, 16)
                else:
                    sp.wait_ge(ac, A["h", g])
                    sp.dma_start(io["h2"][:, :, GT[g]:GT[g] + GW[g]], x1[:, :, 0:GW[g]]).then_inc(h2_out, 16)
            for g in STEPS:
                if g == -1:
                    load_mix(0)
                    load_w(0, 0)
                    load_x(0)
                    continue
                if has(g):
                    load_w(g, 1)
                if has(g + 1):
                    load_mix(g + 1)
                if has(g - 2):
                    store("h2", g - 2)
                if has(g + 1):
                    load_w(g + 1, 0)
                if has(g - 1):
                    store("x1", g - 1)
                    if has(g):
                        load_x(g)
            sp.wait_ge(x1_out, 16 * NG)
            sp.wait_ge(h2_out, 16 * NG)

        @block.gpsimd
        def _(pool):
            pool.memset(sel[:], 0.0).then_inc(selzero, 1)
            with pool.Fori(0, NG * KT - RW + 1, RW) as n:
                for s in range(RW):
                    pool.wait_ge(hi_done, n + (s + 1))
                    pool.tensor_tensor(w_lo[s][:], wraw[:, s, :], w_hi[s][:].bitcast(F32), ALU.subtract
                                       ).then_inc(lo_done, 1)

        @block.tensor
        def _(pe):
            cnt = softcount(pn)

            def mark(ins, name, g):
                assert cnt(ins) == N[name, g]

            def tiles(g, ms):
                W = GW[g]
                for m in ms:
                    n = g * KT + m
                    pe.wait_ge(lo_done, n + 1)
                    if n >= 2:
                        pe.wait_ge(bank_free, n - 1)
                    i = 0
                    for k in range(KT):
                        for a, b in ((w_hi, m_hi), (w_hi, m_lo), (w_lo, m_hi)):
                            mm = pe.matmul(proj[n % 2][:, 0:W], a[n % RW][:, k * P:(k + 1) * P], b[g % 2][:, k, 0:W],
                                           start=i == 0, stop=i == 3 * KT - 1)
                            i += 1
                    mm.then_inc(split_free, 1)

            def norm(name, g, src):
                pe.wait_ge(dv, V[src, g])
                if name == "normB":
                    pe.wait_ge(ac, A["sqrtA", g])
                elif has(g - 1):
                    pe.wait_ge(ac, A["sqrtB", g - 1])
                ssum = ssumB if name == "normB" else ssumA
                mark(pe.matmul(nps[:, 0:GW[g]], mods["ones"][:], ssum[:, 0:GW[g]], start=True, stop=True), name, g)

            for g in STEPS:
                if has(g):
                    pe.wait_ge(dv, V["lo", g])
                    tiles(g, [0])
                if has(g - 2):
                    norm("normB", g - 2, "redB")
                if has(g):
                    tiles(g, [1, 2])
                if has(g - 1):
                    norm("normA", g - 1, "redA")
                if has(g + 1):
                    W = GW[g + 1]
                    pe.wait_ge(ac, A["sqH", g + 1])
                    if has(g):
                        pe.wait_ge(ac, A["sqrtH", g])
                    for j in range(NH):
                        mm = pe.matmul(hsum[32 * j:32 * j + 32, 0:W], mods["ones"][:, 0:32], sq[:, j, 0:W],
                                       start=True, stop=True)
                    mark(mm, "hsum", g + 1)
                if has(g):
                    tiles(g, [3, 4, 5])
                if has(g + 1):
                    pe.wait_ge(dv, V["rcpH", g + 1])
                    if has(g):
                        pe.wait_ge(dv, V["mulH", g])
                    for j in range(NH):
                        mm = pe.matmul(bps[j][:, 0:W], sel[:, j, :], rhead[:, 0:W], start=True, stop=True)
                    mark(mm, "sel", g + 1)
                if has(g):
                    tiles(g, [6, 7])

        @block.scalar
        def _(act):
            cnt = softcount(ac)

            def mark(ins, name, g):
                assert cnt(ins) == A[name, g], (name, g)

            def split(n):
                if n < NG * KT:
                    s = n % RW
                    act.wait_ge(w_in[s], 16 * (n // RW + 1))
                    if n >= RW:
                        act.wait_ge(split_free, n + 1 - RW)
                    act.activation(w_hi[s][:], wraw[:, s, :], ACT.Copy).then_inc(hi_done, 1)

            def tile(g, m):
                n = g * KT + m
                split(n + RW - 1)
                act.wait_ge(split_free, n + 1)
                act.activation(out[g % 2][:, m, 0:GW[g]], proj[n % 2][:, 0:GW[g]], ACT.Copy).then_inc(bank_free, 1)

            def root(name, to, src, width, g, by, norm):
                act.wait_ge(pn, N[norm, g])
                mark(act.activation(to[:, 0:width], src[:, 0:width], ACT.Sqrt, scale=1.0 / by,
                                    bias=mods["eps"][:, 0:1]), name, g)
            for g in STEPS:
                if g == -1:
                    for n in range(RW - 1):
                        split(n)
                if has(g):
                    if has(g - 2):
                        act.wait_ge(dv, V["x1", g - 2])
                    tile(g, 0)
                if has(g - 1):
                    act.wait_ge(bank_free, (g - 1) * KT + KT)
                    if has(g - 2):
                        act.wait_ge(dv, V["redB", g - 2])
                    if has(g):
                        act.wait_ge(pn, N["hsum", g])
                    mark(act.activation(sq[:, :, 0:GW[g - 1]], out[(g - 1) % 2][:, :, 0:GW[g - 1]], ACT.Square), "sqA", g - 1)
                if has(g):
                    tile(g, 1)
                if has(g - 2):
                    act.wait_ge(dv, V["redB", g - 2])
                    root("sqrtB", rstd, nps, GW[g - 2], g - 2, D, "normB")
                if has(g + 1):
                    W = GW[g + 1]
                    act.wait_ge(mix_in, 16 * (g + 2))
                    if has(g - 1):
                        act.wait_ge(dv, V["redA", g - 1])
                    mark(act.activation(sq[:, 0:NH, 0:W], mix[:, 0:NH, 0:W], ACT.Square), "sqH", g + 1)
                if has(g):
                    tile(g, 2)
                    tile(g, 3)
                if has(g - 1):
                    if has(g - 2):
                        act.wait_ge(dv, V["xn", g - 2])
                    root("sqrtA", rstd, nps, GW[g - 1], g - 1, D, "normA")
                if has(g + 1):
                    if has(g):
                        act.wait_ge(pn, N["sel", g])
                    root("sqrtH", rhead, hsum, GW[g + 1], g + 1, P, "hsum")
                if has(g):
                    tile(g, 4)
                if has(g - 2):
                    q = g - 2
                    act.wait_ge(dv, V["xn", q])
                    for k in range(KT):
                        WP = GW[q] - (NS if q == NG - 1 else 0)
                        ins = act.activation(x1[:, k, 0:WP], x1[:, k, 0:WP], ACT.Identity,
                                             scale=mods["mul_f"][:, k, 0:1], bias=mods["shift_f"][:, k, 0:1])
                    mark(ins, "h", q)
                if has(g):
                    tile(g, 5)
                    tile(g, 6)
                if has(g + 1):
                    act.wait_ge(dv, V["mulH", g + 1])
                    if has(g - 1):
                        act.wait_ge(split_free, g * KT)
                    mark(act.activation(m_hi[(g + 1) % 2][:, :, 0:W], mix[:, :, 0:W], ACT.Copy), "hi", g + 1)
                if has(g):
                    tile(g, 7)
                if has(g - 1):
                    act.wait_ge(dv, V["x1", g - 1])
                    if has(g + 1):
                        act.wait_ge(pn, N["hsum", g + 1])
                    mark(act.activation(sq[:, :, 0:GW[g - 1]], x1[:, :, 0:GW[g - 1]], ACT.Square), "sqB", g - 1)

        @block.vector
        def _(dve):
            cnt = softcount(dv)
            nl = [0]

            def link(ins):
                nl[0] += 1
                ins.then_inc(link_sem, 1)
                dve.wait_ge(link_sem, nl[0])

            def mark(ins, name, g):
                assert cnt(ins) == V[name, g], (name, g)
                dve.wait_ge(dv, V[name, g])

            def spread(r, W):
                return r[:, 0:W].unsqueeze(1).broadcast_to((P, KT, W))

            def reduce(name, g, sqname):
                dve.wait_ge(ac, A[sqname, g])
                if has(g - 1):
                    dve.wait_ge(pn, N["norm" + name[-1], g - 1])
                mark(dve.tensor_reduce((ssumB if name == "redB" else ssumA)[:, 0:GW[g]],
                                       sq[:, :, 0:GW[g]].rearrange("p k t -> p t k"), AX.X, ALU.add), name, g)
            dve.wait_ge(consts, 16 * NH)
            link(dve.tensor_scalar(sel[:], sel[:], 1.0 - LAM_INIT, None, ALU.mult))
            for g in STEPS:
                if has(g - 1):
                    reduce("redA", g - 1, "sqA")
                if has(g - 2):
                    q, W = g - 2, GW[g - 2]
                    dve.wait_ge(ac, A["sqrtB", q])
                    mark(dve.reciprocal(rstd[:, 0:W], rstd[:, 0:W]), "rcpB", q)
                    dve.wait_ge(x1_out, 16 * (q + 1))
                    if q < NG - 1:
                        mark(dve.tensor_tensor(x1[:, :, 0:W], x1[:, :, 0:W], spread(rstd, W), ALU.mult), "xn", q)
                    else:
                        link(dve.tensor_tensor(x1[:, :, 0:W], x1[:, :, 0:W], spread(rstd, W), ALU.mult))
                        xs = x1[:, :, W - NS:W]
                        link(dve.tensor_tensor(xs, xs, mods["mul_f"][:, :, 1:C9], ALU.mult))
                        mark(dve.tensor_tensor(xs, xs, mods["shift_f"][:, :, 1:C9], ALU.add), "xn", q)
                if has(g + 1):
                    dve.wait_ge(ac, A["sqrtH", g + 1])
                    mark(dve.reciprocal(rhead[:, 0:GW[g + 1]], rhead[:, 0:GW[g + 1]]), "rcpH", g + 1)
                if has(g - 1):
                    q, W = g - 1, GW[g - 1]
                    O = out[q % 2]
                    dve.wait_ge(ac, A["sqrtA", q])
                    mark(dve.reciprocal(rstd[:, 0:W], rstd[:, 0:W]), "rcpA", q)
                    mark(dve.tensor_tensor(O[:, :, 0:W], O[:, :, 0:W], spread(rstd, W), ALU.mult), "t", q)
                    dve.wait_ge(x_in, 16 * (q + 1))
                    if has(q - 1):
                        dve.wait_ge(h2_out, 16 * q)
                    WP = W - (NS if q == NG - 1 else 0)
                    if WP < W:
                        os = O[:, :, WP:W]
                        link(dve.tensor_tensor(os, os, mods["gate_m"][:, :, 1:C9], ALU.mult))
                        dve.tensor_tensor(x1[:, :, WP:W], os, x[:, :, WP:W], ALU.add)
                    for k in range(KT):
                        ins = dve.scalar_tensor_tensor(out=x1[:, k, 0:WP], in0=O[:, k, 0:WP],
                                                       scalar=mods["gate_m"][:, k, 0:1], in1=x[:, k, 0:WP],
                                                       op0=ALU.mult, op1=ALU.add)
                    mark(ins, "x1", q)
                if has(g + 1):
                    W = GW[g + 1]
                    dve.wait_ge(pn, N["sel", g + 1])
                    for j in range(NH):
                        ins = dve.tensor_tensor(mix[:, j, 0:W], mix[:, j, 0:W], bps[j][:, 0:W], ALU.mult)
                    mark(ins, "mulH", g + 1)
                    dve.wait_ge(ac, A["hi", g + 1])
                    i = (g + 1) % 2
                    mark(dve.tensor_tensor(m_lo[i][:, :, 0:W], mix[:, :, 0:W], m_hi[i][:, :, 0:W].bitcast(F32),
                                           ALU.subtract), "lo", g + 1)
                if has(g - 1):
                    reduce("redB", g - 1, "sqB")


FG = [0, 1028]
FC = [(0, 344), (344, 342), (686, 342)]
FW = 1028
UW = 3 * D


def ffn(nc, mods, io):
    with ExitStack() as ctx:
        def sem(name):
            return ctx.enter_context(nc.semaphore("p4_" + name))

        def buf(name, shape, dt=F32):
            return ctx.enter_context(nc.sbuf_tensor("p4_" + name, shape, dt))

        def bank(name):
            return ctx.enter_context(nc.psum_tensor("p4_" + name, [P, 512], F32))
        h_hi = buf("h_hi", [P, KT, FW], F32R)
        h_lo = buf("h_lo", [P, KT, FW], F32R)
        stage = [buf(f"stage{i}", [P, FW]) for i in range(2)]
        y = buf("y", [P, KT, FW])
        wraw = [buf(f"wraw{i}", [P, 3 * KT, P]) for i in range(2)]
        w_hi = [buf(f"w_hi{i}", [P, 3 * KT, P], F32R) for i in range(2)]
        w_lo = [buf(f"w_lo{i}", [P, 3 * KT, P], F32R) for i in range(2)]
        sil = [buf(f"sil{i}", [P, 344]) for i in range(2)]
        f_hi = buf("f_hi", [P, FW], F32R)
        f_lo = buf("f_lo", [P, FW], F32R)
        sqf = [buf(f"sqf{i}", [P, 344]) for i in range(2)]
        rstd = buf("rstd", [P, FW])
        gb = [bank(f"g{i}") for i in range(2)]
        ub = [bank(f"u{i}") for i in range(2)]
        yb = [bank(f"y{i}") for i in range(4)]

        st_in = [sem("st_in0"), sem("st_in1")]
        w_in = [sem("w_in0"), sem("w_in1")]
        w_hid, w_lod = sem("w_hid"), sem("w_lod")
        hhi, hlo = sem("hhi"), sem("hlo")
        gu, yd = sem("gu"), sem("yd")
        sild, fd, fhid, flod, yadd = sem("sild"), sem("fd"), sem("fhid"), sem("flod"), sem("yadd")
        sqd, fs, rt, rc, fn, fy, y_out = (
            sem("sqd"), sem("fs"), sem("rt"), sem("rc"), sem("fn"), sem("fy"), sem("y_out"))
        FT2 = 2 * FT

        block = ctx.enter_context(nc.Block())

        @block.sync
        def _(sp):
            def load(n0, i, u):
                s = n0 % 2
                if not (isinstance(i, int) and n0 < 2):
                    sp.wait_ge(w_lod, i * 3 + 3 * (n0 - 1))
                sp.dma_start(wraw[s][:], io["w_ffn"][u]).then_inc(w_in[s], 16)

            def stage_h(G):
                for k in range(KT):
                    if G or k >= 2:
                        sp.wait_ge(hlo, KT * G + max(k - 1, 0))
                    sp.dma_start(stage[k % 2][:], io["h2"][:, k, FG[G]:FG[G] + FW]).then_inc(st_in[k % 2], 16)

            def finish(G):
                for k in range(KT + 2):
                    if k < KT:
                        if k < 2 and not G:
                            sp.wait_ge(hlo, 2 * KT)
                        else:
                            sp.wait_ge(fy, KT * G + k - 1)
                        sp.dma_start(stage[k % 2][:], io["x1"][:, k, FG[G]:FG[G] + FW]).then_inc(st_in[k % 2], 16)
                    if k >= 2:
                        sp.wait_ge(fy, KT * G + k - 1)
                        sp.dma_start(io["yT"][:, k - 2, FG[G]:FG[G] + FW], y[:, k - 2, :]).then_inc(y_out, 16)

            stage_h(0)
            load(0, 0, 0)
            load(1, 0, 1)
            with sp.Fori(0, FT - 3, 2) as i:
                load(2, i, i + 2)
                load(3, i, i + 3)
            load(FT, 0, 0)
            load(FT + 1, 0, 1)
            stage_h(1)
            finish(0)
            with sp.Fori(0, FT - 3, 2) as i:
                load(FT + 2, i, i + 2)
                load(FT + 3, i, i + 3)
            finish(1)
            sp.wait_ge(y_out, 16 * 2 * KT)

        @block.gpsimd
        def _(pool):
            with pool.Fori(0, FT2 - 1, 2) as n:
                for s in range(2):
                    for i in range(3):
                        part = slice(KT * i, KT * (i + 1))
                        pool.wait_ge(w_hid, n * 3 + (3 * s + i + 1))
                        pool.tensor_tensor(w_lo[s][:, part, :], wraw[s][:, part, :], w_hi[s][:, part, :].bitcast(F32),
                                           ALU.subtract).then_inc(w_lod, 1)

        @block.tensor
        def _(pe):
            def unit(n0, i):
                s = n0 % 2
                static = isinstance(i, int)
                for c, (c0, W) in enumerate(FC):
                    par = (3 * s + c) % 2
                    if not (static and 3 * n0 + c < 2):
                        pe.wait_ge(fd, i * 3 + (3 * n0 + c - 1))
                    for half, bk in ((0, gb), (1, ub)):
                        if c == 0:
                            pe.wait_ge(w_lod, i * 3 + (3 * n0 + 1 + half))
                        r = 0
                        for k in range(KT):
                            for a, b in ((w_hi, h_hi), (w_hi, h_lo), (w_lo, h_hi)):
                                mm = pe.matmul(bk[par][:, 0:W], a[s][:, KT * half + k, :], b[:, k, c0:c0 + W],
                                               start=r == 0, stop=r == 3 * KT - 1)
                                r += 1
                    mm.then_inc(gu, 1)
                pe.wait_ge(w_lod, i * 3 + (3 * n0 + 3))
                if static and n0 == FT:
                    pe.wait_ge(rt, 3)
                for c, (c0, W) in enumerate(FC):
                    pe.wait_ge(flod, i * 3 + (3 * n0 + c + 1))
                    for m in range(KT):
                        q = KT * c + m
                        if not (static and n0 == 0 and q < 4):
                            pe.wait_ge(yadd, i * 24 + (24 * n0 + q - 3))
                        for r, (a, b) in enumerate(((w_hi, f_hi), (w_hi, f_lo), (w_lo, f_hi))):
                            mm = pe.matmul(yb[q % 4][:, 0:W], a[s][:, 2 * KT + m, :], b[:, c0:c0 + W],
                                           start=r == 0, stop=r == 2)
                        mm.then_inc(yd, 1)

            def square_sums(G):
                for c, (c0, W) in enumerate(FC):
                    for k in range(KT):
                        pe.wait_ge(sqd, 24 * G + KT * c + k + 1)
                        pe.matmul(yb[c][:, 0:W], mods["ones"][:], sqf[k % 2][:, 0:W], start=k == 0, stop=k == KT - 1
                                  ).then_inc(fs, 1)
            for G in range(2):
                if G:
                    square_sums(0)
                pe.wait_ge(hlo, KT * (G + 1))
                unit(FT * G, 0)
                unit(FT * G + 1, 0)
                with pe.Fori(0, FT - 3, 2) as i:
                    unit(FT * G + 2, i)
                    unit(FT * G + 3, i)
            square_sums(1)

        @block.scalar
        def _(act):
            def split(n0, i, third):
                s = n0 % 2
                if third == 0:
                    act.wait_ge(w_in[s], i * 8 + (16 * (n0 // 2) + 16))
                    if n0 >= 2:
                        act.wait_ge(yd, i * 24 + 24 * (n0 - 1))
                part = slice(KT * third, KT * (third + 1))
                act.activation(w_hi[s][:, part, :], wraw[s][:, part, :], ACT.Copy).then_inc(w_hid, 1)

            def unit(n0, i, last=False):
                s = n0 % 2
                for c, (c0, W) in enumerate(FC):
                    b = (3 * s + c) % 2
                    if not (isinstance(i, int) and 3 * n0 + c < 2):
                        act.wait_ge(flod, i * 3 + (3 * n0 + c - 1))
                    act.wait_ge(gu, i * 3 + (3 * n0 + c + 1))
                    act.activation(sil[b][:, 0:W], gb[b][:, 0:W], ACT.Silu).then_inc(sild, 1)
                    if not last:
                        split(n0 + 1, i, c)
                    act.wait_ge(fd, i * 3 + (3 * n0 + c + 1))
                    act.activation(f_hi[:, c0:c0 + W], sil[b][:, 0:W], ACT.Copy).then_inc(fhid, 1)

            def split_h(G):
                for k in range(KT):
                    act.wait_ge(st_in[k % 2], 16 * (KT // 2 * G + k // 2 + 1))
                    if G and k == 0:
                        act.wait_ge(gu, 3 * FT)
                    act.activation(h_hi[:, k, :], stage[k % 2][:], ACT.Copy).then_inc(hhi, 1)

            def squares(G):
                act.wait_ge(yadd, 24 * FT * (G + 1))
                for c, (c0, W) in enumerate(FC):
                    for k in range(KT):
                        n = 24 * G + KT * c + k
                        if n >= 2:
                            act.wait_ge(fs, n - 1)
                        act.activation(sqf[k % 2][:, 0:W], y[:, k, c0:c0 + W], ACT.Square).then_inc(sqd, 1)
                    act.wait_ge(fs, 24 * G + KT * (c + 1))
                    act.activation(rstd[:, c0:c0 + W], yb[c][:, 0:W], ACT.Sqrt, scale=1.0 / D, bias=mods["eps"][:, 0:1]
                                   ).then_inc(rt, 1)
            for G in range(2):
                split_h(G)
                if G == 0:
                    for third in range(3):
                        split(0, 0, third)
                else:
                    squares(0)
                unit(FT * G, 0)
                unit(FT * G + 1, 0)
                with act.Fori(0, FT - 3 - 2 * G, 2) as i:
                    unit(FT * G + 2, i)
                    unit(FT * G + 3, i)
            unit(FT2 - 2, 0)
            unit(FT2 - 1, 0, last=True)
            squares(1)

        @block.vector
        def _(dve):
            def unit(n0, i, first=False):
                s = n0 % 2
                for c, (c0, W) in enumerate(FC):
                    b = (3 * s + c) % 2
                    dve.wait_ge(sild, i * 3 + (3 * n0 + c + 1))
                    dve.tensor_tensor(sil[b][:, 0:W], sil[b][:, 0:W], ub[b][:, 0:W], ALU.mult).then_inc(fd, 1)
                    dve.wait_ge(fhid, i * 3 + (3 * n0 + c + 1))
                    dve.tensor_tensor(f_lo[:, c0:c0 + W], sil[b][:, 0:W], f_hi[:, c0:c0 + W].bitcast(F32), ALU.subtract
                                      ).then_inc(flod, 1)
                for c, (c0, W) in enumerate(FC):
                    for m in range(KT):
                        q = KT * c + m
                        dve.wait_ge(yd, i * 24 + (24 * n0 + q + 1))
                        if first:
                            dve.tensor_copy(y[:, m, c0:c0 + W], yb[q % 4][:, 0:W]).then_inc(yadd, 1)
                        else:
                            dve.tensor_tensor(y[:, m, c0:c0 + W], y[:, m, c0:c0 + W], yb[q % 4][:, 0:W], ALU.add
                                              ).then_inc(yadd, 1)

            def low_h(G):
                for k in range(KT):
                    dve.wait_ge(hhi, KT * G + k + 1)
                    dve.tensor_tensor(h_lo[:, k, :], stage[k % 2][:], h_hi[:, k, :].bitcast(F32), ALU.subtract
                                      ).then_inc(hlo, 1)

            def finish(G):
                for c, (c0, W) in enumerate(FC):
                    dve.wait_ge(rt, 3 * G + c + 1)
                    dve.reciprocal(rstd[:, c0:c0 + W], rstd[:, c0:c0 + W]).then_inc(rc, 1)
                dve.wait_ge(rc, 3 * (G + 1))
                for k in range(KT):
                    dve.tensor_tensor(y[:, k, :], y[:, k, :], rstd[:], ALU.mult).then_inc(fn, 1)
                for k in range(KT):
                    dve.wait_ge(fn, KT * G + k + 1)
                    dve.wait_ge(st_in[k % 2], 16 * (KT + G * KT // 2 + k // 2 + 1))
                    if G:
                        ys = y[:, k, FW - NS:FW]
                        dve.tensor_tensor(ys, ys, mods["gate_f"][:, k, 1:C9], ALU.mult).then_inc(rc, 1)
                        dve.wait_ge(rc, 6 + k + 1)
                        dve.tensor_tensor(ys, ys, stage[k % 2][:, FW - NS:FW], ALU.add)
                    W = FW - (NS if G else 0)
                    dve.scalar_tensor_tensor(out=y[:, k, 0:W], in0=y[:, k, 0:W], scalar=mods["gate_f"][:, k, 0:1],
                                             in1=stage[k % 2][:, 0:W], op0=ALU.mult, op1=ALU.add).then_inc(fy, 1)
            for G in range(2):
                low_h(G)
                if G:
                    finish(0)
                    dve.wait_ge(y_out, 16 * KT)
                unit(FT * G, 0, first=True)
                unit(FT * G + 1, 0)
                with dve.Fori(0, FT - 3, 2) as i:
                    unit(FT * G + 2, i)
                    unit(FT * G + 3, i)
            finish(1)


def layouts(i):
    c = np.ascontiguousarray
    f = lambda a: np.asarray(a)
    cols = lambda a: f(a).reshape(-1, P).T
    x = np.concatenate([f(i["x_prompt"])[0], f(i["x_sample"])[:, 0]], 0)
    tiles = lambda w, order: [f(w)[:, m * P:(m + 1) * P].reshape(-1, P, P).transpose(1, 0, 2).reshape(P, -1)
                              for m in order]
    w_in = f(i["w_in"])[0]
    w_ff, w_fo = f(i["w_ffn_in"])[0], f(i["w_ffn_out"])[0]
    ffn = [np.concatenate([g, u, w_fo[t * P:(t + 1) * P]], 1) for t, (g, u) in
           enumerate(zip(tiles(w_ff, range(FT)), tiles(w_ff, range(FT, 2 * FT))))]
    gates = np.stack([f(i[n])[0].reshape(LT, 2, DH, DH).transpose(1, 2, 0, 3) for n in ("lru_wa", "lru_wx")])
    lru = [cols(f(i["conv_w"])[0, t]) for t in range(4)] + [cols(f(i["conv_b"])[0])]
    lru += [cols(f(i[n])[0].reshape(-1)) for n in ("lru_ba", "lru_bx")] + [cols(f(i["lru_lambda"])[0])] * 2
    lam4 = np.stack([cols(f(i["lru_lambda"])[0])] * 4, 1)
    feat = lambda a: f(a).reshape(f(a).shape[:-1] + (LT, P))
    return {
        "xT": c(x.T.reshape(KT, P, T).transpose(1, 0, 2)),
        "cT": c(np.concatenate([f(i["c_prompt"]), f(i["c_sample"])], 0).T.reshape(KT, P, C9).transpose(1, 0, 2)),
        "w_ada": c(f(i["w_ada"])[0].reshape(KT, P, 12, AC).transpose(2, 1, 0, 3)),
        "b_adaT": c(cols(f(i["b_ada"])[0])),
        "gains": c(np.stack([cols(f(i[n])[0]) for n in ("g_pre_mix", "g_post_mix", "g_pre_ffn", "g_post_ffn")], 1)),
        "lams": c(np.stack([f(i[n])[0] for n in ("lam_q1", "lam_k1", "lam_q2", "lam_k2")])),
        "lruv": c(lam4),
        "w_in": c(np.stack(tiles(w_in, [12, 13, 14, 15, 16, 17, 18, 19, 0, 1, 2, 3, 4, 5, 6, 7, 8, 9, 10, 11]))),
        "lru_cols": c(np.stack(lru, 1)),
        "w_gates": c(gates),
        "sconvT": c(feat(i["state_conv"][0]).transpose(3, 2, 1, 0)),
        "shT": c(feat(i["state_h"][0]).transpose(2, 1, 0)),
        "state_conv": c(f(i["state_conv"])[0]),
        "w_out": c(np.stack(tiles(f(i["w_out"])[0], range(KT)))),
        "w_ffn": c(np.stack(ffn).reshape(FT, P, 3 * KT, P)),
        "g_subln": c(f(i["g_subln"])),
        "cache_k": c(f(i["cache_k"])[0].reshape(-1, P, NH * P)),
        "cache_v": c(f(i["cache_v"])[0].reshape(-1, P, NH * P)),
        "page_table": c(f(i["page_table"]).reshape(1, -1)),
    }


def sample_constants():
    r = np.arange(RS)
    head = r // 2 % NH
    slope = 2.0 ** (-8.0 * (head + 1) / NH) / SCALE
    return {
        "half": (np.arange(P)[:, None] // DH == np.arange(2)).astype(np.float32),
        "pair": (r[:, None] // 2 == np.arange(BH)).astype(np.float32),
        "sign": (r[:, None] % 2 == np.arange(2)).astype(np.float32),
        "alibi": (slope[:, None] * (np.arange(PAST + 1) - PAST)).astype(np.float32),
    }


OUTS = {
    "yT": (P, KT, T),
    "z": (3 * NH, P, T),
    "hT": (P, LT, C9),
    "conv_new": (P, LT, 3 + NS),
    "conv_kept": (NS, 2, LT * P),
}
SCRATCH = {"mix": (KT, P, T), "x1": (P, KT, T), "h2": (P, KT, T)}


def program(nc, io):
    with ExitStack() as ctx:
        mods = {}
        for name, shape in [("gains_sb", [P, 4, KT]), ("silu_c", [P, KT, C9])] + [
                (n, [P, KT, C9]) for n in ("shift_m", "shift_f", "mul_m", "mul_f", "gate_m", "gate_f")] + [
                ("one", [P, 1]), ("bada", [P, 6 * KT]), ("ident", [P, P]), ("eps", [P, 1]), ("neglam", [P, 1]),
                ("sp2", [P, LT]), ("ones", [P, P])]:
            mods[name] = ctx.enter_context(nc.sbuf_tensor(name, shape, F32))
        mods["gains"] = mods["gains_sb"]
        modulation(nc, mods, io)
        input_projection(nc, mods, io)
        attention(nc, mods, io)
        sample_attention(nc, mods, io)
        output_projection(nc, mods, io)
        ffn(nc, mods, io)


def kernel(**inputs):
    import concourse.bacc as _bacc
    from concourse.bass_utils import run_bass_kernel_spmd as _run

    nc = _bacc.Bacc("TRN2", target_bir_lowering=False, num_devices=1)
    arrays = layouts(inputs)
    arrays.update(sample_constants())
    io = {}
    for name, a in arrays.items():
        io[name] = nc.dram_tensor(name, a.shape, mybir.dt.from_np(a.dtype), kind="ExternalInput").ap()
    for name, shape in OUTS.items():
        io[name] = nc.dram_tensor(name, shape, F32, kind="ExternalOutput").ap()
    for name, shape in SCRATCH.items():
        io[name] = nc.dram_tensor(name, shape, F32, kind="Internal").ap()
    program(nc, io)
    r = _run(nc, [arrays], core_ids=[0]).results[0]

    y = r["yT"].transpose(2, 1, 0).reshape(T, D)
    k = r["z"][NH:2 * NH].transpose(2, 0, 1)
    v = r["z"][2 * NH:].transpose(2, 0, 1)
    h = r["hT"].transpose(2, 1, 0).reshape(C9, LT * P)
    conv = r["conv_new"].transpose(2, 1, 0).reshape(3 + NS, LT * P)
    c = np.ascontiguousarray
    return (c(y[None, :SEQ]), c(y[SEQ:, None]), c(k[None, None, :SEQ]), c(v[None, None, :SEQ]), c(h[None, 0:1]),
            c(conv[None, None, 0:3]), c(k[SEQ:][None, :, None]), c(v[SEQ:][None, :, None]), c(h[None, 1:]),
            c(np.concatenate([r["conv_kept"], conv[3:, None]], 1)[None]))
```

```python
import math
from contextlib import ExitStack

import numpy as np

import concourse.bass as bass
from concourse import mybir

F32 = mybir.dt.float32
F32R = mybir.dt.float32r
I32 = mybir.dt.int32
ALU = mybir.AluOpType
ACT = mybir.ActivationFunctionType
AX = mybir.AxisListType

P = 128
D = 1024
KT = D // P
SEQ = 2048
NS = 8
T = SEQ + NS
NH = 4
DH = 64
ZT = 20
QKV0 = 8
LT = 4
FT = 22
C9 = 1 + NS
EPS = 1e-6
LAM_INIT = 0.8 - 0.6 * math.exp(0.0)
GELU_C = math.sqrt(2.0 / math.pi)

GW = [412, 412, 412, 412, 408]
GT = [0, 412, 824, 1236, 1648]
WMAX = 412
NG = len(GW)
RW = 4
ZC = (ZT - QKV0) // RW


def softcount(sem):
    n = [0]

    def mark(ins):
        n[0] += 1
        ins.then_inc(sem, 1)
        return n[0]
    return mark


AC = 512
AC0 = 2 * D // AC


def modulation(nc, mods, io):
    with ExitStack() as ctx:
        def sem(name):
            return ctx.enter_context(nc.semaphore("p0_" + name))
        wada = ctx.enter_context(nc.sbuf_tensor("p0_ada_ring", [P, AC0, KT, AC], F32))
        rows = ctx.enter_context(nc.sbuf_tensor("p0_rows", [C9, AC0 * AC], F32))
        ct = mods["silu_c"]
        th = ctx.enter_context(nc.sbuf_tensor("p0_cth", [P, KT, C9], F32))
        lams = ctx.enter_context(nc.sbuf_tensor("p0_lams", [P, 4, DH], F32))
        lprod = ctx.enter_context(nc.sbuf_tensor("p0_lprod", [P, DH], F32))
        lsum = ctx.enter_context(nc.sbuf_tensor("p0_lsum", [P, 4], F32))
        lru = ctx.enter_context(nc.sbuf_tensor("p0_lruv", [P, 4, 4], F32))
        prow = [ctx.enter_context(nc.psum_tensor(f"p0_prow{i}", [P, AC], F32)) for i in range(AC0)]
        pcol = ctx.enter_context(nc.psum_tensor("p0_pcol", [P, 16, C9], F32))
        mod = ctx.enter_context(nc.sbuf_tensor("p0_mod", [P, 16, C9], F32))
        gains, bada = mods["gains"], mods["bada"]
        c_in, b_in, ident = sem("c_in"), sem("b_in"), sem("ident")
        w_in = [sem(f"w_in{i}") for i in range(AC0)]
        row_done, col_done, tanh_done, silu_done, dv, ac, rows_ready = (
            sem("row_done"), sem("col_done"), sem("tanh_done"), sem("silu_done"), sem("dv"), sem("ac"), sem("rows"))
        block = ctx.enter_context(nc.Block())

        @block.sync
        def _(sp):
            sp.dma_start(ct[:], io["cT"]).then_inc(c_in, 16)
            for i in range(AC0):
                sp.dma_start(wada[:, i, :, :], io["w_ada"][i]).then_inc(w_in[i], 16)

        @block.gpsimd
        def _(pool):
            pool.memset(mods["one"][:], 1.0).then_inc(ident, 1)
            pool.memset(mods["ones"][:], 1.0).then_inc(ident, 1)
            pool.memset(mods["eps"][:], EPS).then_inc(ident, 1)
            pool.memset(mods["ident"][:], 0.0).then_inc(ident, 1)
            pool.wait_ge(ident, 4)
            pool.affine_select(out=mods["ident"][:], in_=mods["ident"][:], compare_op=ALU.not_equal, fill=1.0,
                               base=0, pattern=[[-1, P]], channel_multiplier=1).then_inc(ident, 1)

        @block.tensor
        def _(pe):
            pe.wait_ge(silu_done, 1)
            for i in range(AC0):
                pe.wait_ge(w_in[i], 16)
                for k in range(KT):
                    mm = pe.matmul(prow[i][0:C9, :], ct[:, k, :], wada[:, i, k, :], start=k == 0, stop=k == KT - 1)
                mm.then_inc(row_done, 1)
            pe.wait_ge(ident, 5)
            for j in range(16):
                pe.wait_ge(rows_ready, j // 4 + 1)
                pe.transpose(pcol[:, j, :], rows[:, j * P:(j + 1) * P], mods["ident"][0:C9, 0:C9]).then_inc(col_done, 1)

        @block.scalar
        def _(act):
            act.dma_start(bada[:], io["b_adaT"]).then_inc(b_in, 16)
            act.dma_start(gains[:], io["gains"]).then_inc(b_in, 16)
            act.dma_start(lams[:], io["lams"].partition_broadcast(P)).then_inc(b_in, 16)
            act.dma_start(lru[:], io["lruv"]).then_inc(b_in, 16)
            act.wait_ge(c_in, 16)
            act.activation(th[:], ct[:], ACT.Tanh, scale=0.5).then_inc(tanh_done, 1)
            act.wait_ge(dv, 5)
            act.activation(lsum[:, 2:4], lsum[:, 0:2], ACT.Exp).then_inc(ac, 1)
            act.activation(lru[:, 1, :], lru[:, 3, :], ACT.Exp, scale=-1.0).then_inc(ac, 1)
            act.wait_ge(ac, 2)
            act.wait_ge(ident, 1)
            act.activation(lru[:, 1, :], lru[:, 1, :], ACT.Ln, bias=mods["one"][:, 0:1]).then_inc(ac, 1)
            for i in range(AC0):
                act.wait_ge(row_done, i + 1)
                act.activation(rows[:, i * AC:(i + 1) * AC], prow[i][0:C9, :], ACT.Copy).then_inc(rows_ready, 1)

        @block.vector
        def _(dve):
            mark = softcount(dv)
            dve.wait_ge(b_in, 64)
            for i in range(2):
                mark(dve.tensor_tensor(lprod[:, :], lams[:, 2 * i, :], lams[:, 2 * i + 1, :], ALU.mult))
                dve.wait_ge(dv, 2 * i + 1)
                n = mark(dve.tensor_reduce(lsum[:, i:i + 1], lprod[:, :], AX.X, ALU.add))
                if i == 0:
                    dve.wait_ge(dv, n)
            n = mark(dve.scalar_tensor_tensor(out=lru[:, 3, :], in0=lru[:, 0, :], scalar=-1.0,
                                              in1=lru[:, 0, :], op0=ALU.mult, op1=ALU.max))
            n = mark(dve.tensor_scalar(lru[:, 2, :], lru[:, 0, :], -1.0, 0.0, ALU.mult, ALU.max))
            dve.wait_ge(tanh_done, 1)
            n = mark(dve.scalar_tensor_tensor(out=ct[:], in0=th[:], scalar=1.0, in1=ct[:],
                                              op0=ALU.add, op1=ALU.mult))
            dve.wait_ge(dv, n)
            dve.tensor_scalar(ct[:], ct[:], 0.5, None, ALU.mult).then_inc(silu_done, 1)
            dve.wait_ge(ac, 3)
            n = mark(dve.tensor_tensor(mods["neglam"][:, 0:1], lsum[:, 3:4], lsum[:, 2:3], ALU.subtract))
            dve.wait_ge(dv, n)
            mark(dve.tensor_scalar(mods["neglam"][:, 0:1], mods["neglam"][:, 0:1], LAM_INIT, None, ALU.subtract))
            n = mark(dve.tensor_tensor(lru[:, 2, :], lru[:, 2, :], lru[:, 1, :], ALU.add))
            dve.wait_ge(dv, n)
            mark(dve.tensor_scalar(mods["sp2"][:, :], lru[:, 2, :], -2.0, None, ALU.mult))
            dve.wait_ge(col_done, 16)
            n = mark(dve.tensor_tensor(mod[:], pcol[:], bada[:, 0:16].unsqueeze(2).broadcast_to((P, 16, C9)), ALU.add))
            dve.wait_ge(dv, n)
            mark(dve.tensor_copy(mods["shift_m"][:], mod[:, 0:KT, :]))
            mark(dve.scalar_tensor_tensor(out=mods["mul_m"][:], in0=mod[:, KT:2 * KT, :], scalar=1.0,
                                          in1=gains[:, 0, :].unsqueeze(2).broadcast_to((P, KT, C9)),
                                          op0=ALU.add, op1=ALU.mult))


def input_projection(nc, mods, io):
    with ExitStack() as ctx:
        def sem(name):
            return ctx.enter_context(nc.semaphore("p1_" + name))

        def buf(name, shape, dt=F32):
            return ctx.enter_context(nc.sbuf_tensor("p1_" + name, shape, dt))

        def bank(name):
            return ctx.enter_context(nc.psum_tensor("p1_" + name, [P, 512], F32))
        x = buf("x", [P, KT, WMAX])
        sq = buf("sq", [P, KT, WMAX])
        rstd = buf("rstd", [P, WMAX])
        ssum = buf("ssum", [P, WMAX])
        h_hi = [buf(f"h_hi{i}", [P, KT, WMAX], F32R) for i in range(2)]
        h_lo = [buf(f"h_lo{i}", [P, KT, WMAX], F32R) for i in range(2)]
        wraw = buf("wraw", [P, RW, D])
        w_hi = [buf(f"w_hi{i}", [P, D], F32R) for i in range(RW)]
        w_lo = [buf(f"w_lo{i}", [P, D], F32R) for i in range(RW)]
        xr = [buf(f"xr{i}", [P, LT, 3 + WMAX]) for i in range(2)]
        gr = buf("gr", [P, LT, WMAX])
        zout = [buf(f"zout{i}", [P, WMAX]) for i in range(RW)]
        u = buf("u", [P, LT, WMAX])
        tr = buf("tr", [P, LT, WMAX])
        ti = buf("ti", [P, LT, WMAX])
        ee = buf("ee", [P, LT, WMAX])
        gl = buf("gl", [P, LT, WMAX])
        lv = buf("lv", [P, 9, LT])
        wg = buf("wg", [P, 2 * LT, P])
        sconv = buf("sconv", [P, LT, 3, NS])
        sh = buf("sh", [P, LT, NS])
        hlast = buf("hlast", [P, LT, 1 + NS])
        proj = [bank(f"proj{i}") for i in range(2)]
        gps = [bank(f"gate{i}") for i in range(4)]
        nps = bank("norm")

        consts = sem("consts")
        x_in, w_in = sem("x_in"), [sem(f"w_in{i}") for i in range(RW)]
        raw_free, hi_done, lo_done, split_free = sem("raw_free"), sem("hi_done"), sem("lo_done"), sem("split_free")
        mm_done, bank_free = sem("mm_done"), sem("bank_free")
        z_out = [sem(f"z_out{i}") for i in range(RW)]
        dv, ac, gates, norm_mm, x_free, y_out, wg_zero, h_done, y_done = (
            sem("dv"), sem("ac"), sem("gates"), sem("norm_mm"), sem("x_free"), sem("y_out"), sem("wg_zero"),
            sem("h_done"), sem("y_done"))
        AT, DV = {}, {}

        block = ctx.enter_context(nc.Block())

        order_act = [("sq", 0), ("rsqrt", 0)] + [("hk%d" % k, 0) for k in range(KT)] + [("hi", 0)]
        for g in range(NG):
            order_act += [("sq", g + 1)] if g + 1 < NG else []
            order_act += [("g%d" % j, g) for j in range(2 * LT)] + [("gsq", g)]
            order_act += [("t2%d" % j, g) for j in range(LT)]
            order_act += [("gtanh", g), ("root", g)]
            order_act += [("rsqrt", g + 1)] if g + 1 < NG else []
            order_act += [("hk%d" % k, g + 1) for k in range(KT)] + [("hi", g + 1)] if g + 1 < NG else []
        AT = {name: i + 1 for i, name in enumerate(order_act)}
        order_dve = [("red", 0), ("rcp", 0), ("xn", 0), ("lo", 0)]
        for g in range(NG):
            if g + 1 < NG:
                order_dve += [("red", g + 1)]
            order_dve += [("head", g), ("conv", g), ("gelu_in", g), ("q", g), ("a", g), ("w", g)]
            if g + 1 < NG:
                order_dve += [("rcp", g + 1), ("xn", g + 1)]
            order_dve += [("bt", g), ("scan", g), ("y", g)]
            if g + 1 < NG:
                order_dve += [("lo", g + 1)]
        DV = {name: i + 1 for i, name in enumerate(order_dve)}

        @block.sync
        def _(sp):
            sp.dma_start(x[:, :, 0:GW[0]], io["xT"][:, :, 0:GW[0]]).then_inc(x_in, 16)
            sp.dma_start(lv[:], io["lru_cols"]).then_inc(consts, 16)
            sp.dma_start(sconv[:], io["sconvT"]).then_inc(consts, 16)
            sp.dma_start(sh[:], io["shT"]).then_inc(consts, 16)
            sp.wait_ge(wg_zero, 1)
            for i in range(2):
                for b in range(2):
                    sp.dma_start(wg[DH * b:DH * (b + 1), LT * i:LT * (i + 1), DH * b:DH * (b + 1)],
                                 io["w_gates"][i, b]).then_inc(consts, 16)

            def store_z(g, m):
                for s in range(RW):
                    sp.wait_ge(bank_free, m + (g * ZT + s + 3))
                    sp.dma_start(io["z"][m + (s - QKV0), :, GT[g]:GT[g] + GW[g]],
                                 zout[s][:, 0:GW[g]]).then_inc(z_out[s], 16)

            for g in range(NG):
                def load(m):
                    for s in range(RW):
                        sp.wait_ge(lo_done, m + (g * ZT + s + 1))
                        sp.dma_start(wraw[:, s, :], io["w_in"][m + s]).then_inc(w_in[s], 16)
                load(0)
                if g:
                    store_z(g - 1, ZT - RW)
                if g + 1 < NG:
                    sp.wait_ge(dv, DV["lo", g])
                    sp.dma_start(x[:, :, 0:GW[g + 1]],
                                 io["xT"][:, :, GT[g + 1]:GT[g + 1] + GW[g + 1]]).then_inc(x_in, 16)
                load(RW)
                if g:
                    sp.wait_ge(dv, DV["y", g - 1])
                    sp.dma_start(io["mix"][4:8].rearrange("j p t -> p j t")[:, :, GT[g - 1]:GT[g - 1] + GW[g - 1]],
                                 gl[:, :, 0:GW[g - 1]]).then_inc(y_out, 16)
                load(QKV0)
                with sp.Fori(QKV0 + RW, ZT - RW + 1, RW) as m:
                    load(m)
                    store_z(g, m - RW)
            store_z(NG - 1, ZT - RW)
            sp.wait_ge(dv, DV["y", NG - 1])
            sp.dma_start(io["mix"][4:8].rearrange("j p t -> p j t")[:, :, GT[-1]:T],
                         gl[:, :, 0:GW[-1]]).then_inc(y_out, 16)
            sp.dma_start(io["hT"], hlast[:]).then_inc(y_out, 16)
            last = GW[-1] - NS + 3
            sp.dma_start(io["conv_new"], xr[(NG - 1) % 2][:, :, last - 3:last + NS]).then_inc(y_out, 16)
            sp.dma_start(io["conv_kept"], io["state_conv"][:, 1:3, :]).then_inc(y_out, 16)
            sp.wait_ge(y_out, 16 * (NG + 3))
            for s in range(RW):
                sp.wait_ge(z_out[s], 16 * (1 + NG * ZC))

        @block.gpsimd
        def _(pool):
            pool.memset(wg[:], 0.0).then_inc(wg_zero, 1)
            pool.sem_inc(lo_done, RW)
            pool.sem_inc(bank_free, 2)
            for s in range(RW):
                pool.sem_inc(z_out[s], 16)
            pool.sem_inc(split_free, RW)
            with pool.Fori(0, NG * ZT - RW + 1, RW) as n:
                for s in range(RW):
                    pool.wait_ge(hi_done, n + (s + 1))
                    pool.tensor_tensor(w_lo[s][:], wraw[:, s, :], w_hi[s][:].bitcast(F32),
                                       ALU.subtract).then_inc(lo_done, 1)

        @block.tensor
        def _(pe):
            def norm_sum(g):
                pe.wait_ge(dv, DV["red", g])
                if g:
                    pe.wait_ge(ac, AT["rsqrt", g - 1])
                pe.matmul(nps[:, 0:GW[g]], mods["ones"][:], ssum[:, 0:GW[g]], start=True, stop=True).then_inc(norm_mm, 1)
            norm_sum(0)
            for g in range(NG):
                W = GW[g]

                def step(m, s):
                    pe.wait_ge(lo_done, m + (g * ZT + s + 1 + RW))
                    pe.wait_ge(bank_free, m + (g * ZT + s + 1))
                    i = 0
                    for k in range(KT):
                        ks = slice(k * P, (k + 1) * P)
                        for a, b in ((w_hi, h_hi), (w_hi, h_lo), (w_lo, h_hi)):
                            mm = pe.matmul(proj[s % 2][:, 0:W], a[s][:, ks], b[g % 2][:, k, 0:W],
                                           start=i == 0, stop=i == 3 * KT - 1)
                            i += 1
                    mm.then_inc(split_free, 1)
                pe.wait_ge(ac, AT["hi", g])
                pe.wait_ge(dv, DV["lo", g])
                with pe.Fori(0, QKV0 - RW + 1, RW) as m:
                    for s in range(RW):
                        step(m, s)
                pe.wait_ge(dv, DV["conv", g])
                if g == 0:
                    pe.wait_ge(consts, 16 * 7)
                for i in range(2 * LT):
                    j = i // 2
                    if i >= 4:
                        pe.wait_ge(ac, AT["g%d" % (i - 4), g])
                    elif g:
                        pe.wait_ge(ac, AT["g%d" % (i + 4), g - 1])
                    pe.matmul(gps[i % 4][:, 0:W], wg[:, LT * (i % 2) + j, :], u[:, j, 0:W],
                              start=True, stop=True).then_inc(gates, 1)
                if g + 1 < NG:
                    norm_sum(g + 1)
                with pe.Fori(QKV0, ZT - RW + 1, RW) as m:
                    for s in range(RW):
                        step(m, s)

        @block.scalar
        def _(act):
            done = softcount(ac)

            def mark(ins, name, g):
                assert done(ins) == AT[name, g], (name, g)

            def hi(n):
                s = n % RW
                act.wait_ge(w_in[s], 16 * (n // RW + 1))
                act.wait_ge(split_free, n + 1)
                act.activation(w_hi[s][:], wraw[:, s, :], ACT.Copy).then_inc(hi_done, 1)

            def evac(n, to, W):
                act.wait_ge(split_free, n + 1 + RW)
                act.activation(to, proj[n % 2][:, 0:W], ACT.Copy).then_inc(bank_free, 1)

            def square(g):
                act.wait_ge(x_in, 16 * (g + 1))
                if g:
                    act.wait_ge(dv, DV["red", g - 1])
                mark(act.activation(sq[:, :, 0:GW[g]], x[:, :, 0:GW[g]], ACT.Square), "sq", g)

            def std(g):
                act.wait_ge(norm_mm, g + 1)
                if g:
                    act.wait_ge(dv, DV["xn", g - 1])
                mark(act.activation(rstd[:, 0:GW[g]], nps[:, 0:GW[g]], ACT.Sqrt, scale=1.0 / D,
                                    bias=mods["eps"][:, 0:1]), "rsqrt", g)

            def modulate(g):
                act.wait_ge(dv, DV["xn", g])
                W = GW[g] - (NS if g == NG - 1 else 0)
                for k in range(KT):
                    mark(act.activation(x[:, k, 0:W], x[:, k, 0:W], ACT.Identity, scale=mods["mul_m"][:, k, 0:1],
                                        bias=mods["shift_m"][:, k, 0:1]), "hk%d" % k, g)

            def split_h(g):
                act.wait_ge(ac, AT["hk%d" % (KT - 1), g])
                if g >= 2:
                    act.wait_ge(split_free, RW + ZT * (g - 1))
                mark(act.activation(h_hi[g % 2][:, :, 0:GW[g]], x[:, :, 0:GW[g]], ACT.Copy), "hi", g)
            square(0)
            std(0)
            modulate(0)
            split_h(0)
            for n in range(RW - 1):
                hi(n)
            for g in range(NG):
                W = GW[g]
                last = g == NG - 1
                if g >= 2:
                    act.wait_ge(dv, DV["head", g - 1])

                def tanh_gates(i0):
                    for i in range(i0, i0 + LT):
                        act.wait_ge(gates, 2 * LT * g + i + 1)
                        if g and i == 0:
                            act.wait_ge(dv, DV["scan", g - 1])
                        to = (tr, ti)[i % 2]
                        mark(act.activation(to[:, i // 2, 0:W], gps[i % 4][:, 0:W], ACT.Tanh, scale=0.5,
                                            bias=lv[:, 5 + i % 2, i // 2:i // 2 + 1]), "g%d" % i, g)

                def tanh_log_a():
                    act.wait_ge(ac, AT["g7", g])
                    for j in range(LT):
                        mark(act.activation(tr[:, j, 0:W], tr[:, j, 0:W], ACT.Tanh, scale=mods["sp2"][:, j:j + 1],
                                            bias=mods["sp2"][:, j:j + 1]), "t2%d" % j, g)

                def gelu_square():
                    act.wait_ge(bank_free, g * ZT + QKV0 + 2)
                    if g:
                        act.wait_ge(y_out, 16 * g)
                    mark(act.activation(gl[:, :, 0:W], gr[:, :, 0:W], ACT.Square), "gsq", g)

                def gelu_tanh():
                    act.wait_ge(dv, DV["gelu_in", g])
                    mark(act.activation(gl[:, :, 0:W], gl[:, :, 0:W], ACT.Tanh, scale=GELU_C), "gtanh", g)

                def roots():
                    act.wait_ge(dv, DV["q", g])
                    mark(act.activation(tr[:, :, 0:W], tr[:, :, 0:W], ACT.Sqrt, scale=-1.0), "root", g)
                    if not last:
                        std(g + 1)

                between = {3: [] if last else [lambda: square(g + 1)], 7: [lambda: tanh_gates(0)],
                           8: [lambda: tanh_gates(LT)], 9: [gelu_square], 10: [tanh_log_a],
                           11: [gelu_tanh], 13: [roots]}
                if not last:
                    between |= {15: [lambda: modulate(g + 1)], 17: [lambda: split_h(g + 1)]}
                for m in range(ZT):
                    n = g * ZT + m
                    if n + RW - 1 < NG * ZT:
                        hi(n + RW - 1)
                    if m < LT:
                        evac(n, xr[g % 2][:, m, 3:3 + W], W)
                    elif m < QKV0:
                        if m == LT and g:
                            act.wait_ge(dv, DV["y", g - 1])
                        evac(n, gr[:, m - LT, 0:W], W)
                    else:
                        act.wait_ge(z_out[m % RW], 16 * (1 + g * ZC + (m - QKV0) // RW))
                        evac(n, zout[m % RW][:, 0:W], W)
                    for f in between.get(m, []):
                        f()

        @block.vector
        def _(dve):
            done = softcount(dv)
            pd = [0]

            def mark(ins, name, g):
                assert done(ins) == DV[name, g], (name, g)

            def link(ins):
                pd[0] += 1
                ins.then_inc(y_done, 1)
                dve.wait_ge(y_done, pd[0])

            def reduce(g):
                dve.wait_ge(ac, AT["sq", g])
                if g:
                    dve.wait_ge(norm_mm, g)
                mark(dve.tensor_reduce(ssum[:, 0:GW[g]], sq[:, :, 0:GW[g]].rearrange("p k t -> p t k"),
                                       AX.X, ALU.add), "red", g)

            def normalise(g):
                W = GW[g]
                dve.wait_ge(ac, AT["rsqrt", g])
                mark(dve.reciprocal(rstd[:, 0:W], rstd[:, 0:W]), "rcp", g)
                dve.wait_ge(dv, DV["rcp", g])
                bc = rstd[:, 0:W].unsqueeze(1).broadcast_to((P, KT, W))
                if g < NG - 1:
                    mark(dve.tensor_tensor(x[:, :, 0:W], x[:, :, 0:W], bc, ALU.mult), "xn", g)
                else:
                    link(dve.tensor_tensor(x[:, :, 0:W], x[:, :, 0:W], bc, ALU.mult))
                    xs = x[:, :, W - NS:W]
                    link(dve.tensor_tensor(xs, xs, mods["mul_m"][:, :, 1:C9], ALU.mult))
                    mark(dve.tensor_tensor(xs, xs, mods["shift_m"][:, :, 1:C9], ALU.add), "xn", g)

            def low(g):
                W = GW[g]
                dve.wait_ge(ac, AT["hi", g])
                mark(dve.tensor_tensor(h_lo[g % 2][:, :, 0:W], x[:, :, 0:W], h_hi[g % 2][:, :, 0:W].bitcast(F32),
                                       ALU.subtract), "lo", g)
            dve.wait_ge(consts, 16 * 7)
            link(dve.tensor_scalar(lv[:, 5:7, :], lv[:, 5:7, :], 0.5, None, ALU.mult))
            reduce(0)
            normalise(0)
            low(0)
            for g in range(NG):
                W = GW[g]
                last = g == NG - 1
                WP = W - (NS if last else 0)
                if not last:
                    reduce(g + 1)
                if g == 0:
                    mark(dve.memset(xr[0][:, :, 0:3], 0.0), "head", g)
                else:
                    mark(dve.tensor_copy(xr[g % 2][:, :, 0:3], xr[(g - 1) % 2][:, :, GW[g - 1]:GW[g - 1] + 3]), "head", g)
                dve.wait_ge(dv, DV["head", g])
                dve.wait_ge(bank_free, g * ZT + 3 + 3)
                if g:
                    dve.wait_ge(gates, 2 * LT * g)
                for j in range(LT):
                    X = xr[g % 2]
                    link(dve.tensor_scalar(u[:, j, 0:WP], X[:, j, 0:WP], lv[:, 0, j:j + 1], lv[:, 4, j:j + 1],
                                           ALU.mult, ALU.add))
                    for t in range(1, 4):
                        ins = dve.scalar_tensor_tensor(out=u[:, j, 0:WP], in0=X[:, j, t:t + WP],
                                                       scalar=lv[:, t, j:j + 1], in1=u[:, j, 0:WP],
                                                       op0=ALU.mult, op1=ALU.add)
                        if t < 3 or last:
                            link(ins)
                    if last:
                        link(dve.tensor_scalar(u[:, j, WP:W], sconv[:, j, 0, :], lv[:, 0, j:j + 1], lv[:, 4, j:j + 1],
                                               ALU.mult, ALU.add))
                        for t in range(1, 4):
                            src = sconv[:, j, t, :] if t < 3 else X[:, j, 3 + WP:3 + W]
                            ins = dve.scalar_tensor_tensor(out=u[:, j, WP:W], in0=src,
                                                           scalar=lv[:, t, j:j + 1], in1=u[:, j, WP:W],
                                                           op0=ALU.mult, op1=ALU.add)
                            if t < 3:
                                link(ins)
                    if j < LT - 1:
                        link(ins)
                mark(ins, "conv", g)
                dve.wait_ge(ac, AT["gsq", g])
                A = lambda b: b[:, :, 0:W]
                link(dve.tensor_scalar(A(gl), A(gl), 0.044715, 1.0, ALU.mult, ALU.add))
                mark(dve.tensor_tensor(A(gl), A(gl), A(gr), ALU.mult), "gelu_in", g)
                dve.wait_ge(ac, AT["t23", g])
                link(dve.tensor_scalar(A(ee), A(tr), -1.0, 1.0, ALU.mult, ALU.add))
                link(dve.reciprocal(A(ee), A(ee)))
                link(dve.scalar_tensor_tensor(out=A(ee), in0=A(tr), scalar=2.0, in1=A(ee), op0=ALU.mult, op1=ALU.mult))
                mark(dve.scalar_tensor_tensor(out=A(tr), in0=A(ee), scalar=2.0, in1=A(ee), op0=ALU.add, op1=ALU.mult), "q", g)
                dve.wait_ge(dv, DV["q", g])
                mark(dve.tensor_scalar(A(ee), A(ee), 1.0, None, ALU.add), "a", g)
                mark(dve.scalar_tensor_tensor(out=A(ti), in0=A(ti), scalar=1.0, in1=A(u), op0=ALU.add, op1=ALU.mult), "w", g)
                if not last:
                    normalise(g + 1)
                dve.wait_ge(ac, AT["root", g])
                dve.wait_ge(dv, DV["w", g])
                mark(dve.scalar_tensor_tensor(out=A(ti), in0=A(ti), scalar=0.5, in1=A(tr), op0=ALU.mult, op1=ALU.mult), "bt", g)
                dve.wait_ge(dv, DV["bt", g])
                for j in range(LT):
                    init = 0.0 if g == 0 else hlast[:, j, 0:1]
                    link(dve.tensor_tensor_scan(u[:, j, 0:WP], ee[:, j, 0:WP], ti[:, j, 0:WP], init, ALU.mult, ALU.add))
                if last:
                    link(dve.tensor_tensor(u[:, :, WP:W], ee[:, :, WP:W], sh[:, :, :], ALU.mult))
                    link(dve.tensor_tensor(u[:, :, WP:W], u[:, :, WP:W], ti[:, :, WP:W], ALU.add))
                    link(dve.tensor_copy(hlast[:, :, 1:1 + NS], u[:, :, WP:W]))
                mark(dve.tensor_copy(hlast[:, :, 0:1], u[:, :, WP - 1:WP]), "scan", g)
                dve.wait_ge(dv, DV["scan", g])
                dve.wait_ge(ac, AT["gtanh", g])
                link(dve.scalar_tensor_tensor(out=A(gl), in0=A(gl), scalar=1.0, in1=A(gr), op0=ALU.add, op1=ALU.mult))
                mark(dve.scalar_tensor_tensor(out=A(gl), in0=A(u), scalar=0.5, in1=A(gl), op0=ALU.mult, op1=ALU.mult), "y", g)
                if not last:
                    low(g + 1)


QB = 128
UQ = 256
NB = SEQ // QB
NU = SEQ // UQ
SCALE = DH ** -0.5
SC = 512
SCB = SC // P
MASKED = -1e30
LAG = 2
LATE = 2
POOLED = (0, 1)
ADA0 = 2 * KT
NADA = 4 * KT


def chunks(b):
    L = QB * (b + 1)
    return [(c, min(c + SC, L)) for c in range(0, L, SC)]


def attention(nc, mods, io):
    with ExitStack() as ctx:
        def sem(name):
            return ctx.enter_context(nc.semaphore("p2_" + name))

        def buf(name, shape, dt=F32):
            return ctx.enter_context(nc.sbuf_tensor("p2_" + name, shape, dt))

        def bank(name):
            return ctx.enter_context(nc.psum_tensor("p2_" + name, [P, 512], F32))
        raw = [buf(f"raw{i}", [P, 4, UQ]) for i in range(2)]
        vraw = [buf(f"vraw{i}", [P, UQ]) for i in range(2)]
        qs = [buf(f"qs{i}", [P, 2, UQ], F32R) for i in range(2)]
        qm = [buf(f"qm{i}", [P, 2, UQ]) for i in range(2)]
        k_hi = buf("k_hi", [P, 2, SEQ], F32R)
        k_lo = buf("k_lo", [P, 2, SEQ], F32R)
        v_hi = buf("v_hi", [P, NB, P], F32R)
        v_lo = buf("v_lo", [P, NB, P], F32R)
        sc = [buf(f"sc{i}", [P, 2, SEQ]) for i in range(4)]
        p_hi = buf("p_hi", [P, NB, UQ], F32R)
        p_lo = buf("p_lo", [P, NB, UQ], F32R)
        praw = [buf(f"praw{i}", [P, SC]) for i in range(2)]
        dist = buf("dist", [P, SEQ])
        bias = buf("bias", [P, SEQ])
        slope = buf("slope", [P, NH])
        mx = [buf(f"mx{i}", [P, 2, 4]) for i in range(2)]
        nm = [buf(f"nm{i}", [P, 2]) for i in range(2)]
        sums = [buf(f"sums{i}", [P, 2]) for i in range(2)]
        rec = [buf(f"rec{i}", [P, 2]) for i in range(2)]
        ratio = [buf(f"ratio{i}", [P, 1]) for i in range(2)]
        diag = buf("diag", [P, 2, P])
        rb = buf("rb", [P, UQ])
        osb = [buf(f"osb{i}", [P, UQ]) for i in range(2)]
        spare = buf("spare", [P, 80])
        ada = [buf(f"ada{i}", [P, KT, P]) for i in range(2)]
        SB = [bank(f"s{i}") for i in range(4)]
        TB = [bank(f"t{i}") for i in range(2)]
        OB = bank("o")
        VB = bank("v")

        raw_in, v_in, ada_in, o_out = ([sem("raw_in0"), sem("raw_in1")], [sem("v_in0"), sem("v_in1")],
                                       [sem("ada_in0"), sem("ada_in1")], [sem("o_out0"), sem("o_out1")])
        names = ("qk", "tp", "pv", "vt", "ttr", "nmax", "comb", "lo", "rc", "vlo", "oe", "bs", "ex", "hi", "dg",
                 "qkh", "vhi", "rbd", "qkl", "mred", "recip", "praw", "plo", "adm", "ads", "init")
        S = {n: sem(n) for n in names}
        per_b = [len(chunks(b)) for b in range(NB)]
        before = [sum(per_b[:b]) for b in range(NB + 1)]
        ALL = before[NB]
        kinds = [i in POOLED for b in range(NB) for i in range(per_b[b])]
        by_dve = [sum(not p for p in kinds[:r]) for r in range(ALL + 1)]
        by_pool = [sum(kinds[:r]) for r in range(ALL + 1)]
        assert by_pool[ALL] % 2 == 0 and ALL % 2 == 0
        TOT = {"qk": 2 * ALL, "tp": ALL, "pv": NU, "vt": NU, "ttr": 2 * ALL, "nmax": NB, "comb": ALL,
               "lo": by_dve[ALL], "rc": NB, "vlo": NU, "oe": NU, "bs": 1, "ex": NB, "hi": ALL, "dg": NB, "qkh": NU,
               "vhi": NU, "rbd": NU, "qkl": 2 * NU, "mred": NB, "recip": NB, "praw": by_pool[ALL],
               "plo": by_pool[ALL], "adm": NU, "ads": NU}

        def wait_sem(e, s, h, per_head, count):
            if not isinstance(h, int) or h * per_head + count > 0:
                e.wait_ge(s, h * per_head + count)

        def wait(e, name, h, count):
            wait_sem(e, S[name], h, TOT[name], count)

        def read_out(e, h, r):
            if r < 0:
                h, r = h - 1, r + ALL
            if kinds[r]:
                wait(e, "praw", h, by_pool[r + 1])
            else:
                wait(e, "lo", h, by_dve[r + 1])

        def real(h):
            return not isinstance(h, int) or 0 <= h < NH

        def back(h, b):
            return (h, b) if b >= 0 else (h - 1, b + NB)

        def unit_back(h, j):
            return (h, j) if j >= 0 else (h - 1, j + NU)

        def heads(e, step):
            for b in range(NB):
                step(0, b)
            with e.Fori(1, NH) as h:
                for b in range(NB):
                    step(h, b)
            for b in range(4):
                step(NH, b)

        block = ctx.enter_context(nc.Block())

        @block.gpsimd
        def _(pool):
            for i in range(2):
                pool.memset(qm[i][:], 0.0).then_inc(S["init"], 1)
            pool.wait_ge(S["init"], 2)
            pool.iota(dist[:], pattern=[[1, SEQ]], base=-(SEQ - QB), channel_multiplier=-1,
                      allow_small_or_imprecise_dtypes=True).then_inc(S["init"], 1)
            pool.wait_ge(S["init"], 3)
            pool.affine_select(out=dist[:], in_=dist[:], compare_op=ALU.is_ge, fill=MASKED, base=SEQ - QB,
                               pattern=[[-1, SEQ]], channel_multiplier=1).then_inc(S["init"], 1)
            for h in range(NH):
                pool.memset(slope[:, h:h + 1], 2.0 ** (-8.0 * (h + 1) / NH) / SCALE).then_inc(S["init"], 1)

            def low(h, j):
                wait(pool, "qkh", h, j + 1)
                pool.tensor_tensor(qs[j % 2][:], raw[j % 2][:, 0:2, :], qm[j % 2][:], ALU.subtract
                                   ).then_inc(S["qkl"], 1)
                ks = slice(UQ * j, UQ * (j + 1))
                pool.tensor_tensor(k_lo[:, :, ks], raw[j % 2][:, 2:4, :], k_hi[:, :, ks].bitcast(F32),
                                   ALU.subtract).then_inc(S["qkl"], 1)

            def step(h, b):
                if b == 0 and real(h):
                    low(h, 0)
                    low(h, 1)
                ht, bt = back(h, b - LAG)
                if real(ht):
                    for i in POOLED:
                        if i < per_b[bt]:
                            c0, c1 = chunks(bt)[i]
                            r, n = before[bt] + i, (c1 - c0) // P
                            s = by_pool[r]
                            wait(pool, "praw", ht, s + 1)
                            ps = (slice(None), slice(SCB * i, SCB * i + n), slice(QB * (bt % 2), QB * (bt % 2 + 1)))
                            pool.tensor_tensor(p_lo[ps], praw[s % 2][:, 0:c1 - c0].rearrange("p (s q) -> p s q", q=P),
                                               p_hi[ps].bitcast(F32), ALU.subtract).then_inc(S["plo"], 1)
                if b and b % 2 == 0 and b // 2 + 1 < NU and real(h):
                    low(h, b // 2 + 1)
            pool.wait_ge(S["init"], 4 + NH)
            heads(pool, step)

        @block.sync
        def _(sp):
            def load_qk(h, j):
                ts = slice(UQ * j, UQ * (j + 1))
                wait(sp, "qkl", h, 2 * (j - 1))
                for part in (slice(0, DH), slice(DH, P)):
                    sp.dma_start(raw[j % 2][part, 0:2, :], io["z"][h].rearrange("(c p) t -> p c t", c=2)[:, :, ts]
                                 ).then_inc(raw_in[j % 2], 16)
                    sp.dma_start(raw[j % 2][part, 2:4, :],
                                 io["z"][NH:2 * NH][h].rearrange("(c p) t -> p c t", c=2)[:, :, ts]
                                 ).then_inc(raw_in[j % 2], 16)

            def load(h, j):
                ts = slice(UQ * j, UQ * (j + 1))
                wait(sp, "vt", h, j - 1)
                sp.dma_start(vraw[j % 2][:], io["z"][2 * NH:3 * NH][h, :, ts]).then_inc(v_in[j % 2], 16)
                wait(sp, "adm", h, j - 1)
                sp.dma_start(ada[j % 2][:], io["w_ada"][AC0:][h * 2 + j // 4, :, :, P * (j % 4):P * (j % 4 + 1)]
                             ).then_inc(ada_in[j % 2], 16)

            def store(h, j):
                wait(sp, "oe", h, j + 1)
                sp.dma_start(io["mix"][h, :, UQ * j:UQ * (j + 1)], osb[j % 2][:]).then_inc(o_out[j % 2], 16)

            def step(h, b):
                if b % 2 == 0:
                    if real(h):
                        if b == 0:
                            load_qk(h, 0)
                        if b // 2 + 1 < NU:
                            load_qk(h, b // 2 + 1)
                        load(h, b // 2)
                    ho, jo = unit_back(h, b // 2 - 4)
                    if real(ho):
                        store(ho, jo)
            heads(sp, step)
            for j in range(NU - 2, NU):
                store(NH - 1, j)
            for i in range(2):
                sp.wait_ge(o_out[i], 16 * NH * NU // 2)

        @block.tensor
        def _(pe):
            def scores(h, b, i):
                j = b // 2
                if i == 0 and b % 2 == 0:
                    wait(pe, "qkl", h, 2 * (j + 1))
                c0, c1 = chunks(b)[i]
                for c in range(2):
                    r = 2 * (before[b] + i) + c
                    wait(pe, "ttr", h, r - 3)
                    for n, kk in enumerate((k_hi, k_lo)):
                        mm = pe.matmul(SB[r % 4][:, 0:c1 - c0], qs[j % 2][:, c, QB * (b % 2):QB * (b % 2 + 1)],
                                       kk[:, c, c0:c1], start=n == 0, stop=n == 1)
                    mm.then_inc(S["qk"], 1)

            def turn(h, b, i):
                r = before[b] + i
                c0, c1 = chunks(b)[i]
                wait(pe, "comb", h, r + 1)
                read_out(pe, h, r - 2)
                for s, k0 in enumerate(range(c0, c1, P)):
                    mm = pe.transpose(TB[r % 2][:, s * P:(s + 1) * P], sc[b % 4][:, 0, k0:k0 + P], mods["ident"][:])
                mm.then_inc(S["tp"], 1)

            def turn_v(h, j):
                wait_sem(pe, v_in[j % 2], h, 16 * NU // 2, 16 * (j // 2 + 1))
                wait(pe, "ads", h, j)
                for s in range(2):
                    mm = pe.transpose(VB[:, s * P:(s + 1) * P], vraw[j % 2][:, s * P:(s + 1) * P], mods["ident"][:])
                mm.then_inc(S["vt"], 1)

            def modulate(h, j):
                wait_sem(pe, ada_in[j % 2], h, 16 * NU // 2, 16 * (j // 2 + 1))
                wait(pe, "vlo", h, j + 1)
                for k in range(KT):
                    mm = pe.matmul(VB[:, 0:C9], ada[j % 2][:, k, :], mods["silu_c"][:, k, :], start=k == 0,
                                   stop=k == KT - 1)
                mm.then_inc(S["adm"], 1)

            def inverse_sums(h, j):
                wait(pe, "oe", h, j)
                wait(pe, "dg", h, 2 * j + 2)
                for s in range(2):
                    pe.matmul(OB[:, UQ + s * P:UQ + (s + 1) * P], mods["ones"][:], diag[:, s, :], start=True,
                              stop=True)

            def weigh(h, j, i):
                blocks = range(SCB * i, min(SCB * (i + 1), 2 * j + 2))
                r = before[2 * j + 1] + i
                if i == 0:
                    wait(pe, "vlo", h, j + 1)
                if kinds[r]:
                    wait(pe, "plo", h, by_pool[r + 1])
                else:
                    wait(pe, "lo", h, by_dve[r + 1])
                for kb in blocks:
                    q0 = QB if kb == 2 * j + 1 else 0
                    for n, (a, p) in enumerate(((v_hi, p_hi), (v_hi, p_lo), (v_lo, p_hi))):
                        mm = pe.matmul(OB[:, q0:UQ], a[:, kb, :], p[:, kb, q0:UQ], start=kb == 0 and n == 0,
                                       stop=kb == 2 * j + 1 and n == 2)
                if kb == 2 * j + 1:
                    mm.then_inc(S["pv"], 1)

            def step(h, b):
                ht, bt = back(h, b - LAG)
                nt = per_b[bt] if real(ht) else 0
                ahead = []
                if real(h):
                    ahead = [(b, i) for i in range(1 if b else 0, per_b[b])] + [(b + 1, 0)] * (b + 1 < NB)
                hw, jw = unit_back(h, b // 2 - 2)
                nw = -(-(2 * jw + 2) // SCB) if b % 2 == 0 and real(hw) else 0
                if nw:
                    inverse_sums(hw, jw)
                hv, jv = unit_back(h, (b - 3) // 2)
                late = LATE if b == 0 and nt else 0
                for i in range(max(nt, nw, late + len(ahead), 1)):
                    if i >= late and ahead:
                        scores(h, *ahead.pop(0))
                    if i < nw:
                        weigh(hw, jw, i)
                    if i < nt:
                        turn(ht, bt, i)
                    if i == 0 and b % 2 and real(hv):
                        turn_v(hv, jv)
                if b % 2 == 0 and real(hw):
                    modulate(hw, jw)
            heads(pe, step)

        @block.scalar
        def _(act):
            act.wait_ge(S["init"], 2)

            def prepare(h, j):
                wait_sem(act, raw_in[j % 2], h, 64 * NU // 2, 64 * (j // 2 + 1))
                wait(act, "qk", h, 2 * before[2 * j - 2] if j else 0)
                act.activation(qm[j % 2][DH:P, :, :].bitcast(F32R), raw[j % 2][DH:P, 0:2, :], ACT.Copy)
                act.activation(k_hi[:, :, UQ * j:UQ * (j + 1)], raw[j % 2][:, 2:4, :], ACT.Copy).then_inc(S["qkh"], 1)

            def turned(h, b, i):
                c0, c1 = chunks(b)[i]
                r, n = before[b] + i, (c1 - c0) // P
                wait(act, "tp", h, r + 1)
                src = TB[r % 2][:, 0:c1 - c0]
                act.activation(p_hi[:, SCB * i:SCB * i + n, QB * (b % 2):QB * (b % 2 + 1)],
                               src.rearrange("p (s q) -> p s q", q=P), ACT.Copy).then_inc(S["hi"], 1)
                if kinds[r]:
                    s = by_pool[r]
                    wait(act, "plo", h, s - 1)
                    act.activation(praw[s % 2][:, 0:c1 - c0], src, ACT.Copy).then_inc(S["praw"], 1)

            def spread_sum(h, b):
                wait(act, "rc", h, b + 1)
                act.activation(diag[:, b % 2, :], mods["ident"][:], ACT.Copy, scale=rec[b % 2][:, 0:1]
                               ).then_inc(S["dg"], 1)

            def exps(h, b, c):
                if c == 0:
                    wait(act, "nmax", h, b + 1)
                L = QB * (b + 1)
                ins = act.activation(sc[b % 4][:, c, 0:L], sc[b % 4][:, c, 0:L], ACT.Exp, scale=SCALE,
                                     bias=nm[b % 2][:, c:c + 1], accum_out=sums[b % 2][:, c:c + 1])
                if c:
                    ins.then_inc(S["ex"], 1)

            def sums_row(h, j):
                wait(act, "pv", h, j + 1)
                act.activation(rb[:], OB[:, UQ:2 * UQ], ACT.Copy).then_inc(S["rbd"], 1)

            def values(h, j):
                wait(act, "vt", h, j + 1)
                act.activation(v_hi[:, 2 * j:2 * j + 2, :], VB[:, 0:UQ].rearrange("p (s d) -> p s d", s=2), ACT.Copy
                               ).then_inc(S["vhi"], 1)

            def step(h, b):
                if b == 0 and real(h):
                    prepare(h, 0)
                he, be = back(h, b - 1)
                ht, bt = back(h, b - LAG)
                nt = per_b[bt] if real(ht) else 0
                if b % 2 == 0 and b // 2 + 1 < NU and real(h):
                    prepare(h, b // 2 + 1)
                if real(he):
                    exps(he, be, 0)
                if real(he):
                    exps(he, be, 1)
                if nt:
                    turned(ht, bt, 0)
                if b % 2:
                    ho, jo = unit_back(h, (b - 5) // 2)
                    if real(ho):
                        sums_row(ho, jo)
                for i in range(1, nt):
                    turned(ht, bt, i)
                if nt:
                    spread_sum(ht, bt)
                if b % 2:
                    hv, jv = unit_back(h, (b - 3) // 2)
                    if real(hv):
                        values(hv, jv)
            heads(act, step)

        @block.vector
        def _(dve):
            dve.wait_ge(S["init"], 4 + NH)

            def scored(h, b, i, c):
                if i == 0 and c == 0:
                    hs, bs = back(h, b - 4)
                    if real(hs):
                        wait(dve, "tp", hs, before[bs + 1])
                y0 = SEQ - QB * (b + 1)
                c0, c1 = chunks(b)[i]
                r = 2 * (before[b] + i) + c
                wait(dve, "qk", h, r + 1)
                if not isinstance(h, int):
                    dve.memset(spare[:, r:r + 1], 0.0)
                dve.tensor_tensor_reduce(out=sc[b % 4][:, c, c0:c1], in0=SB[r % 4][:, 0:c1 - c0],
                                         in1=bias[:, y0 + c0:y0 + c1], scale=1.0, scalar=-3e38, op0=ALU.add,
                                         op1=ALU.max, accum_out=mx[b % 2][:, c, i:i + 1]).then_inc(S["ttr"], 1)

            def maxima(h, b):
                wait(dve, "ttr", h, 2 * before[b + 1])
                dve.tensor_reduce(nm[b % 2][:], mx[b % 2][:, :, 0:per_b[b]], AX.X, ALU.max).then_inc(S["mred"], 1)

            def negate(h, b):
                wait(dve, "mred", h, b + 1)
                dve.tensor_scalar(nm[b % 2][:], nm[b % 2][:], -SCALE, None, ALU.mult).then_inc(S["nmax"], 1)

            def invert(h, b):
                wait(dve, "ex", h, b + 1)
                wait(dve, "dg", h, b - 1)
                dve.reciprocal(rec[b % 2][:], sums[b % 2][:]).then_inc(S["recip"], 1)

            def ratios(h, b):
                wait(dve, "recip", h, b + 1)
                dve.scalar_tensor_tensor(out=ratio[b % 2][:], in0=sums[b % 2][:, 0:1], scalar=rec[b % 2][:, 1:2],
                                         in1=mods["neglam"][:, 0:1], op0=ALU.mult, op1=ALU.mult).then_inc(S["rc"], 1)

            def combine(h, b, i):
                if i == 0:
                    wait(dve, "rc", h, b + 1)
                c0, c1 = chunks(b)[i]
                dve.scalar_tensor_tensor(out=sc[b % 4][:, 0, c0:c1], in0=sc[b % 4][:, 1, c0:c1],
                                         scalar=ratio[b % 2][:, 0:1], in1=sc[b % 4][:, 0, c0:c1],
                                         op0=ALU.mult, op1=ALU.add).then_inc(S["comb"], 1)

            def low(h, b, i):
                c0, c1 = chunks(b)[i]
                r, n = before[b] + i, (c1 - c0) // P
                if not kinds[r]:
                    wait(dve, "hi", h, r + 1)
                    ps = (slice(None), slice(SCB * i, SCB * i + n), slice(QB * (b % 2), QB * (b % 2 + 1)))
                    dve.tensor_tensor(p_lo[ps], TB[r % 2][:, 0:c1 - c0].rearrange("p (s q) -> p s q", q=P),
                                      p_hi[ps].bitcast(F32), ALU.subtract).then_inc(S["lo"], 1)

            def output(h, j):
                wait(dve, "rbd", h, j + 1)
                wait_sem(dve, o_out[j % 2], h, 16 * NU // 2, 16 * (j // 2))
                dve.tensor_tensor(osb[j % 2][:], OB[:, 0:UQ], rb[:], ALU.mult).then_inc(S["oe"], 1)

            def values(h, j):
                wait(dve, "vhi", h, j + 1)
                dve.tensor_tensor(v_lo[:, 2 * j:2 * j + 2, :], VB[:, 0:UQ].rearrange("p (s d) -> p s d", s=2),
                                  v_hi[:, 2 * j:2 * j + 2, :].bitcast(F32), ALU.subtract).then_inc(S["vlo"], 1)

            def modulated(h, j):
                wait(dve, "adm", h, j + 1)
                if isinstance(h, int):
                    n = h * NU + j
                    out, bada = mods["mod"][:, n:n + 1, :], mods["bada"][:, ADA0 + n:ADA0 + n + 1]
                else:
                    out, bada = mods["mod"][:, bass.ds(h * NU + j, 1), :], mods["bada"][:, bass.ds(h * NU + (ADA0 + j), 1)]
                dve.tensor_tensor(out, VB[:, 0:C9].unsqueeze(1), bada.unsqueeze(2).broadcast_to((P, 1, C9)), ALU.add
                                  ).then_inc(S["ads"], 1)

            def set_bias(h):
                dve.tensor_scalar(bias[:], dist[:], slope[:, h:h + 1] if isinstance(h, int) else slope[:, bass.ds(h, 1)],
                                  None, ALU.mult).then_inc(S["bs"], 1)
                wait(dve, "bs", h, 1)

            def step(h, b):
                ht, bt = back(h, b - LAG)
                nt = per_b[bt] if real(ht) else 0
                ns = per_b[b] if real(h) else 0
                if nt:
                    invert(ht, bt)
                late = LATE if b == 0 and nt else 0
                if b == 0 and ns:
                    set_bias(h)
                if late:
                    ratios(ht, bt)
                for i in range(max(nt, ns + late, 1)):
                    if 0 <= i - late < ns:
                        scored(h, b, i - late, 0)
                        if i == 0 and nt:
                            ratios(ht, bt)
                        scored(h, b, i - late, 1)
                    elif i == 0 and nt and not late:
                        ratios(ht, bt)
                    if i < nt:
                        combine(ht, bt, i)
                        if i:
                            low(ht, bt, i - 1)
                        else:
                            hl, bl = back(ht, bt - 1)
                            if real(hl):
                                low(hl, bl, per_b[bl] - 1)
                    if i == 0 and b % 2:
                        ha, ja = unit_back(h, (b - 5) // 2)
                        if real(ha):
                            modulated(ha, ja)
                if ns:
                    maxima(h, b)
                    negate(h, b)
                if b % 2:
                    ho, jo = unit_back(h, (b - 5) // 2)
                    if real(ho):
                        output(ho, jo)
                    hv, jv = unit_back(h, (b - 3) // 2)
                    if real(hv):
                        values(hv, jv)
                if not real(h) and b == 1:
                    low(ht, bt, nt - 1)
            heads(dve, step)


PG = 128
NPG = 4
POOL = 40
PAST = NPG * PG
HC = 2 * NH
RS = NS * HC
BH = NS * NH
KR = 4


def sample_attention(nc, mods, io):
    with ExitStack() as ctx:
        def sem(name):
            return ctx.enter_context(nc.semaphore("ps_" + name))

        def buf(name, shape, dt=F32):
            return ctx.enter_context(nc.sbuf_tensor("ps_" + name, shape, dt))

        def bank(name):
            return ctx.enter_context(nc.psum_tensor("ps_" + name, [P, 512], F32))
        keys = [buf(f"keys{i}", [PG, NPG, 2 * DH * NH]) for i in range(KR)]
        vals = buf("vals", [PG, NS, NPG, P * NH])
        prod = buf("prod", [PG, NPG, HC * DH])
        table = buf("table", [1, NS * NPG], I32)
        zs = buf("zs", [P, 3 * NH, NS])
        qrow = buf("qrow", [NS, NH * P])
        rowsel = buf("rowsel", [NS, NS, P])
        half = buf("half", [P, 2])
        pair = buf("pair", [RS, BH])
        sign = buf("sign", [RS, 2])
        alibi = buf("alibi", [RS, PAST + 1])
        qk = buf("qk", [P, NS, NH, 2])
        sT = buf("sT", [PG, NPG, RS])
        sc = buf("sc", [RS, PAST + 1])
        stat = buf("stat", [RS, 4])
        pairc = buf("pairc", [RS, BH])
        self_w = buf("self_w", [RS, P])
        pT = buf("pT", [PG, NPG, NS, BH])
        pick = buf("pick", [BH, NH, BH])
        rows = buf("rows", [BH, NH * P])
        pself = buf("pself", [P, NS, NH])
        oT = buf("oT", [P, NH, NS])
        tz = bank("tz")
        qb = [bank(f"qb{i}") for i in range(2)]
        small = bank("small")
        vb = bank("v")
        ob = bank("o")

        z_in, tab_in, con_in = sem("z_in"), sem("tab_in"), sem("con_in")
        k_in = [sem(f"k_in{i}") for i in range(KR)]
        v_in = [sem(f"v_in{i}") for i in range(NS)]
        pe_s, dv, kdone, ac, brow, o_out = (
            sem("pe"), sem("dv"), sem("keys_used"), sem("ac"), sem("q_spread"), sem("o_out"))
        names_p = ["qT", "self"] + [f"sT{g}" for g in range(NPG)] + ["pT", "pself", "pv", "oT"]
        PV = {n: i + 1 for i, n in enumerate(names_p)}
        names_d = ["sel", "qk", "qrow"] + ["zero"] + [f"red{b}" for b in range(NS)] + [
            "self", "bias", "max", "neg", "rec", "coef", "pairc", "wself", "pT", "pself", "rows", "o1", "out"]
        DV = {n: i + 1 for i, n in enumerate(names_d)}

        block = ctx.enter_context(nc.Block())

        def load(e, cache, to, landed, b):
            for g in range(NPG):
                page = e.value_load(table[0:1, b * NPG + g:b * NPG + g + 1], min_val=0, max_val=POOL - 1)
                e.dma_start(to[:, g, :], io[cache][bass.ds(page, 1)].rearrange("o p f -> (o p) f")
                            ).then_inc(landed, 16)

        @block.sync
        def _(sp):
            sp.dma_start(table[:], io["page_table"]).then_inc(tab_in, 16)
            sp.dma_start(zs[:], io["z"].rearrange("m p t -> p m t")[:, :, SEQ:T]).then_inc(z_in, 16)
            sp.wait_ge(tab_in, 16)

            for b in range(NS):
                if b >= KR:
                    sp.wait_ge(kdone, b + 1 - KR)
                load(sp, "cache_k", keys[b % KR], k_in[b % KR], b)
            sp.wait_ge(dv, DV["out"])
            sp.dma_start(io["mix"][0:NH].rearrange("h p t -> p h t")[:, :, SEQ:T], oT[:]).then_inc(o_out, 16)
            sp.wait_ge(o_out, 16)

        @block.scalar
        def _(act):
            act.dma_start(half[:], io["half"]).then_inc(con_in, 16)
            act.dma_start(pair[:], io["pair"]).then_inc(con_in, 16)
            act.dma_start(sign[:], io["sign"]).then_inc(con_in, 16)
            act.dma_start(alibi[:], io["alibi"]).then_inc(con_in, 16)
            act.dma_start(pick[:], io["pick"]).then_inc(con_in, 16)
            act.wait_ge(tab_in, 16)
            for b in range(NS):
                load(act, "cache_v", vals[:, b], v_in[b], b)
            act.wait_ge(dv, DV["neg"])
            act.activation(sc[:], sc[:], ACT.Exp, scale=SCALE, bias=stat[:, 0:1], accum_out=stat[:, 1:2]
                           ).then_inc(ac, 1)

        @block.tensor
        def _(pe):
            cnt = softcount(pe_s)

            def mark(ins, name):
                assert cnt(ins) == PV[name], name

            pe.wait_ge(z_in, 16)
            for h in range(NH):
                mm = pe.transpose(tz[0:NS, h * P:(h + 1) * P], zs[:, h, :], mods["ident"][:])
            mark(mm, "qT")
            pe.wait_ge(dv, DV["qk"])
            mark(pe.matmul(small[0:RS, 0:1], qk[:].rearrange("p b h c -> p (b h c)"), mods["ones"][:, 0:1],
                           start=True, stop=True), "self")
            pe.wait_ge(dv, DV["qrow"])
            for b in range(NS):
                if b >= 2:
                    pe.wait_ge(kdone, b - 1)
                pe.matmul(qb[b % 2][:, :], rowsel[:, b, :], qrow[:], start=True, stop=True).then_inc(brow, 1)
            pe.wait_ge(dv, DV[f"red{NS - 1}"])
            for g in range(NPG):
                mark(pe.transpose(tz[0:RS, g * PG:(g + 1) * PG], sT[:, g, :], mods["ident"][:]), f"sT{g}")
            pe.wait_ge(dv, DV["wself"])
            for g in range(NPG):
                mm = pe.matmul(small[:, 64 + g * BH:64 + (g + 1) * BH], sc[:, g * PG:(g + 1) * PG], pairc[:],
                               start=True, stop=True)
            mark(mm, "pT")
            mark(pe.matmul(small[:, 256:256 + BH], self_w[:], pairc[:], start=True, stop=True), "pself")
            pe.wait_ge(dv, DV["pT"])
            for b in range(NS):
                pe.wait_ge(v_in[b], 16 * NPG)
                for g in range(NPG):
                    mm = pe.matmul(vb[0:BH, :], pT[:, g, b, :], vals[:, b, g, :], start=b == 0 and g == 0,
                                   stop=b == NS - 1 and g == NPG - 1)
            mark(mm, "pv")
            pe.wait_ge(dv, DV["rows"])
            for h in range(NH):
                mm = pe.matmul(ob[:, 0:BH], rows[:, h * P:(h + 1) * P], pick[:, h, :], start=h == 0, stop=h == NH - 1)
            mark(mm, "oT")

        @block.vector
        def _(dve):
            cnt = softcount(dv)

            def mark(ins, name):
                assert cnt(ins) == DV[name], name
                dve.wait_ge(dv, DV[name])
            def gain(n):
                return mods["gains"][:, n, :].unsqueeze(2).broadcast_to((P, KT, C9))
            dve.tensor_tensor(mods["gate_m"][:], mods["mod"][:, 0:KT, :], gain(1), ALU.mult)
            dve.tensor_copy(mods["shift_f"][:], mods["mod"][:, KT:2 * KT, :])
            dve.scalar_tensor_tensor(out=mods["mul_f"][:], in0=mods["mod"][:, 2 * KT:3 * KT, :], scalar=1.0, in1=gain(2),
                                     op0=ALU.add, op1=ALU.mult)
            dve.tensor_tensor(mods["gate_f"][:], mods["mod"][:, 3 * KT:4 * KT, :], gain(3), ALU.mult)
            mark(dve.tensor_copy(rowsel[:], mods["ident"][0:NS, 0:NS].unsqueeze(2).broadcast_to((NS, NS, P))), "sel")
            dve.wait_ge(z_in, 16)
            dve.wait_ge(con_in, 80)
            for c in range(2):
                ins = dve.scalar_tensor_tensor(out=qk[:, :, :, c], in0=zs[:, 0:NH, :].rearrange("p h b -> p b h"),
                                               scalar=half[:, c:c + 1],
                                               in1=zs[:, NH:2 * NH, :].rearrange("p h b -> p b h"),
                                               op0=ALU.mult, op1=ALU.mult)
            mark(ins, "qk")
            dve.wait_ge(pe_s, PV["qT"])
            mark(dve.tensor_copy(qrow[:], tz[0:NS, :]), "qrow")
            dve.memset(pT[:], 0.0)
            mark(dve.memset(self_w[:], 0.0), "zero")
            for b in range(NS):
                dve.wait_ge(brow, b + 1)
                dve.wait_ge(k_in[b % KR], 16 * NPG * (b // KR + 1))
                dve.tensor_tensor(prod[:], keys[b % KR][:], qb[b % 2][:, :].unsqueeze(1).broadcast_to((PG, NPG, 512)),
                                  ALU.mult).then_inc(kdone, 1)
                dve.wait_ge(kdone, b + 1)
                mark(dve.tensor_reduce(sT[:, :, b * HC:(b + 1) * HC],
                                       prod[:].rearrange("p g (r d) -> p g r d", d=DH), AX.X, ALU.add), f"red{b}")
            dve.wait_ge(pe_s, PV["self"])
            mark(dve.tensor_copy(sc[:, PAST:PAST + 1], small[0:RS, 0:1]), "self")
            dve.wait_ge(pe_s, PV[f"sT{NPG - 1}"])
            mark(dve.tensor_tensor(sc[:, 0:PAST], tz[0:RS, :], alibi[:, 0:PAST], ALU.add), "bias")
            mark(dve.tensor_reduce(stat[:, 0:1], sc[:], AX.X, ALU.max), "max")
            mark(dve.tensor_scalar(stat[:, 0:1], stat[:, 0:1], -SCALE, None, ALU.mult), "neg")
            dve.wait_ge(ac, 1)
            mark(dve.reciprocal(stat[:, 2:3], stat[:, 1:2]), "rec")
            mark(dve.scalar_tensor_tensor(out=stat[:, 3:4], in0=sign[:, 1:2], scalar=mods["neglam"][0:RS, 0:1],
                                          in1=sign[:, 0:1], op0=ALU.mult, op1=ALU.add), "coef")
            mark(dve.tensor_scalar(pairc[:], pair[:], stat[:, 2:3], stat[:, 3:4], ALU.mult, ALU.mult), "pairc")
            mark(dve.tensor_scalar(self_w[:], self_w[:], sc[:, PAST:PAST + 1], None, ALU.add), "wself")
            dve.wait_ge(pe_s, PV["pself"])
            for b in range(NS):
                ins = dve.tensor_copy(pT[:, :, b, b * NH:(b + 1) * NH],
                                      small[:, 64:64 + NPG * BH].rearrange("p (g n) -> p g n", g=NPG)
                                      [:, :, b * NH:(b + 1) * NH])
            mark(ins, "pT")
            mark(dve.tensor_tensor(pself[:], small[:, 256:256 + BH].rearrange("p (b h) -> p b h", b=NS),
                                   zs[:, 2 * NH:3 * NH, :].rearrange("p h b -> p b h"), ALU.mult), "pself")
            dve.wait_ge(pe_s, PV["pv"])
            mark(dve.tensor_copy(rows[:], vb[0:BH, :]), "rows")
            dve.wait_ge(pe_s, PV["oT"])
            mark(dve.tensor_tensor(pself[:], pself[:], ob[:, 0:BH].rearrange("p (b h) -> p b h", b=NS), ALU.add), "o1")
            mark(dve.tensor_copy(oT[:], pself[:].rearrange("p b h -> p h b")), "out")


OW = [264, 424, 424, 424, 264, 256]
OG = len(OW)
OT = [sum(OW[:g]) for g in range(OG)]
OMAX = max(OW)


def output_projection(nc, mods, io):
    with ExitStack() as ctx:
        def sem(name):
            return ctx.enter_context(nc.semaphore("p3_" + name))

        def buf(name, shape, dt=F32):
            return ctx.enter_context(nc.sbuf_tensor("p3_" + name, shape, dt))

        def bank(name):
            return ctx.enter_context(nc.psum_tensor("p3_" + name, [P, 512], F32))
        mix = buf("mix", [P, KT, OMAX])
        m_hi = [buf(f"m_hi{i}", [P, KT, OMAX], F32R) for i in range(2)]
        m_lo = [buf(f"m_lo{i}", [P, KT, OMAX], F32R) for i in range(2)]
        out = [buf(f"out{i}", [P, KT, OMAX]) for i in range(3)]
        x = buf("x", [P, KT, OMAX])
        sq = buf("sq", [P, KT, OMAX])
        ssumA = buf("ssumA", [P, OMAX])
        ssumB = buf("ssumB", [P, OMAX])
        rstd = buf("rstd", [P, OMAX])
        rhead = buf("rhead", [P, OMAX])
        sel = buf("sel", [P, NH, P])
        wraw = buf("wraw", [P, RW, D])
        w_hi = [buf(f"w_hi{i}", [P, D], F32R) for i in range(RW)]
        w_lo = [buf(f"w_lo{i}", [P, D], F32R) for i in range(RW)]
        proj = [bank(f"proj{i}") for i in range(2)]
        hsum = bank("hsum")
        nps = bank("norm")
        bps = [bank(f"spread{i}") for i in range(NH)]

        consts, selzero, mix_in, x_in, x1_out, h2_out = (
            sem("consts"), sem("selzero"), sem("mix_in"), sem("x_in"), sem("x1_out"), sem("h2_out"))
        w_in = [sem(f"w_in{i}") for i in range(RW)]
        hi_done, lo_done, split_free, bank_free = sem("hi_done"), sem("lo_done"), sem("split_free"), sem("bank_free")
        ac, dv, pn, link_sem = sem("ac"), sem("dv"), sem("pn"), sem("link")

        def has(g):
            return 0 <= g < OG
        STEPS = range(-1, OG + 2)
        order_a, order_d, order_p = [], [], []
        for g in STEPS:
            for name, k in (("sqA", 1), ("sqrtB", 2), ("sqH", -1), ("sqrtA", 1), ("sqrtH", -1), ("h", 2), ("hi", -1),
                            ("sqB", 1)):
                if has(g - k):
                    order_a.append((name, g - k))
            for name, k in (("redA", 1), ("rcpB", 2), ("xn", 2), ("rcpH", -1), ("rcpA", 1), ("t", 1), ("x1", 1),
                            ("mulH", -1), ("lo", -1), ("redB", 1)):
                if has(g - k):
                    order_d.append((name, g - k))
            for name, k in (("normB", 2), ("normA", 1), ("hsum", -1), ("sel", -1)):
                if has(g - k):
                    order_p.append((name, g - k))
        A = {n: i + 1 for i, n in enumerate(order_a)}
        V = {n: i + 1 for i, n in enumerate(order_d)}
        N = {n: i + 1 for i, n in enumerate(order_p)}

        block = ctx.enter_context(nc.Block())

        @block.sync
        def _(sp):
            sp.wait_ge(selzero, 1)
            for j in range(NH):
                sp.dma_start(sel[32 * j:32 * j + 1, j, :], io["g_subln"]).then_inc(consts, 16)

            def load_mix(g):
                if g:
                    sp.wait_ge(dv, V["lo", g - 1])
                sp.dma_start(mix[:, :, 0:OW[g]], io["mix"].rearrange("k p t -> p k t")[:, :, OT[g]:OT[g] + OW[g]]
                             ).then_inc(mix_in, 16)

            def load_x(g):
                if g:
                    sp.wait_ge(dv, V["x1", g - 1])
                sp.dma_start(x[:, :, 0:OW[g]], io["xT"][:, :, OT[g]:OT[g] + OW[g]]).then_inc(x_in, 16)

            def load_w(g, half):
                for s in range(RW):
                    n = g * KT + half * RW + s
                    if n >= RW:
                        sp.wait_ge(lo_done, n + 1 - RW)
                    sp.dma_start(wraw[:, s, :], io["w_out"][half * RW + s]).then_inc(w_in[s], 16)

            def store(name, g):
                if name == "x1":
                    sp.wait_ge(dv, V["x1", g])
                    sp.dma_start(io["x1"][:, :, OT[g]:OT[g] + OW[g]], out[g % 3][:, :, 0:OW[g]]).then_inc(x1_out, 16)
                else:
                    sp.wait_ge(ac, A["h", g])
                    sp.dma_start(io["h2"][:, :, OT[g]:OT[g] + OW[g]], out[g % 3][:, :, 0:OW[g]]).then_inc(h2_out, 16)
            for g in STEPS:
                if g == -1:
                    load_mix(0)
                    load_w(0, 0)
                    load_x(0)
                    continue
                if has(g):
                    load_w(g, 1)
                if has(g + 1):
                    load_mix(g + 1)
                if has(g - 2):
                    store("h2", g - 2)
                if has(g + 1):
                    load_w(g + 1, 0)
                if has(g - 1):
                    store("x1", g - 1)
                    if has(g):
                        load_x(g)
            sp.dma_start(mods["wraw0"][:], io["w_ffn"][0]).then_inc(mods["w_in0"], 16)
            sp.wait_ge(x1_out, 16 * OG)
            sp.wait_ge(h2_out, 16 * OG)

        @block.gpsimd
        def _(pool):
            pool.memset(sel[:], 0.0).then_inc(selzero, 1)
            with pool.Fori(0, OG * KT - RW + 1, RW) as n:
                for s in range(RW):
                    pool.wait_ge(hi_done, n + (s + 1))
                    pool.tensor_tensor(w_lo[s][:], wraw[:, s, :], w_hi[s][:].bitcast(F32), ALU.subtract
                                       ).then_inc(lo_done, 1)

        @block.tensor
        def _(pe):
            cnt = softcount(pn)

            def mark(ins, name, g):
                assert cnt(ins) == N[name, g]

            def tiles(g, ms):
                W = OW[g]
                for m in ms:
                    n = g * KT + m
                    pe.wait_ge(lo_done, n + 1)
                    if n >= 2:
                        pe.wait_ge(bank_free, n - 1)
                    i = 0
                    for k in range(KT):
                        for a, b in ((w_hi, m_hi), (w_hi, m_lo), (w_lo, m_hi)):
                            mm = pe.matmul(proj[n % 2][:, 0:W], a[n % RW][:, k * P:(k + 1) * P], b[g % 2][:, k, 0:W],
                                           start=i == 0, stop=i == 3 * KT - 1)
                            i += 1
                    mm.then_inc(split_free, 1)

            def norm(name, g, src):
                pe.wait_ge(dv, V[src, g])
                if name == "normB":
                    pe.wait_ge(ac, A["sqrtA", g])
                elif has(g - 1):
                    pe.wait_ge(ac, A["sqrtB", g - 1])
                ssum = ssumB if name == "normB" else ssumA
                mark(pe.matmul(nps[:, 0:OW[g]], mods["ones"][:], ssum[:, 0:OW[g]], start=True, stop=True), name, g)

            for g in STEPS:
                if has(g):
                    pe.wait_ge(dv, V["lo", g])
                    tiles(g, [0])
                if has(g - 2):
                    norm("normB", g - 2, "redB")
                if has(g):
                    tiles(g, [1, 2])
                if has(g - 1):
                    norm("normA", g - 1, "redA")
                if has(g + 1):
                    W = OW[g + 1]
                    pe.wait_ge(ac, A["sqH", g + 1])
                    if has(g):
                        pe.wait_ge(ac, A["sqrtH", g])
                    for j in range(NH):
                        mm = pe.matmul(hsum[32 * j:32 * j + 32, 0:W], mods["ones"][:, 0:32], sq[:, j, 0:W],
                                       start=True, stop=True)
                    mark(mm, "hsum", g + 1)
                if has(g):
                    tiles(g, [3, 4, 5])
                if has(g + 1):
                    pe.wait_ge(dv, V["rcpH", g + 1])
                    if has(g):
                        pe.wait_ge(dv, V["mulH", g])
                    for j in range(NH):
                        mm = pe.matmul(bps[j][:, 0:W], sel[:, j, :], rhead[:, 0:W], start=True, stop=True)
                    mark(mm, "sel", g + 1)
                if has(g):
                    tiles(g, [6, 7])

        @block.scalar
        def _(act):
            cnt = softcount(ac)

            def mark(ins, name, g):
                assert cnt(ins) == A[name, g], (name, g)

            def split(n):
                if n < OG * KT:
                    s = n % RW
                    act.wait_ge(w_in[s], 16 * (n // RW + 1))
                    if n >= RW:
                        act.wait_ge(split_free, n + 1 - RW)
                    act.activation(w_hi[s][:], wraw[:, s, :], ACT.Copy).then_inc(hi_done, 1)

            def tile(g, m):
                n = g * KT + m
                split(n + RW - 1)
                act.wait_ge(split_free, n + 1)
                act.activation(out[g % 3][:, m, 0:OW[g]], proj[n % 2][:, 0:OW[g]], ACT.Copy).then_inc(bank_free, 1)

            def root(name, to, src, width, g, by, norm):
                act.wait_ge(pn, N[norm, g])
                mark(act.activation(to[:, 0:width], src[:, 0:width], ACT.Sqrt, scale=1.0 / by,
                                    bias=mods["eps"][:, 0:1]), name, g)
            for g in STEPS:
                if g == -1:
                    for n in range(RW - 1):
                        split(n)
                if has(g):
                    if has(g - 3):
                        act.wait_ge(h2_out, 16 * (g - 2))
                    tile(g, 0)
                if has(g - 1):
                    act.wait_ge(bank_free, (g - 1) * KT + KT)
                    if has(g - 2):
                        act.wait_ge(dv, V["redB", g - 2])
                    if has(g):
                        act.wait_ge(pn, N["hsum", g])
                    mark(act.activation(sq[:, :, 0:OW[g - 1]], out[(g - 1) % 3][:, :, 0:OW[g - 1]], ACT.Square), "sqA", g - 1)
                if has(g):
                    tile(g, 1)
                if has(g - 2):
                    act.wait_ge(dv, V["redB", g - 2])
                    root("sqrtB", rstd, nps, OW[g - 2], g - 2, D, "normB")
                if has(g + 1):
                    W = OW[g + 1]
                    act.wait_ge(mix_in, 16 * (g + 2))
                    if has(g - 1):
                        act.wait_ge(dv, V["redA", g - 1])
                    mark(act.activation(sq[:, 0:NH, 0:W], mix[:, 0:NH, 0:W], ACT.Square), "sqH", g + 1)
                if has(g):
                    tile(g, 2)
                    tile(g, 3)
                if has(g - 1):
                    if has(g - 2):
                        act.wait_ge(dv, V["xn", g - 2])
                    root("sqrtA", rstd, nps, OW[g - 1], g - 1, D, "normA")
                if has(g + 1):
                    if has(g):
                        act.wait_ge(pn, N["sel", g])
                    root("sqrtH", rhead, hsum, OW[g + 1], g + 1, P, "hsum")
                if has(g):
                    tile(g, 4)
                if has(g - 2):
                    q = g - 2
                    act.wait_ge(dv, V["xn", q])
                    for k in range(KT):
                        WP = OW[q] - (NS if q == OG - 1 else 0)
                        ins = act.activation(out[q % 3][:, k, 0:WP], out[q % 3][:, k, 0:WP], ACT.Identity,
                                             scale=mods["mul_f"][:, k, 0:1], bias=mods["shift_f"][:, k, 0:1])
                    mark(ins, "h", q)
                if has(g):
                    tile(g, 5)
                    tile(g, 6)
                if has(g + 1):
                    act.wait_ge(dv, V["mulH", g + 1])
                    if has(g - 1):
                        act.wait_ge(split_free, g * KT)
                    mark(act.activation(m_hi[(g + 1) % 2][:, :, 0:W], mix[:, :, 0:W], ACT.Copy), "hi", g + 1)
                if has(g):
                    tile(g, 7)
                if has(g - 1):
                    act.wait_ge(dv, V["x1", g - 1])
                    if has(g + 1):
                        act.wait_ge(pn, N["hsum", g + 1])
                    mark(act.activation(sq[:, :, 0:OW[g - 1]], out[(g - 1) % 3][:, :, 0:OW[g - 1]], ACT.Square), "sqB", g - 1)

        @block.vector
        def _(dve):
            cnt = softcount(dv)
            nl = [0]

            def link(ins):
                nl[0] += 1
                ins.then_inc(link_sem, 1)
                dve.wait_ge(link_sem, nl[0])

            def mark(ins, name, g):
                assert cnt(ins) == V[name, g], (name, g)
                dve.wait_ge(dv, V[name, g])

            def spread(r, W):
                return r[:, 0:W].unsqueeze(1).broadcast_to((P, KT, W))

            def reduce(name, g, sqname):
                dve.wait_ge(ac, A[sqname, g])
                if has(g - 1):
                    dve.wait_ge(pn, N["norm" + name[-1], g - 1])
                mark(dve.tensor_reduce((ssumB if name == "redB" else ssumA)[:, 0:OW[g]],
                                       sq[:, :, 0:OW[g]].rearrange("p k t -> p t k"), AX.X, ALU.add), name, g)
            dve.wait_ge(consts, 16 * NH)
            link(dve.tensor_scalar(sel[:], sel[:], 1.0 - LAM_INIT, None, ALU.mult))
            for g in STEPS:
                if has(g - 1):
                    reduce("redA", g - 1, "sqA")
                if has(g - 2):
                    q, W = g - 2, OW[g - 2]
                    dve.wait_ge(ac, A["sqrtB", q])
                    mark(dve.reciprocal(rstd[:, 0:W], rstd[:, 0:W]), "rcpB", q)
                    dve.wait_ge(x1_out, 16 * (q + 1))
                    x1 = out[q % 3]
                    if q < OG - 1:
                        mark(dve.tensor_tensor(x1[:, :, 0:W], x1[:, :, 0:W], spread(rstd, W), ALU.mult), "xn", q)
                    else:
                        link(dve.tensor_tensor(x1[:, :, 0:W], x1[:, :, 0:W], spread(rstd, W), ALU.mult))
                        xs = x1[:, :, W - NS:W]
                        link(dve.tensor_tensor(xs, xs, mods["mul_f"][:, :, 1:C9], ALU.mult))
                        mark(dve.tensor_tensor(xs, xs, mods["shift_f"][:, :, 1:C9], ALU.add), "xn", q)
                if has(g + 1):
                    dve.wait_ge(ac, A["sqrtH", g + 1])
                    mark(dve.reciprocal(rhead[:, 0:OW[g + 1]], rhead[:, 0:OW[g + 1]]), "rcpH", g + 1)
                if has(g - 1):
                    q, W = g - 1, OW[g - 1]
                    O = out[q % 3]
                    dve.wait_ge(ac, A["sqrtA", q])
                    mark(dve.reciprocal(rstd[:, 0:W], rstd[:, 0:W]), "rcpA", q)
                    mark(dve.tensor_tensor(O[:, :, 0:W], O[:, :, 0:W], spread(rstd, W), ALU.mult), "t", q)
                    dve.wait_ge(x_in, 16 * (q + 1))
                    WP = W - (NS if q == OG - 1 else 0)
                    if WP < W:
                        os = O[:, :, WP:W]
                        link(dve.tensor_tensor(os, os, mods["gate_m"][:, :, 1:C9], ALU.mult))
                        dve.tensor_tensor(os, os, x[:, :, WP:W], ALU.add)
                    for k in range(KT):
                        ins = dve.scalar_tensor_tensor(out=O[:, k, 0:WP], in0=O[:, k, 0:WP],
                                                       scalar=mods["gate_m"][:, k, 0:1], in1=x[:, k, 0:WP],
                                                       op0=ALU.mult, op1=ALU.add)
                    mark(ins, "x1", q)
                if has(g + 1):
                    W = OW[g + 1]
                    dve.wait_ge(pn, N["sel", g + 1])
                    for j in range(NH):
                        ins = dve.tensor_tensor(mix[:, j, 0:W], mix[:, j, 0:W], bps[j][:, 0:W], ALU.mult)
                    mark(ins, "mulH", g + 1)
                    dve.wait_ge(ac, A["hi", g + 1])
                    i = (g + 1) % 2
                    mark(dve.tensor_tensor(m_lo[i][:, :, 0:W], mix[:, :, 0:W], m_hi[i][:, :, 0:W].bitcast(F32),
                                           ALU.subtract), "lo", g + 1)
                if has(g - 1):
                    reduce("redB", g - 1, "sqB")


FG = [0, 1028]
FC = [(0, 344), (344, 342), (686, 342)]
FW = 1028
FCM = 344
NC = len(FC)
YB = 3


def ffn(nc, mods, io):
    with ExitStack() as ctx:
        def sem(name):
            return ctx.enter_context(nc.semaphore("p4_" + name))

        def buf(name, shape, dt=F32):
            return ctx.enter_context(nc.sbuf_tensor("p4_" + name, shape, dt))

        def bank(name):
            return ctx.enter_context(nc.psum_tensor("p4_" + name, [P, 512], F32))
        h_hi = buf("h_hi", [P, KT, FW], F32R)
        h_lo = buf("h_lo", [P, KT, FW], F32R)
        stage = buf("stage", [P, KT, FCM])
        y = buf("y", [P, KT, FW])
        wraw = [mods["wraw0"], buf("wraw1", [P, 3 * KT, P])]
        w_hi = [buf(f"w_hi{i}", [P, 3 * KT, P], F32R) for i in range(2)]
        w_lo = [buf(f"w_lo{i}", [P, 3 * KT, P], F32R) for i in range(2)]
        sil = [buf(f"sil{i}", [P, FCM]) for i in range(2)]
        f_hi = buf("f_hi", [P, FW], F32R)
        f_lo = buf("f_lo", [P, FW], F32R)
        ssum = buf("ssum", [P, FCM])
        rstd = buf("rstd", [P, FCM])
        xin = buf("xin", [P, KT, FCM])
        gb = [bank(f"g{i}") for i in range(2)]
        ub = [bank(f"u{i}") for i in range(2)]
        yb = [bank(f"y{i}") for i in range(YB)]
        nb = bank("norm")

        st_in = sem("st_in")
        w_in = [mods["w_in0"], sem("w_in1")]
        x_in = sem("x_in")
        w_hid, w_lod = sem("w_hid"), sem("w_lod")
        hhi, hlo = sem("hhi"), sem("hlo")
        gu, yd = sem("gu"), sem("yd")
        sild, fd, fhid, flod, yadd = sem("sild"), sem("fd"), sem("fhid"), sem("flod"), sem("yadd")
        sqd, tree, fs, rt, rc, fn, fy, y_out = (
            sem("sqd"), sem("tree"), sem("fs"), sem("rt"), sem("rc"), sem("fn"), sem("fy"), sem("y_out"))
        UT = NC * KT

        block = ctx.enter_context(nc.Block())

        @block.sync
        def _(sp):
            def load(n0, i, u):
                s = n0 % 2
                if not (isinstance(i, int) and n0 < 2):
                    sp.wait_ge(w_lod, i * 3 + 3 * (n0 - 1))
                sp.dma_start(wraw[s][:], io["w_ffn"][u]).then_inc(w_in[s], 16)

            def load_h(G, c):
                c0, W = FC[c]
                if NC * G + c:
                    sp.wait_ge(hlo, NC * G + c)
                sp.dma_start(stage[:, :, 0:W], io["h2"][:, :, FG[G] + c0:FG[G] + c0 + W]).then_inc(st_in, 16)

            def finish(G, c):
                c0, W = FC[c]
                n = NC * G + c
                if n:
                    sp.wait_ge(y_out, 16 * n)
                sp.dma_start(xin[:, :, 0:W], io["x1"][:, :, FG[G] + c0:FG[G] + c0 + W]).then_inc(x_in, 16)
                sp.wait_ge(fy, KT * (n + 1))
                sp.dma_start(io["yT"][:, :, FG[G] + c0:FG[G] + c0 + W], xin[:, :, 0:W]).then_inc(y_out, 16)

            load_h(0, 0)
            load_h(0, 1)
            load(1, 0, 1)
            load_h(0, 2)
            load_h(1, 0)
            with sp.Fori(0, FT - 3, 2) as i:
                load(2, i, i + 2)
                load(3, i, i + 3)
            load(FT, 0, 0)
            load(FT + 1, 0, 1)
            load_h(1, 1)
            load_h(1, 2)
            finish(0, 0)
            load(FT + 2, 0, 2)
            finish(0, 1)
            finish(0, 2)
            load(FT + 3, 0, 3)
            with sp.Fori(0, FT - 5, 2) as i:
                load(FT + 4, i, i + 4)
                load(FT + 5, i, i + 5)
            for c in range(NC):
                finish(1, c)
            sp.wait_ge(y_out, 16 * 2 * NC)

        @block.gpsimd
        def _(pool):
            def low(n0, i, third):
                s = n0 % 2
                part = slice(KT * third, KT * (third + 1))
                pool.wait_ge(w_hid, i * 3 + (3 * n0 + third + 1))
                pool.tensor_tensor(w_lo[s][:, part, :], wraw[s][:, part, :], w_hi[s][:, part, :].bitcast(F32),
                                   ALU.subtract).then_inc(w_lod, 1)

            def add_squares(G, c):
                n, W = NC * G + c, FC[c][1]
                pool.wait_ge(sqd, n + 1)
                for k in (4, 2):
                    pool.tensor_tensor(stage[:, 0:k, 0:W], stage[:, 0:k, 0:W], stage[:, k:2 * k, 0:W], ALU.add
                                       ).then_inc(tree, 1)
                    pool.wait_ge(tree, 3 * n + (1 if k == 4 else 2))
                if n:
                    pool.wait_ge(fs, n)
                pool.tensor_tensor(ssum[:, 0:W], stage[:, 0, 0:W], stage[:, 1, 0:W], ALU.add).then_inc(tree, 1)

            def units(start, end):
                with pool.Fori(0, end - start - 1, 2) as i:
                    for n0 in (start, start + 1):
                        for third in range(3):
                            low(n0, i, third)
            units(0, FT)
            for third in range(3):
                low(FT, 0, third)
            add_squares(0, 0)
            low(FT + 1, 0, 0)
            add_squares(0, 1)
            low(FT + 1, 0, 1)
            low(FT + 1, 0, 2)
            add_squares(0, 2)
            units(FT + 2, 2 * FT)
            for c in range(NC):
                add_squares(1, c)

        @block.tensor
        def _(pe):
            def gate_up(n0, i, c):
                s, par = n0 % 2, (3 * n0 + c) % 2
                c0, W = FC[c]
                if not (isinstance(i, int) and 3 * n0 + c < 2):
                    pe.wait_ge(fd, i * 3 + (3 * n0 + c - 1))
                if isinstance(i, int) and n0 % FT == 0:
                    pe.wait_ge(hlo, NC * (n0 // FT) + c + 1)
                for half, bk in ((0, gb), (1, ub)):
                    if c == 0:
                        pe.wait_ge(w_lod, i * 3 + (3 * n0 + 1 + half))
                    r = 0
                    for k in range(KT):
                        for a, b in ((w_hi, h_hi), (w_hi, h_lo), (w_lo, h_hi)):
                            mm = pe.matmul(bk[par][:, 0:W], a[s][:, KT * half + k, :], b[:, k, c0:c0 + W],
                                           start=r == 0, stop=r == 3 * KT - 1)
                            r += 1
                mm.then_inc(gu, 1)

            def down(n0, i, c):
                s = n0 % 2
                c0, W = FC[c]
                if c == 0:
                    pe.wait_ge(w_lod, i * 3 + (3 * n0 + 3))
                pe.wait_ge(flod, i * 3 + (3 * n0 + c + 1))
                for m in range(KT):
                    q = KT * c + m
                    if not (isinstance(i, int) and n0 == 0 and q < YB):
                        pe.wait_ge(yadd, i * UT + (UT * n0 + q + 1 - YB))
                    for r, (a, b) in enumerate(((w_hi, f_hi), (w_hi, f_lo), (w_lo, f_hi))):
                        mm = pe.matmul(yb[q % YB][:, 0:W], a[s][:, 2 * KT + m, :], b[:, c0:c0 + W],
                                       start=r == 0, stop=r == 2)
                    mm.then_inc(yd, 1)

            def square_sum(G, c):
                c0, W = FC[c]
                if NC * G + c:
                    pe.wait_ge(rt, NC * G + c)
                pe.wait_ge(tree, 3 * (NC * G + c + 1))
                pe.matmul(nb[:, 0:W], mods["ones"][:], ssum[:, 0:W], start=True, stop=True).then_inc(fs, 1)

            def unit(n0, i):
                gate_up(n0, i, 0)
                if not (isinstance(i, int) and n0 == 0):
                    down(n0 - 1, i, 2)
                gate_up(n0, i, 1)
                down(n0, i, 0)
                gate_up(n0, i, 2)
                down(n0, i, 1)
            unit(0, 0)
            unit(1, 0)
            with pe.Fori(0, FT - 3, 2) as i:
                unit(2, i)
                unit(3, i)
            gate_up(FT, 0, 0)
            down(FT - 1, 0, 2)
            square_sum(0, 0)
            gate_up(FT, 0, 1)
            gate_up(FT, 0, 2)
            square_sum(0, 1)
            down(FT, 0, 0)
            gate_up(FT + 1, 0, 0)
            square_sum(0, 2)
            down(FT, 0, 1)
            gate_up(FT + 1, 0, 1)
            down(FT, 0, 2)
            down(FT + 1, 0, 0)
            gate_up(FT + 1, 0, 2)
            down(FT + 1, 0, 1)
            with pe.Fori(0, FT - 3, 2) as i:
                unit(FT + 2, i)
                unit(FT + 3, i)
            down(2 * FT - 1, 0, 2)
            for c in range(NC):
                square_sum(1, c)

        @block.scalar
        def _(act):
            def split(n0, i, third):
                s = n0 % 2
                if third == 0:
                    act.wait_ge(w_in[s], i * 8 + (16 * (n0 // 2) + 16))
                part = slice(KT * third, KT * (third + 1))
                act.activation(w_hi[s][:, part, :], wraw[s][:, part, :], ACT.Copy).then_inc(w_hid, 1)

            def chunk(n0, i, c, last=False):
                s = n0 % 2
                W = FC[c][1]
                c0 = FC[c][0]
                b = (3 * n0 + c) % 2
                if not (isinstance(i, int) and 3 * n0 + c < 2):
                    act.wait_ge(flod, i * 3 + (3 * n0 + c - 1))
                act.wait_ge(gu, i * 3 + (3 * n0 + c + 1))
                act.activation(sil[b][:, 0:W], gb[b][:, 0:W], ACT.Silu).then_inc(sild, 1)
                if not last:
                    split(n0 + 1, i, c)
                act.wait_ge(fd, i * 3 + (3 * n0 + c + 1))
                act.activation(f_hi[:, c0:c0 + W], sil[b][:, 0:W], ACT.Copy).then_inc(fhid, 1)

            def unit(n0, i, last=False):
                for c in range(NC):
                    chunk(n0, i, c, last)

            def split_h(G, c):
                c0, W = FC[c]
                act.wait_ge(st_in, 16 * (NC * G + c + 1))
                act.activation(h_hi[:, :, c0:c0 + W], stage[:, :, 0:W], ACT.Copy).then_inc(hhi, 1)

            def squares(G, c):
                c0, W = FC[c]
                n = NC * G + c
                act.wait_ge(yadd, UT * (FT * (G + 1) - 1) + KT * (c + 1))
                act.wait_ge(hlo, 2 * NC)
                if n:
                    act.wait_ge(tree, 3 * n)
                act.activation(stage[:, :, 0:W], y[:, :, c0:c0 + W], ACT.Square).then_inc(sqd, 1)

            def root(G, c):
                act.wait_ge(fs, NC * G + c + 1)
                if NC * G + c:
                    act.wait_ge(fn, KT * (NC * G + c))
                W = FC[c][1]
                act.activation(rstd[:, 0:W], nb[:, 0:W], ACT.Sqrt, scale=1.0 / D, bias=mods["eps"][:, 0:1]
                               ).then_inc(rt, 1)
            split(0, 0, 0)
            split_h(0, 0)
            split(0, 0, 1)
            split(0, 0, 2)
            split_h(0, 1)
            split_h(0, 2)
            unit(0, 0)
            with act.Fori(0, FT - 3, 2) as i:
                unit(1, i)
                unit(2, i)
            for c in range(NC):
                chunk(FT - 1, 0, c)
                split_h(1, c)
            squares(0, 0)
            chunk(FT, 0, 0)
            root(0, 0)
            squares(0, 1)
            chunk(FT, 0, 1)
            chunk(FT, 0, 2)
            root(0, 1)
            squares(0, 2)
            chunk(FT + 1, 0, 0)
            root(0, 2)
            chunk(FT + 1, 0, 1)
            chunk(FT + 1, 0, 2)
            with act.Fori(0, FT - 5, 2) as i:
                unit(FT + 2, i)
                unit(FT + 3, i)
            unit(2 * FT - 2, 0)
            unit(2 * FT - 1, 0, last=True)
            squares(1, 0)
            for c in range(NC):
                root(1, c)
                if c + 1 < NC:
                    squares(1, c + 1)

        @block.vector
        def _(dve):
            def product(n0, i, c):
                c0, W = FC[c]
                b = (3 * n0 + c) % 2
                dve.wait_ge(sild, i * 3 + (3 * n0 + c + 1))
                dve.tensor_tensor(sil[b][:, 0:W], sil[b][:, 0:W], ub[b][:, 0:W], ALU.mult).then_inc(fd, 1)
                dve.wait_ge(fhid, i * 3 + (3 * n0 + c + 1))
                dve.tensor_tensor(f_lo[:, c0:c0 + W], sil[b][:, 0:W], f_hi[:, c0:c0 + W].bitcast(F32), ALU.subtract
                                  ).then_inc(flod, 1)

            def collect(n0, i, c, first=False):
                c0, W = FC[c]
                for m in range(KT):
                    q = KT * c + m
                    dve.wait_ge(yd, i * UT + (UT * n0 + q + 1))
                    if first:
                        dve.tensor_copy(y[:, m, c0:c0 + W], yb[q % YB][:, 0:W]).then_inc(yadd, 1)
                    else:
                        dve.tensor_tensor(y[:, m, c0:c0 + W], y[:, m, c0:c0 + W], yb[q % YB][:, 0:W], ALU.add
                                          ).then_inc(yadd, 1)

            def low_h(G, c):
                c0, W = FC[c]
                dve.wait_ge(hhi, NC * G + c + 1)
                dve.tensor_tensor(h_lo[:, :, c0:c0 + W], stage[:, :, 0:W], h_hi[:, :, c0:c0 + W].bitcast(F32),
                                  ALU.subtract).then_inc(hlo, 1)

            def finish(G, c):
                c0, W = FC[c]
                n = NC * G + c
                dve.wait_ge(rt, n + 1)
                dve.reciprocal(rstd[:, 0:W], rstd[:, 0:W]).then_inc(rc, 1)
                dve.wait_ge(rc, n + 1)
                for k in range(KT):
                    dve.tensor_tensor(y[:, k, c0:c0 + W], y[:, k, c0:c0 + W], rstd[:, 0:W], ALU.mult).then_inc(fn, 1)
                samples = NS if n == 2 * NC - 1 else 0
                WP = W - samples
                dve.wait_ge(x_in, 16 * (n + 1))
                for k in range(KT):
                    dve.wait_ge(fn, KT * n + k + 1)
                    if samples:
                        ys, xs = y[:, k, c0 + WP:c0 + W], xin[:, k, WP:W]
                        dve.tensor_tensor(ys, ys, mods["gate_f"][:, k, 1:C9], ALU.mult).then_inc(rc, 1)
                        dve.wait_ge(rc, n + 1 + k + 1)
                        dve.tensor_tensor(xs, ys, xs, ALU.add)
                    dve.scalar_tensor_tensor(out=xin[:, k, 0:WP], in0=y[:, k, c0:c0 + WP],
                                             scalar=mods["gate_f"][:, k, 0:1], in1=xin[:, k, 0:WP],
                                             op0=ALU.mult, op1=ALU.add).then_inc(fy, 1)

            def unit(n0, i, second=False):
                collect(n0 - 1, i, 2, first=second)
                product(n0, i, 0)
                collect(n0, i, 0)
                product(n0, i, 1)
                collect(n0, i, 1)
                product(n0, i, 2)
            for c in range(NC):
                low_h(0, c)
            product(0, 0, 0)
            collect(0, 0, 0, first=True)
            product(0, 0, 1)
            collect(0, 0, 1, first=True)
            product(0, 0, 2)
            unit(1, 0, second=True)
            with dve.Fori(0, FT - 5, 2) as i:
                unit(2, i)
                unit(3, i)
            unit(FT - 2, 0)
            collect(FT - 2, 0, 2)
            for c in range(NC):
                if c:
                    collect(FT - 1, 0, c - 1)
                product(FT - 1, 0, c)
                low_h(1, c)
            collect(FT - 1, 0, 2)
            product(FT, 0, 0)
            finish(0, 0)
            product(FT, 0, 1)
            product(FT, 0, 2)
            collect(FT, 0, 0, first=True)
            finish(0, 1)
            product(FT + 1, 0, 0)
            collect(FT, 0, 1, first=True)
            finish(0, 2)
            product(FT + 1, 0, 1)
            collect(FT, 0, 2, first=True)
            collect(FT + 1, 0, 0)
            product(FT + 1, 0, 2)
            collect(FT + 1, 0, 1)
            with dve.Fori(0, FT - 3, 2) as i:
                unit(FT + 2, i)
                unit(FT + 3, i)
            collect(2 * FT - 1, 0, 2)
            for c in range(NC):
                finish(1, c)


def layouts(i):
    c = np.ascontiguousarray
    f = lambda a: np.asarray(a)
    cols = lambda a: f(a).reshape(-1, P).T
    x = np.concatenate([f(i["x_prompt"])[0], f(i["x_sample"])[:, 0]], 0)
    tiles = lambda w, order: [f(w)[:, m * P:(m + 1) * P].reshape(-1, P, P).transpose(1, 0, 2).reshape(P, -1)
                              for m in order]
    w_in = f(i["w_in"])[0]
    w_ff, w_fo = f(i["w_ffn_in"])[0], f(i["w_ffn_out"])[0]
    ffn = [np.concatenate([g, u, w_fo[t * P:(t + 1) * P]], 1) for t, (g, u) in
           enumerate(zip(tiles(w_ff, range(FT)), tiles(w_ff, range(FT, 2 * FT))))]
    gates = np.stack([f(i[n])[0].reshape(LT, 2, DH, DH).transpose(1, 2, 0, 3) for n in ("lru_wa", "lru_wx")])
    lru = [cols(f(i["conv_w"])[0, t]) for t in range(4)] + [cols(f(i["conv_b"])[0])]
    lru += [cols(f(i[n])[0].reshape(-1)) for n in ("lru_ba", "lru_bx")] + [cols(f(i["lru_lambda"])[0])] * 2
    lam4 = np.stack([cols(f(i["lru_lambda"])[0])] * 4, 1)
    feat = lambda a: f(a).reshape(f(a).shape[:-1] + (LT, P))
    return {
        "xT": c(x.T.reshape(KT, P, T).transpose(1, 0, 2)),
        "cT": c(np.concatenate([f(i["c_prompt"]), f(i["c_sample"])], 0).T.reshape(KT, P, C9).transpose(1, 0, 2)),
        "w_ada": c(f(i["w_ada"])[0].reshape(KT, P, 12, AC).transpose(2, 1, 0, 3)),
        "b_adaT": c(cols(f(i["b_ada"])[0])),
        "gains": c(np.stack([cols(f(i[n])[0]) for n in ("g_pre_mix", "g_post_mix", "g_pre_ffn", "g_post_ffn")], 1)),
        "lams": c(np.stack([f(i[n])[0] for n in ("lam_q1", "lam_k1", "lam_q2", "lam_k2")])),
        "lruv": c(lam4),
        "w_in": c(np.stack(tiles(w_in, [12, 13, 14, 15, 16, 17, 18, 19, 0, 1, 2, 3, 4, 5, 6, 7, 8, 9, 10, 11]))),
        "lru_cols": c(np.stack(lru, 1)),
        "w_gates": c(gates),
        "sconvT": c(feat(i["state_conv"][0]).transpose(3, 2, 1, 0)),
        "shT": c(feat(i["state_h"][0]).transpose(2, 1, 0)),
        "state_conv": c(f(i["state_conv"])[0]),
        "w_out": c(np.stack(tiles(f(i["w_out"])[0], range(KT)))),
        "w_ffn": c(np.stack(ffn).reshape(FT, P, 3 * KT, P)),
        "g_subln": c(f(i["g_subln"])),
        "cache_k": c(f(i["cache_k"])[0].reshape(-1, P, NH * P)),
        "cache_v": c(f(i["cache_v"])[0].reshape(-1, P, NH * P)),
        "page_table": c(f(i["page_table"]).reshape(1, -1)),
    }


def sample_constants():
    r = np.arange(RS)
    head = r // 2 % NH
    slope = 2.0 ** (-8.0 * (head + 1) / NH) / SCALE
    n = np.arange(BH)
    return {
        "pick": ((n[:, None, None] == n) & (n[:, None, None] % NH == np.arange(NH)[:, None])).astype(np.float32),
        "half": (np.arange(P)[:, None] // DH == np.arange(2)).astype(np.float32),
        "pair": (r[:, None] // 2 == np.arange(BH)).astype(np.float32),
        "sign": (r[:, None] % 2 == np.arange(2)).astype(np.float32),
        "alibi": (slope[:, None] * (np.arange(PAST + 1) - PAST)).astype(np.float32),
    }


OUTS = {
    "yT": (P, KT, T),
    "z": (3 * NH, P, T),
    "hT": (P, LT, C9),
    "conv_new": (P, LT, 3 + NS),
    "conv_kept": (NS, 2, LT * P),
}
SCRATCH = {"mix": (KT, P, T), "x1": (P, KT, T), "h2": (P, KT, T)}


def program(nc, io):
    with ExitStack() as ctx:
        mods = {}
        for name, shape in [("gains_sb", [P, 4, KT]), ("silu_c", [P, KT, C9]), ("mod", [P, NADA, C9])] + [
                (n, [P, KT, C9]) for n in ("shift_m", "shift_f", "mul_m", "mul_f", "gate_m", "gate_f")] + [
                ("one", [P, 1]), ("bada", [P, 6 * KT]), ("ident", [P, P]), ("eps", [P, 1]), ("neglam", [P, 1]),
                ("sp2", [P, LT]), ("ones", [P, P])]:
            mods[name] = ctx.enter_context(nc.sbuf_tensor(name, shape, F32))
        mods["gains"] = mods["gains_sb"]
        modulation(nc, mods, io)
        input_projection(nc, mods, io)
        attention(nc, mods, io)
        sample_attention(nc, mods, io)
        mods["wraw0"] = ctx.enter_context(nc.sbuf_tensor("ffn_wraw0", [P, 3 * KT, P], F32))
        mods["w_in0"] = ctx.enter_context(nc.semaphore("ffn_w_in0"))
        output_projection(nc, mods, io)
        ffn(nc, mods, io)


def kernel(**inputs):
    import concourse.bacc as _bacc
    from concourse.bass_utils import run_bass_kernel_spmd as _run

    nc = _bacc.Bacc("TRN2", target_bir_lowering=False, num_devices=1)
    arrays = layouts(inputs)
    arrays.update(sample_constants())
    io = {}
    for name, a in arrays.items():
        io[name] = nc.dram_tensor(name, a.shape, mybir.dt.from_np(a.dtype), kind="ExternalInput").ap()
    for name, shape in OUTS.items():
        io[name] = nc.dram_tensor(name, shape, F32, kind="ExternalOutput").ap()
    for name, shape in SCRATCH.items():
        io[name] = nc.dram_tensor(name, shape, F32, kind="Internal").ap()
    program(nc, io)
    r = _run(nc, [arrays], core_ids=[0]).results[0]

    y = r["yT"].transpose(2, 1, 0).reshape(T, D)
    k = r["z"][NH:2 * NH].transpose(2, 0, 1)
    v = r["z"][2 * NH:].transpose(2, 0, 1)
    h = r["hT"].transpose(2, 1, 0).reshape(C9, LT * P)
    conv = r["conv_new"].transpose(2, 1, 0).reshape(3 + NS, LT * P)
    c = np.ascontiguousarray
    return (c(y[None, :SEQ]), c(y[SEQ:, None]), c(k[None, None, :SEQ]), c(v[None, None, :SEQ]), c(h[None, 0:1]),
            c(conv[None, None, 0:3]), c(k[SEQ:][None, :, None]), c(v[SEQ:][None, :, None]), c(h[None, 1:]),
            c(np.concatenate([r["conv_kept"], conv[3:, None]], 1)[None]))
```
